# Optimizing a Trainium2 kernel written in Bass

```python
import math
import jax, jax.numpy as jnp
from jax import lax
import numpy as np

D_MODEL = 1024
BATCH = 1
SEQ = 1024
DEPTH = 1
DEC_BATCH = 8
DEC_SEQ = 4
PAST_LEN = 4096
PAGE_SIZE = 128

MIX = D_MODEL
DA_HEADS = 4
DA_QK = 64
DA_V = 2 * DA_QK
DA_W = DA_HEADS * DA_V
HG_HEADS = 4
HG_K = 128
HG_V = 128
HG_W = HG_HEADS * HG_V
HG_CHUNK = 16
N_BUCKETS = 32
MAX_DISTANCE = 128
Q_BLOCK = 128
N_GROUPS = 4
EXPERTS_PER_GROUP = 4
N_EXPERTS = N_GROUPS * EXPERTS_PER_GROUP
D_EXPERT = 256
EPS = 1e-6
SPLITS = (DA_HEADS * 2 * DA_QK, DA_HEADS * 2 * DA_QK, DA_W,
          HG_HEADS * HG_K, HG_HEADS * HG_K, HG_W, HG_W)
IN_TOTAL = sum(SPLITS)

kernel_name = 'hybrid_diffattn_hgrn2_hmoe_step'

def rmsnorm(x, w):
    xf = x.astype(jnp.float32)
    y = xf * lax.rsqrt(jnp.mean(xf * xf, axis=-1, keepdims=True) + EPS)
    return (y * w.astype(jnp.float32)).astype(x.dtype)

def split_proj(p):
    offs = np.cumsum(SPLITS)[:-1].tolist()
    return jnp.split(p, offs, axis=-1)

def t5_bucket(n):
    n = jnp.maximum(n, 0)
    max_exact = N_BUCKETS // 2
    nf = jnp.maximum(n, max_exact).astype(jnp.float32)
    large = max_exact + (jnp.log(nf / max_exact) / math.log(MAX_DISTANCE / max_exact)
                         * (N_BUCKETS - max_exact)).astype(jnp.int32)
    large = jnp.minimum(large, N_BUCKETS - 1)
    return jnp.where(n < max_exact, n, large)

def diff_attend(q, segments, q_pos, rel_bias, lam):
    scale = DA_QK ** -0.5
    logits = []
    for k, _, k_pos in segments:
        s = jnp.einsum('bqhmd,bkhmd->bmhqk', q, k).astype(jnp.float32) * scale
        n = q_pos[:, None] - k_pos[None, :]
        bias = jnp.transpose(rel_bias[t5_bucket(n)], (2, 0, 1)).astype(jnp.float32)
        logits.append(jnp.where(n >= 0, s + bias, -jnp.inf))
    p = jax.nn.softmax(jnp.concatenate(logits, axis=-1), axis=-1)
    attn = p[:, 0] - lam * p[:, 1]
    out = 0.0
    off = 0
    for k, v, k_pos in segments:
        kl = k_pos.shape[0]
        out = out + jnp.einsum('bhqk,bkhv->bqhv', attn[..., off:off + kl], v)
        off += kl
    return out.astype(jnp.float32)

def diff_attn_prompt(q, k, v, rel_bias, lam):
    b, s = q.shape[:2]
    k_pos = jnp.arange(s, dtype=jnp.int32)

    def block(i):
        start = i * Q_BLOCK
        qb = lax.dynamic_slice_in_dim(q, start, Q_BLOCK, axis=1)
        q_pos = start + jnp.arange(Q_BLOCK, dtype=jnp.int32)
        return diff_attend(qb, [(k, v, k_pos)], q_pos, rel_bias, lam)

    out = lax.map(block, jnp.arange(s // Q_BLOCK, dtype=jnp.int32))
    return jnp.moveaxis(out, 0, 1).reshape(b, s, DA_HEADS, DA_V)

def hgrn2_scan(q, k, v, g, s0, chunk):
    b, l, h, _ = q.shape
    n = l // chunk

    def to_chunks(t):
        return jnp.moveaxis(t.reshape((b, n, chunk) + t.shape[2:]), 1, 0)

    causal = jnp.tril(jnp.ones((chunk, chunk), dtype=bool))[None, :, :, None, None]

    def step(S, inp):
        qc, kc, vc, gc = inp
        G = jnp.cumsum(gc, axis=1)
        o_inter = jnp.einsum('bthk,bhkv->bthv', qc * jnp.exp(G), S)
        decay = jnp.exp(jnp.where(causal, G[:, :, None] - G[:, None, :], -jnp.inf))
        A = jnp.einsum('bthk,bshk,btshk->bhts', qc, kc, decay)
        o_intra = jnp.einsum('bhts,bshv->bthv', A, vc)
        G_last = G[:, -1]
        S_new = (jnp.exp(G_last)[..., None] * S
                 + jnp.einsum('bshk,bshv->bhkv', kc * jnp.exp(G_last[:, None] - G), vc))
        return S_new, o_inter + o_intra

    S_fin, o = lax.scan(step, s0, (to_chunks(q), to_chunks(k), to_chunks(v), to_chunks(g)))
    return jnp.moveaxis(o, 0, 1).reshape(b, l, h, v.shape[-1]), S_fin

def hgrn2_mixer(hq, hf, hi, hgate, lb, s0, chunk, norm_w):
    b, l = hq.shape[:2]
    f32 = jnp.float32
    q = jax.nn.silu(hq.astype(f32)).reshape(b, l, HG_HEADS, HG_K) * (HG_K ** -0.5)
    f = lb + (1.0 - lb) * jax.nn.sigmoid(hf.astype(f32))
    g = jnp.log(f).reshape(b, l, HG_HEADS, HG_K)
    k = (1.0 - f).reshape(b, l, HG_HEADS, HG_K)
    v = hi.astype(f32).reshape(b, l, HG_HEADS, HG_V)
    o, s_fin = hgrn2_scan(q, k, v, g, s0.astype(f32), chunk)
    o = rmsnorm(o, norm_w) * jax.nn.silu(hgate.astype(f32).reshape(b, l, HG_HEADS, HG_V))
    return o.reshape(b, l, HG_W), s_fin

def hier_moe(h, wg, bg, we, be, w1, w3, w2):
    shp = h.shape
    t = h.reshape(-1, shp[-1])
    f32 = jnp.float32
    pg = jax.nn.softmax((t @ wg).astype(f32) + bg.astype(f32), axis=-1)
    p_top, g_idx = lax.top_k(pg, 1)
    le = ((t @ we).astype(f32) + be.astype(f32)).reshape(-1, N_GROUPS, EXPERTS_PER_GROUP)
    le_sel = jnp.take_along_axis(le, g_idx[:, :, None], axis=1)[:, 0]
    top_l, e_idx = lax.top_k(le_sel, 2)
    gate = p_top * jax.nn.softmax(top_l, axis=-1)
    expert_id = g_idx * EXPERTS_PER_GROUP + e_idx
    combine = jnp.sum(jax.nn.one_hot(expert_id, N_EXPERTS, dtype=f32) * gate[..., None], axis=1)
    y = jnp.zeros(t.shape, f32)
    for e in range(N_EXPERTS):
        he = jax.nn.silu(t @ w1[e]) * (t @ w3[e])
        y = y + combine[:, e:e + 1] * (he @ w2[e])
    return y.astype(h.dtype).reshape(shp)

def setup_inputs(seed: int = 0) -> dict:
    key = jax.random.key(seed)
    ks = jax.random.split(key, 24)
    f32 = jnp.float32
    n_pages = PAST_LEN // PAGE_SIZE
    n_used = DEC_BATCH * n_pages
    n_pool = n_used + n_used // 4
    nrm = lambda k, shape, s: jax.random.normal(k, shape, f32) * s
    return {
        'x_prompt': nrm(ks[0], (BATCH, SEQ, D_MODEL), 1.0),
        'x_sample': nrm(ks[1], (DEC_BATCH, DEC_SEQ, D_MODEL), 1.0),
        'cache_k': nrm(ks[2], (DEPTH, n_pool, PAGE_SIZE, DA_HEADS, 2 * DA_QK), 1.0),
        'cache_v': nrm(ks[3], (DEPTH, n_pool, PAGE_SIZE, DA_HEADS, DA_V), 1.0),
        'state_hgrn': nrm(ks[4], (DEPTH, DEC_BATCH, HG_HEADS, HG_K, HG_V), 0.3),
        'page_table': jax.random.permutation(ks[5], n_pool)[:n_used].reshape(DEC_BATCH, n_pages).astype(jnp.int32),
        'norm1_w': 1.0 + nrm(ks[6], (DEPTH, D_MODEL), 0.01),
        'w_in': nrm(ks[7], (DEPTH, D_MODEL, IN_TOTAL), D_MODEL ** -0.5),
        'rel_bias': nrm(ks[8], (N_BUCKETS, DA_HEADS), 0.5),
        'lambda_q1': nrm(ks[9], (DEPTH, DA_QK), 0.1),
        'lambda_k1': nrm(ks[10], (DEPTH, DA_QK), 0.1),
        'lambda_q2': nrm(ks[11], (DEPTH, DA_QK), 0.1),
        'lambda_k2': nrm(ks[12], (DEPTH, DA_QK), 0.1),
        'da_subln_w': 1.0 + nrm(ks[13], (DEPTH, DA_V), 0.01),
        'hg_lb_logits': nrm(ks[14], (DEPTH + 1, HG_HEADS * HG_K), 0.1),
        'hg_norm_w': 1.0 + nrm(ks[15], (DEPTH, HG_V), 0.01),
        'w_out': nrm(ks[16], (DEPTH, MIX, D_MODEL), MIX ** -0.5),
        'norm2_w': 1.0 + nrm(ks[17], (DEPTH, D_MODEL), 0.01),
        'router_g_w': nrm(ks[18], (DEPTH, D_MODEL, N_GROUPS), D_MODEL ** -0.5),
        'router_g_b': nrm(ks[19], (DEPTH, N_GROUPS), 0.01),
        'router_e_w': nrm(ks[20], (DEPTH, D_MODEL, N_EXPERTS), D_MODEL ** -0.5),
        'router_e_b': nrm(ks[21], (DEPTH, N_EXPERTS), 0.01),
        'expert_w1': nrm(ks[22], (DEPTH, N_EXPERTS, D_MODEL, D_EXPERT), D_MODEL ** -0.5),
        'expert_w3': nrm(jax.random.fold_in(ks[22], 1), (DEPTH, N_EXPERTS, D_MODEL, D_EXPERT), D_MODEL ** -0.5),
        'expert_w2': nrm(ks[23], (DEPTH, N_EXPERTS, D_EXPERT, D_MODEL), D_EXPERT ** -0.5),
        'final_norm_w': 1.0 + nrm(jax.random.fold_in(ks[23], 1), (D_MODEL,), 0.01),
    }

def reference(x_prompt, x_sample, cache_k, cache_v, state_hgrn, page_table,
              norm1_w, w_in, rel_bias, lambda_q1, lambda_k1, lambda_q2, lambda_k2,
              da_subln_w, hg_lb_logits, hg_norm_w, w_out, norm2_w,
              router_g_w, router_g_b, router_e_w, router_e_b,
              expert_w1, expert_w3, expert_w2, final_norm_w):
    f32 = jnp.float32
    lb_all = jnp.cumsum(jax.nn.softmax(hg_lb_logits.astype(f32), axis=0), axis=0)
    past = page_table.shape[1] * PAGE_SIZE

    def attend_prompt(q, k, v, lam, l):
        return diff_attn_prompt(q, k, v, rel_bias, lam)

    def attend_sample(q, k, v, lam, l):
        bd, t = q.shape[:2]
        kp = cache_k[l][page_table].reshape(bd, past, DA_HEADS, 2, DA_QK)
        vp = cache_v[l][page_table].reshape(bd, past, DA_HEADS, DA_V)
        past_pos = jnp.arange(past, dtype=jnp.int32)
        new_pos = past + jnp.arange(t, dtype=jnp.int32)
        return diff_attend(q, [(kp, vp, past_pos), (k, v, new_pos)], new_pos, rel_bias, lam)

    def layer(x, l, attend, s0, chunk):
        b, s = x.shape[:2]
        lam_init = 0.8 - 0.6 * math.exp(-0.3 * l)
        lam = (jnp.exp(jnp.sum(lambda_q1[l].astype(f32) * lambda_k1[l].astype(f32)))
               - jnp.exp(jnp.sum(lambda_q2[l].astype(f32) * lambda_k2[l].astype(f32))) + lam_init)
        h = rmsnorm(x, norm1_w[l])
        dq, dk, dv, hq, hf, hi, hgate = split_proj(h @ w_in[l])
        q = dq.reshape(b, s, DA_HEADS, 2, DA_QK)
        k = dk.reshape(b, s, DA_HEADS, 2, DA_QK)
        v = dv.reshape(b, s, DA_HEADS, DA_V)
        o_da = rmsnorm(attend(q, k, v, lam, l), da_subln_w[l]) * (1.0 - lam_init)
        o_hg, s_new = hgrn2_mixer(hq, hf, hi, hgate, lb_all[l], s0, chunk, hg_norm_w[l])
        mixed = jnp.concatenate([o_da.reshape(b, s, DA_W), o_hg], axis=-1).astype(x.dtype)
        x = x + mixed @ w_out[l]
        x = x + hier_moe(rmsnorm(x, norm2_w[l]), router_g_w[l], router_g_b[l], router_e_w[l],
                         router_e_b[l], expert_w1[l], expert_w3[l], expert_w2[l])
        return x, k.reshape(b, s, DA_HEADS, 2 * DA_QK), v, s_new

    xp, xs = x_prompt, x_sample
    kp_l, vp_l, sp_l, ks_l, vs_l, ss_l = [], [], [], [], [], []
    for l in range(DEPTH):
        s0p = jnp.zeros((xp.shape[0], HG_HEADS, HG_K, HG_V), f32)
        xp, kp, vp, sp = layer(xp, l, attend_prompt, s0p, HG_CHUNK)
        xs, ksm, vsm, ssm = layer(xs, l, attend_sample, state_hgrn[l], xs.shape[1])
        kp_l.append(kp); vp_l.append(vp); sp_l.append(sp.astype(xp.dtype))
        ks_l.append(ksm); vs_l.append(vsm); ss_l.append(ssm.astype(state_hgrn.dtype))
    y_prompt = rmsnorm(xp, final_norm_w)
    y_sample = rmsnorm(xs, final_norm_w)
    return (y_prompt, y_sample, jnp.stack(kp_l), jnp.stack(vp_l), jnp.stack(sp_l),
            jnp.stack(ks_l), jnp.stack(vs_l), jnp.stack(ss_l))


_drawn_inputs = setup_inputs


def setup_inputs(seed=0):
    import zlib

    import numpy as np

    out = dict(_drawn_inputs(seed))
    spreads = {}
    factors = {'norm1_w': 2.86,
     'lambda_q1': 3.548,
     'lambda_k1': 8.0,
     'da_subln_w': 4.989,
     'hg_norm_w': 4.664,
     'norm2_w': 3.026,
     'router_g_b': 5.932,
     'router_e_b': 5.149,
     'final_norm_w': 5.532}
    for name, (base, spread) in spreads.items():
        noise = np.random.default_rng([zlib.crc32(name.encode()), seed]).standard_normal(out[name].shape)
        drawn = base * np.exp(spread * noise) if base else spread * noise
        out[name] = __import__('jax').numpy.asarray(drawn.astype(out[name].dtype))
    for name, factor in factors.items():
        out[name] = (out[name] * factor).astype(out[name].dtype)
    return out
```

```python
import math
from contextlib import ExitStack

import numpy as np
import concourse.bass as bass
from concourse import mybir

F32 = mybir.dt.float32
I32 = mybir.dt.int32
U32 = mybir.dt.uint32
ALU = mybir.AluOpType
ACT = mybir.ActivationFunctionType
AX = mybir.AxisListType.X
ds = bass.ds

P = 128
D = 1024
KC = D // P
SEQ = 1024
NB, NT = 8, 4
SMP = NB * NT
TOK = SEQ + SMP
TILES = SEQ // P + 1
ROWS = [P] * (SEQ // P) + [SMP]
H = 4
QK = 64
HW = H * P
PAGES = 32
COLS = H * 2 * NT
NE, NG, EG, FF = 16, 4, 4, 256
CAP = 32
PAIRS = CAP // 2
SURE = -(-(2 * TOK // P + 1) // 2) * 2
LEVELS = [64, 32, 16, 8, 4, 2, 1]
NLEV = len(LEVELS)
BUCKETS = 32
EPS = 1e-6
NEG = -1e30
LAM_INIT = 0.8 - 0.6 * math.exp(-0.3 * 0)

CP = {}


def constants():
    parts = []

    def put(name, a):
        full = np.zeros((P, a.shape[1]), np.float32)
        full[:a.shape[0]] = a
        CP[name] = (sum(x.shape[1] for x in parts), a.shape[1])
        parts.append(full)

    def bucket(n):
        n = np.maximum(n, 0)
        nf = np.maximum(n, 16).astype(np.float32)
        large = 16 + (np.log(nf / np.float32(16)) / np.float32(math.log(8.0)) * 16).astype(np.int32)
        return np.where(n < 16, n, np.minimum(large, 31))

    def onehot(dist):
        a = np.zeros((BUCKETS + 1, dist.size), np.float32)
        dist = dist.reshape(-1)
        ok = dist >= 0
        a[bucket(dist)[ok], np.nonzero(ok)[0]] = 1.0
        a[BUCKETS, ~ok] = NEG
        return a

    t = np.arange(P)
    put("ident", np.eye(P))
    put("tri", (t[:, None] < t[None, :]) * 1.0)
    lv = []
    for w in LEVELS:
        same = t[:, None] // (2 * w) == t[None, :] // (2 * w)
        lv.append(same & (t[:, None] % (2 * w) < w) & (t[None, :] % (2 * w) >= w))
    lv.append(t[:, None] == t[None, :])
    put("level", np.concatenate(lv, 1) * 1.0)
    put("own", (np.arange(SMP)[:, None] // NT == np.arange(NB)[None, :]) * 1.0)
    put("other", (np.arange(SMP)[:, None] // NT != np.arange(NB)[None, :]) * NEG)
    put("valid", (t[:, None] < SMP) * 1.0)
    put("iota", np.broadcast_to(np.arange(CAP)[None, :], (P, CAP)) * 1.0)
    small = sum(x.shape[1] for x in parts)
    put("oh_band", onehot(255 - np.arange(384)))
    tt = np.arange(NT)
    put("oh_last", onehot((P + tt[:, None] - t[None, :])))
    put("oh_far", onehot(np.full(P, 4096)))
    put("oh_new", onehot((tt[:, None] - (np.arange(SMP) % NT)[None, :])))
    return np.concatenate(parts, 1).astype(np.float32), small


TABLE, SMALL = constants()


class Chain:

    def __init__(self, eng, sem):
        self.eng, self.sem, self.n, self.base = eng, sem, 0, 0

    def step(self, ins):
        ins.then_inc(self.sem, 1)
        self.n += 1

    def wait(self):
        self.eng.wait_ge(self.sem, self.base + self.n)

    def enter(self, turn, per_turn):
        self.n0, self.per = self.n, per_turn
        self.base, self.n = turn * per_turn + self.n0, 0

    def leave(self, turns):
        assert self.n == self.per, (self.n, self.per)
        self.base, self.n = 0, self.n0 + turns * self.per


def build(nc, x_prompt, x_sample, cache_k, cache_v, state_hgrn, page_table,
          norm1_w, w_in, rel_bias, lambda_q1, lambda_k1, lambda_q2, lambda_k2,
          da_subln_w, hg_lb_logits, hg_norm_w, w_out, norm2_w,
          router_g_w, router_g_b, router_e_w, router_e_b,
          expert_w1, expert_w3, expert_w2, final_norm_w, table,
          y_prompt, y_sample, k_prompt, v_prompt, s_prompt, k_sample, v_sample, s_sample):

    band_d = nc.dram_tensor("band_scratch", (H * P, 384), F32, kind="Internal").ap()
    rows_d = nc.dram_tensor("rows_scratch", (TOK, D), F32, kind="Internal").ap()
    ids_d = nc.dram_tensor("ids_scratch", (P * CAP, 16), I32, kind="Internal").ap()
    ye_d = nc.dram_tensor("expert_scratch", (CAP * P, D), F32, kind="Internal").ap()

    xp_v = x_prompt.rearrange("b (i p) d -> p (b i) d", p=P)
    xs_v = x_sample.rearrange("b t d -> (b t) d")
    win_v = w_in.rearrange("l (k p) n -> p (l k) n", p=P)
    wout_v = w_out.rearrange("l (k p) n -> p (l k) n", p=P)
    ck_v = cache_k.rearrange("l n p h d -> (l n p) (h d)")
    cv_v = cache_v.rearrange("l n p h d -> (l n p) (h d)")
    st_v = state_hgrn.rearrange("l b h k v -> (l h) k b v")
    so_v = s_sample.rearrange("l b h k v -> (l h) k b v")
    kp_v = k_prompt.rearrange("l b (i p) h d -> p (l b i) (h d)", p=P)
    vp_v = v_prompt.rearrange("l b (i p) h d -> p (l b i) (h d)", p=P)
    ks_v = k_sample.rearrange("l b t h d -> (l b t) (h d)")
    vs_v = v_sample.rearrange("l b t h d -> (l b t) (h d)")
    yp_v = y_prompt.rearrange("b (i p) d -> p (b i) d", p=P)
    ys_v = y_sample.rearrange("b t d -> (b t) d")
    w1_v = expert_w1.rearrange("l e d f -> (l e d) f")
    w3_v = expert_w3.rearrange("l e d f -> (l e d) f")
    w2_v = expert_w2.rearrange("l e f d -> (l e f) d")

    with ExitStack() as ctx:
        def sb(name, cols, dt=F32, rows=P):
            return ctx.enter_context(nc.sbuf_tensor(name, [rows, cols], dt))

        sems = {}
        part = [""]

        def sem(name):
            if name not in sems:
                sems[name] = nc.alloc_semaphore(name=name + part[0])
            return sems[name]

        arena = sb("arena", 8448 + 13056 + 21888 + 6144)
        at = [0]

        def take(cols, start=None):
            if start is None:
                start = at[0]
                at[0] += cols
            return arena[:, start:start + cols]

        A0 = 0
        hT = take(KC * TOK)
        B0 = at[0]
        qT, kT = take(H * TOK), take(H * TOK)
        v_nat = take(TILES * HW)
        C0 = at[0]
        hqT, gT, kkT = take(H * TOK), take(H * TOK), take(H * TOK)
        hi, gate = take(TILES * HW), take(TILES * HW)
        W0 = at[0]
        wring = [take(2048) for _ in range(3)]
        mixT = take(KC * TOK, A0)
        reset = take(TOK, A0)
        x_all = take(TILES * D, C0)
        knat = [take(HW, W0), take(HW, W0 + HW)]
        X = [take(TOK, W0), take(TOK, W0 + TOK)]
        tmp = take(TOK, W0)
        AT = take(1024, W0 + 2112)
        KdN = take(1024, W0 + 3136)
        S = take(9 * P, W0 + 4160)
        ATs = take(SMP, W0 + 5312)
        Qpad = take(NB * SMP, W0 + 5344)
        KdM = take(NB * P, W0 + 3136)
        S0 = take(NB * P, W0 + 2112)
        band = take(H * 1152, C0)
        zp = [take(2048, C0 + 4608), take(2048, C0 + 6656)]
        pT = [take(1024, C0 + 8704), take(1024, C0 + 9728)]
        o_sb = [take(P, C0 + 10752), take(P, C0 + 10880)]
        oh = take(384 + 640 + 128, W0)
        rowb = take(384, W0 + 1200)
        R0 = C0 + 11264
        RING = 16
        pages = [take(HW, R0 + HW * i) for i in range(RING)]
        z = take((PAGES + 1) * COLS, W0)
        kTd = [take(HW, W0 + 1056 + HW * i) for i in range(4)]
        qblk = take(NB * COLS, W0 + 3104)
        oT_all = take(NB * COLS, W0 + 3360)
        sum_all = take(NB * COLS, W0 + 3616)
        knew = take(H * SMP, W0 + 3872)
        fin = take(512, W0 + 4000)
        wout = take(KC * D, C0)
        x1 = take(TILES * D, B0)
        xh = [take(D, W0), take(D, W0 + D)]
        h2T = [take(D, W0 + 2 * D), take(D, W0 + 3 * D)]
        sqj = take(D, W0 + 4 * D)
        wslot = [take(6144, A0), take(6144, R0)]
        xg = [take(D, C0), take(D, C0 + D)]
        xT = [take(D, C0 + 2 * D), take(D, C0 + 3 * D)]
        he = [take(2 * FF, C0 + 4 * D), take(2 * FF, C0 + 4 * D + 512)]
        heT = [take(FF, C0 + 5 * D), take(FF, C0 + 5 * D + 256)]
        ysb = [take(D, C0 + 6 * D), take(D, C0 + 7 * D)]
        zero_rows = take(D, R0)
        ya = [take(D, C0), take(D, C0 + D)]
        yb = [take(D, C0 + 2 * D), take(D, C0 + 3 * D)]
        fw = take(D, C0 + 4 * D)

        tab = sb("tab", SMALL)

        def cst(name, rows=P):
            a, n = CP[name]
            return tab[0:rows, a:a + n]

        ident = cst("ident")
        ones = sb("ones", P)[:, :]
        small = sb("small", 604)
        sat = [0]

        def sm(n, dt=F32):
            a = small[:, sat[0]:sat[0] + n]
            sat[0] += n
            return a if dt == F32 else a.bitcast(dt)

        n1w, n2w, lbT, omlb = sm(KC), sm(KC), sm(H), sm(H)
        lg0, lg1 = sm(H), sm(H)
        daw, hgw = sm(1), sm(1)
        ss, rstd = sm(TILES), sm(TILES)
        ss2, rstd2 = sm(TILES * H), sm(TILES * H)
        lamv, lamp, nlam = sm(4), sm(2), sm(1)
        rb = sm(H)
        far, last_ = sm(COLS), sm(COLS)
        bnew = sm(NT * H)
        biasn = sm(NB * COLS)
        att = sm(16)
        mxc, mxr, dg = sm(COLS), sm(1), sm(COLS)
        psums = sm(COLS)
        ptab = sb("ptab", NB * PAGES, I32, 1)
        rbias = sm(20)
        wr = sb("wr", KC * 20)
        route = sb("route", 624)
        rat = [0]

        def rt(n, dt=F32):
            a = route[:, rat[0]:rat[0] + n]
            rat[0] += n
            return a if dt == F32 else a.bitcast(dt)

        lgall, gpad = rt(TILES * 20), rt(TILES * 8)
        g8, gi, e8, ei = rt(8), rt(8, U32), rt(8), rt(8, U32)
        gidx, v12, i12 = rt(TILES), rt(TILES * 2), rt(TILES * 2)
        gate1, gate2, ptop = rt(TILES), rt(TILES), rt(TILES)
        gexp = rt(TILES * 4)
        slotf, slot_i, row_i, row_j = rt(2 * TILES), rt(2 * TILES, I32), rt(2 * TILES, I32), rt(2 * TILES, I32)
        cnt_i, ntl, endt, base = rt(NE, I32), rt(NE), rt(NE), rt(NE)
        eid_f, eid = rt(CAP), rt(CAP, I32)
        nit_i = rt(1, I32)
        idx_cur = rt(2, I32)
        ids_sb = take(CAP * 16, R0 + 6144).bitcast(I32)
        payload = take(TILES * 16, R0 + 6656).bitcast(I32)
        lm = take(TILES * 16, R0 + 6800)
        oh1, oh2, Mx, cum, rk = (take(TILES * 16, W0 + 4 * D + 144 * i) for i in range(5))
        cmp = take(CAP * 16, W0 + 4 * D + 720)

        ps = [ctx.enter_context(nc.psum_tensor(f"bank{i}", [P, 512], F32)) for i in range(8)]

        Q0, K0, V0, HQ0, HF0, HI0, GA0 = (i * HW for i in range(7))
        slots = []
        for kind, dst, c0 in (("T", hqT, HQ0), ("T", gT, HF0), ("N", hi, HI0), ("N", gate, GA0),
                              ("T", qT, Q0), ("T", kT, K0), ("N", v_nat, V0)):
            for half in range(2):
                slots.append((kind, dst, c0 + half * 256, half))
        items = []
        for s, (kind, dst, c0, half) in enumerate(slots):
            if kind == "T":
                items += [(s, kind, dst, half, c, n) for c in range(2) for n in range(3)]
            else:
                items += [(s, kind, dst, half, i, 0) for i in range(TILES)]
        N3 = TOK // 3
        upto = {"T": [0], "N": [0]}
        for it in items:
            for k in upto:
                upto[k].append(upto[k][-1] + (it[1] == k))

        def tok(t, c, i):
            return t[:, c * TOK + i * P:c * TOK + i * P + ROWS[i]]

        def head3(a, n, **kw):
            return a.rearrange("p (a b) -> p a b", b=n)

        NPH = [0]

        def phase_end(eng, k):
            eng.drain().then_inc(sem("phase"), 1)
            eng.wait_ge(sem("phase"), 5 * k)

        cumT, n = {}, 0
        for h in range(H):
            for i in range(8):
                for j in range(0, i + 1, 4):
                    n += 1
                    cumT[(h, i, j)] = n

        NV_TOTAL = 16 * 11
        block_a = nc.Block()
        block = block_a.__enter__()

        @block.sync
        def _(sp):
            for g in range(4):
                sp.dma_start(head3(x_all, D)[:, 2 * g:2 * g + 2, :],
                             xp_v[:, 2 * g:2 * g + 2, :]).then_inc(sem(f"x_in{g}"), 16)
            sp.dma_start(x_all[0:SMP, 8 * D:9 * D], xs_v).then_inc(sem("x_in4"), 16)
            for s, (kind, dst, c0, half) in enumerate(slots):
                if s >= 3:
                    sp.wait_ge(sem("proj"), sum(it[0] <= s - 3 for it in items))
                sp.dma_start(head3(wring[s % 3], 256), win_v[:, :, c0:c0 + 256]).then_inc(sem(f"w_in{s % 3}"), 16)
            for i in range(TILES):
                sp.wait_ge(sem("knat_ready"), i + 1)
                dst = ks_v if i == TILES - 1 else kp_v[:, i, :]
                sp.dma_start(dst, knat[i % 2][0:ROWS[i], :]).then_inc(sem(f"knat_out{i % 2}"), 16)
            sp.dma_start(vp_v, head3(v_nat, HW)[:, 0:8, :]).then_inc(sem("out"), 16)
            sp.dma_start(vs_v, v_nat[0:SMP, 8 * HW:9 * HW]).then_inc(sem("out"), 16)
            sp.wait_ge(sem("knat_out0"), 16 * 5)
            sp.wait_ge(sem("knat_out1"), 16 * 4)
            phase_end(sp, 1)
            for h in range(H):
                sp.wait_ge(sem("s0_free"), h + 1)
                sp.dma_start(head3(S0, P), st_v[h]).then_inc(sem("s0_in"), 16)
                sp.wait_ge(sem("state_ready"), h + 1)
                sp.dma_start(s_prompt[0, 0, h], S[:, 8 * P:9 * P]).then_inc(sem("state_out"), 16)
                sp.wait_ge(sem("snew_ready"), h + 1)
                sp.dma_start(so_v[h], head3(S0, P)).then_inc(sem("snew_out"), 16)
            phase_end(sp, 2)
            sp.dma_start(oh, table[:, SMALL:]).then_inc(sem("oh_in"), 16)
            for h in range(H):
                sp.wait_ge(sem("rowb"), h + 1)
                sp.dma_start(band_d[h * P:(h + 1) * P, :], rowb).then_inc(sem("band_out"), 16)
                sp.wait_ge(sem("band_out"), 16 * (h + 1))
                skew = bass.AP(tensor=band_d.tensor, offset=h * P * 384 + 127, ap=[[383, P], [1, 256]])
                sp.dma_start(band[:, h * 1152 + 896:(h + 1) * 1152], skew).then_inc(sem("band_in"), 16)
            sp.wait_ge(sem("ptab_in"), 16)

            def page(k, slot, view, entry):
                sp.wait_ge(sem("page_free"), k + 1)
                e = sp.value_load(ptab[0:1, ds(entry, 1)], min_val=0, max_val=319)
                sp.dma_start(pages[slot], view[ds(e * P, P), :]).then_inc(sem(f"page{slot}"), 16)

            def keys(b, k0):
                for j in range(PAGES):
                    page(k0 + j, j % RING, ck_v, b * PAGES + j)

            def values(b, k0):
                for j in range(PAGES):
                    page(k0 + j, j % RING, cv_v, b * PAGES + j)

            keys(0, 0)
            with sp.Fori(0, NB - 1) as t:
                keys(t + 1, t * 64 + 32)
                values(t, t * 64 + 64)
            values(NB - 1, 7 * 64 + 32)
            sp.wait_ge(sem("prompt_done"), 1)
            sp.dma_start(head3(wout, D), wout_v).then_inc(sem("wout_in"), 16)
            sp.wait_ge(sem("wout_in"), 16)
            sp.wait_ge(sem("out"), 32)
            sp.wait_ge(sem("state_out"), 16 * H)
            sp.wait_ge(sem("snew_out"), 16 * H)
        @block.gpsimd
        def _(pool):
            nc.gpsimd.memset(ones[:, :], 1.0).then_inc(sem("ones"), 1)
            nc.gpsimd.memset(small[:, :], 1.0).then_inc(sem("small0"), 1)
            nc.gpsimd.memset(route[:, :], 0.0).then_inc(sem("route0"), 1)
            phase_end(pool, 1)
            nc.gpsimd.memset(reset, 1.0).then_inc(sem("pool"), 1)
            pool.wait_ge(sem("pool"), 1)
            nc.gpsimd.memset(head3(reset[:, 0:SEQ], P)[:, :, 0:1], 0.0).then_inc(sem("pool"), 1)
            nc.gpsimd.memset(head3(reset[:, SEQ:TOK], NT)[:, :, 0:1], 0.0).then_inc(sem("pool"), 1)
            phase_end(pool, 2)
        @block.scalar
        def _(act):
            ch = Chain(act, sem("act"))
            act.dma_start(tab[:, :], table[:, 0:SMALL]).then_inc(sem("tab"), 16)
            act.wait_ge(sem("small0"), 1)
            loads = [(n1w, norm1_w.rearrange("l (k p) -> p (l k)", p=P)),
                     (n2w, norm2_w.rearrange("l (k p) -> p (l k)", p=P)),
                     (lg0, hg_lb_logits[0:1].rearrange("a (h p) -> p (a h)", p=P)),
                     (lg1, hg_lb_logits[1:2].rearrange("a (h p) -> p (a h)", p=P)),
                     (daw, da_subln_w.rearrange("l p -> p l")),
                     (hgw, hg_norm_w.rearrange("l p -> p l")),
                     (lamv[0:QK, 0:1], lambda_q1.rearrange("l p -> p l")),
                     (lamv[0:QK, 1:2], lambda_q2.rearrange("l p -> p l")),
                     (lamv[0:QK, 2:3], lambda_k1.rearrange("l p -> p l")),
                     (lamv[0:QK, 3:4], lambda_k2.rearrange("l p -> p l")),
                     (rb[0:BUCKETS, :], rel_bias)]
            for dst, src in loads:
                with nc.allow_non_contiguous_dma("one column a partition"):
                    act.dma_start(dst, src).then_inc(sem("vecs"), 16)
            assert 16 * len(loads) == NV_TOTAL
            act.dma_start(ptab[:, :], page_table.rearrange("(a b) n -> a (b n)", a=1)).then_inc(sem("ptab_in"), 16)
            act.dma_start(rbias[:, 0:NG], router_g_b.broadcast_to([P, NG])).then_inc(sem("rw"), 16)
            act.dma_start(rbias[:, NG:20], router_e_b.broadcast_to([P, NE])).then_inc(sem("rw"), 16)
            wr3 = wr[:, :].rearrange("p (k n) -> p k n", n=20)
            act.dma_start(wr3[:, :, 0:NG], router_g_w.rearrange("l (k p) n -> p (l k) n", p=P)).then_inc(sem("rw"), 16)
            act.dma_start(wr3[:, :, NG:20], router_e_w.rearrange("l (k p) n -> p (l k) n", p=P)).then_inc(sem("rw"), 16)
            for i in range(TILES):
                act.wait_ge(sem(f"x_in{i // 2}"), 16)
                r = ROWS[i]
                nc.scalar.activation(take(D, A0 + i * D)[0:r, :], x_all[0:r, i * D:(i + 1) * D], ACT.Square,
                                     accum_out=ss[0:r, i:i + 1]).then_inc(sem("ss"), 1)
            act.wait_ge(sem("ms"), 1)
            ch.step(nc.scalar.activation(rstd, ss, ACT.Ln))
            ch.wait()
            nc.scalar.activation(rstd, rstd, ACT.Exp, scale=-0.5).then_inc(sem("rstd"), 1)
            for g, (s, kind, dst, half, c, n) in enumerate(items):
                if kind != "T":
                    continue
                act.wait_ge(sem("proj"), g + 1)
                col = (half * 2 + c) * TOK + n * N3
                nc.scalar.activation(dst[:, col:col + N3], ps[g % 8][:, 0:N3], ACT.Copy,
                                     scale=QK ** -0.5 if dst is qT else 1.0).then_inc(sem("ev_T"), 1)
            phase_end(act, 1)
            act.wait_ge(sem("lbd"), 1)
            nc.scalar.activation(lbT, lg1, ACT.Exp).then_inc(sem("lbe"), 1)
            for h in range(H):
                sl = slice(h * TOK, (h + 1) * TOK)
                nc.scalar.activation(gT[:, sl], gT[:, sl], ACT.Exp, scale=-1.0).then_inc(sem("ef"), 1)
                if h:
                    act.wait_ge(sem("q_ready"), h)
                nc.scalar.activation(tmp, hqT[:, sl], ACT.Exp, scale=-1.0).then_inc(sem("eq"), 1)
                act.wait_ge(sem("f_ready"), h + 1)
                nc.scalar.activation(gT[:, sl], gT[:, sl], ACT.Ln).then_inc(sem("lnf"), 1)
            k = 0
            for h in range(H):
                for l in range(NLEV):
                    k += 1
                    act.wait_ge(sem("diff"), k)
                    n = TOK if LEVELS[l] < NT else SEQ
                    x = X[l % 2]
                    nc.scalar.activation(x[:, 0:n], x[:, 0:n], ACT.Exp).then_inc(sem("expd"), 1)
                act.wait_ge(sem("tails"), h + 1)
                sl = slice(h * TOK, (h + 1) * TOK)
                nc.scalar.activation(X[0], gT[:, sl], ACT.Exp).then_inc(sem("etail"), 1)
                nc.scalar.activation(X[1], X[1], ACT.Exp).then_inc(sem("etail"), 1)
                for c in range(8):
                    if c % 4 == 0:
                        act.wait_ge(sem("kdn_ps"), 2 * h + c // 4 + 1)
                        nc.scalar.activation(KdN[:, (c // 4) * 512:(c // 4 + 1) * 512], ps[2 + c // 4][:, :], ACT.Copy).then_inc(sem("kdn"), 1)
                for c in range(8):
                    act.wait_ge(sem("o_ps"), 8 * h + c + 1)
                    nc.scalar.activation(hi[:, c * HW + h * P:c * HW + (h + 1) * P], ps[4 + c % 2][:, 0:P], ACT.Copy).then_inc(sem("o_ev"), 1)
                act.wait_ge(sem("os_ps"), h + 1)
                nc.scalar.activation(hi[0:SMP, 8 * HW + h * P:8 * HW + (h + 1) * P], ps[0][0:SMP, 0:P], ACT.Copy).then_inc(sem("o_ev"), 1)
            act.wait_ge(sem("o_ev"), 9 * H)
            nc.scalar.activation(kkT[:, 0:4096], hi[:, 0:4096], ACT.Square).then_inc(sem("sq"), 1)
            nc.scalar.activation(gT[0:SMP, 0:512], hi[0:SMP, 4096:4608], ACT.Square).then_inc(sem("sq"), 1)
            nc.scalar.activation(hqT[:, 0:4096], gate[:, 0:4096], ACT.Exp, scale=-1.0).then_inc(sem("sq"), 1)
            nc.scalar.activation(gT[0:SMP, 512:1024], gate[0:SMP, 4096:4608], ACT.Exp, scale=-1.0).then_inc(sem("sq"), 1)
            act.wait_ge(sem("ms2"), 1)
            ch.step(nc.scalar.activation(rstd2, ss2, ACT.Ln))
            ch.wait()
            nc.scalar.activation(rstd2, rstd2, ACT.Exp, scale=-0.5).then_inc(sem("rstd2"), 1)
            phase_end(act, 2)
            act.wait_ge(sem("lam_ps"), 1)
            nc.scalar.activation(lamp, ps[7][:, 0:2], ACT.Exp).then_inc(sem("lam_e"), 1)
            n = 0
            for h in range(H):
                for i in range(8):
                    zb = zp[n % 2]
                    for m in range(2):
                        act.wait_ge(sem("z_ready"), 2 * n + m + 1)
                        sl = slice(m * 1024, m * 1024 + (i + 1) * P)
                        a = att[:, 8 * (n % 2):8 * (n % 2) + 8]
                        nc.scalar.activation(zb[:, sl], zb[:, sl], ACT.Exp, bias=a[:, m:m + 1],
                                             accum_out=a[:, 2 + m:3 + m]).then_inc(sem("p_ready"), 1)
                    for j in range(0, i + 1, 4):
                        act.wait_ge(sem("pT_ps"), cumT[(h, i, j)])
                        w = min(4, i + 1 - j) * P
                        nc.scalar.activation(pT[n % 2][:, j * P:j * P + w], ps[4 + (j // 4)][:, 0:w], ACT.Copy).then_inc(sem("pT"), 1)
                    act.wait_ge(sem("oa_ps"), n + 1)
                    ch.step(nc.scalar.activation(o_sb[n % 2], ps[6][:, 0:P], ACT.Square, accum_out=a[:, 6:7]))
                    ch.wait()
                    act.sem_inc(sem("oss"), 1)
                    act.wait_ge(sem("oms"), n + 1)
                    ch.step(nc.scalar.activation(a[:, 7:8], a[:, 6:7], ACT.Ln))
                    ch.wait()
                    nc.scalar.activation(a[:, 7:8], a[:, 7:8], ACT.Exp, scale=-0.5).then_inc(sem("orstd"), 1)
                    n += 1
            act.drain().then_inc(sem("prompt_left"), 1)

            def keys(b, k0):
                for j in range(0, PAGES, 2):
                    act.wait_ge(sem("page_free"), k0 + RING + j + 1)
                    nc.scalar.activation(kTd[j % 4], ps[j % 4][:, :], ACT.Copy).then_inc(sem("kt_even"), 1)

            def soft(b):
                act.wait_ge(sem("z_shift"), b + 1)
                nc.scalar.activation(z, z, ACT.Exp).then_inc(sem("z_exp"), 1)

            act.wait_ge(sem("prompt_gone"), 1)
            keys(0, 0)
            with act.Fori(0, NB - 1) as t:
                soft(t)
                keys(t + 1, t * 64 + 32)
            soft(NB - 1)
            act.wait_ge(sem("dms"), 1)
            ch.step(nc.scalar.activation(fin[:, 256:384], fin[:, 128:256], ACT.Ln))
            ch.wait()
            nc.scalar.activation(fin[:, 256:384], fin[:, 256:384], ACT.Exp, scale=-0.5).then_inc(sem("drstd"), 1)
            act.wait_ge(sem("rw"), 64)
        @block.tensor
        def _(pe):
            pe.wait_ge(sem("tab"), 16)
            pe.wait_ge(sem("ones"), 1)
            for i in range(TILES):
                r = ROWS[i]
                pe.wait_ge(sem("xn"), i + 1)
                if i >= 4:
                    pe.wait_ge(sem("hT"), i - 3)
                for k in range(KC):
                    b = ps[(2 * i + k // 4) % 8]
                    last_mm = nc.tensor.transpose(b[:, (k % 4) * P:(k % 4) * P + r], x_all[0:r, i * D + k * P:i * D + (k + 1) * P], ident[0:r, 0:r])
                last_mm.then_inc(sem("xT_ps"), 1)
            pe.wait_ge(sem("hT"), TILES)
            for g, (s, kind, dst, half, c, n) in enumerate(items):
                if g == 0 or items[g - 1][0] != s:
                    pe.wait_ge(sem(f"w_in{s % 3}"), 16 * (s // 3 + 1))
                if g >= 8:
                    for q in ("T", "N"):
                        if items[g - 8][1] == q:
                            pe.wait_ge(sem(f"ev_{q}"), upto[q][g - 7])
                w = head3(wring[s % 3], 256)
                for k in range(KC):
                    if kind == "T":
                        mm = nc.tensor.matmul(ps[g % 8][:, 0:N3], w[:, k, c * P:(c + 1) * P],
                                              hT[:, k * TOK + n * N3:k * TOK + (n + 1) * N3], start=(k == 0), stop=(k == KC - 1))
                    else:
                        mm = nc.tensor.matmul(ps[g % 8][0:ROWS[c], 0:256], tok(hT, k, c), w[:, k, :],
                                              start=(k == 0), stop=(k == KC - 1))
                mm.then_inc(sem("proj"), 1)
            pe.wait_ge(sem("ev_T"), upto["T"][-1])
            pe.wait_ge(sem("ev_N"), upto["N"][-1])
            for i in range(TILES):
                r = ROWS[i]
                if i >= 2:
                    pe.wait_ge(sem("knat_ready"), i - 1)
                for h in range(H):
                    mm = nc.tensor.transpose(ps[i % 2][0:r, h * P:(h + 1) * P], tok(kT, h, i), ident)
                mm.then_inc(sem("knat_ps"), 1)
            phase_end(pe, 1)
            k = 0
            for h in range(H):
                if h:
                    pe.wait_ge(sem("o_ev"), 9 * h)
                for l in range(NLEV + 1):
                    if l < NLEV:
                        pe.wait_ge(sem("xl_ready"), NLEV * h + l + 1)
                    else:
                        pe.wait_ge(sem("q_ready"), H)
                    bb = 2 * (l % 2)
                    if k >= 2:
                        pe.wait_ge(sem("lev_ev"), k - 1)
                    for c in range(8):
                        if l < NLEV:
                            a = b_ = X[l % 2][:, c * P:(c + 1) * P]
                        else:
                            a = tok(kkT, h, c)
                            b_ = tok(hqT, h, c)
                        mm = nc.tensor.matmul(ps[bb + c // 4][:, (c % 4) * P:(c % 4 + 1) * P], a, b_, start=True, stop=True)
                    if l >= NLEV - 2:
                        a = X[l % 2][:, SEQ:TOK] if l < NLEV else tok(kkT, h, 8)
                        b_ = X[l % 2][:, SEQ:TOK] if l < NLEV else tok(hqT, h, 8)
                        mm = nc.tensor.matmul(ps[6 + l % 2][0:SMP, 0:SMP], a, b_, start=True, stop=True)
                    mm.then_inc(sem("lev_ps"), 1)
                    k += 1
                pe.wait_ge(sem("kd_ready"), h + 1)
                pe.wait_ge(sem("lev_ev"), k)
                for c in range(9):
                    b = ps[2 + c // 4] if c < 8 else ps[1]
                    mm = nc.tensor.transpose(b[0:ROWS[c], (c % 4) * P:(c % 4 + 1) * P], tok(kkT, h, c), ident)
                    if c in (3, 7):
                        mm.then_inc(sem("kdn_ps"), 1)
                mm.then_inc(sem("kdns_ps"), 1)
                pe.wait_ge(sem("kdn"), 2 * h + 2)
                for c in range(8):
                    vv = hi[:, c * HW + h * P:c * HW + (h + 1) * P]
                    nc.tensor.matmul(ps[6 + c % 2][:, 0:P], KdN[:, c * P:(c + 1) * P], vv, start=True, stop=True).then_inc(sem("ds_ps"), 1)
                    if c >= 2:
                        pe.wait_ge(sem("o_ev"), 9 * h + c - 1)
                    nc.tensor.matmul(ps[4 + c % 2][:, 0:P], AT[:, c * P:(c + 1) * P], vv, start=True, stop=False)
                    pe.wait_ge(sem("state"), 9 * h + c + 1)
                    nc.tensor.matmul(ps[4 + c % 2][:, 0:P], tok(hqT, h, c), S[:, c * P:(c + 1) * P], start=False, stop=True).then_inc(sem("o_ps"), 1)
                pe.wait_ge(sem("state"), 9 * h + 9)
                pe.wait_ge(sem("smp_ready"), h + 1)
                pe.wait_ge(sem("s0_in"), 16 * (h + 1))
                vs = hi[0:SMP, 8 * HW + h * P:8 * HW + (h + 1) * P]
                for b in range(NB):
                    mm = nc.tensor.matmul(ps[2 + b // 4][:, (b % 4) * P:(b % 4 + 1) * P], KdM[0:SMP, b * P:(b + 1) * P], vs, start=True, stop=True)
                mm.then_inc(sem("dss_ps"), 1)
                nc.tensor.matmul(ps[0][0:SMP, 0:P], ATs[0:SMP, :], vs, start=True, stop=False)
                for b in range(NB):
                    mm = nc.tensor.matmul(ps[0][0:SMP, 0:P], Qpad[:, b * SMP:(b + 1) * SMP], S0[:, b * P:(b + 1) * P], start=False, stop=(b == NB - 1))
                mm.then_inc(sem("os_ps"), 1)
            pe.wait_ge(sem("og_ready"), 1)
            for i in range(TILES):
                if i >= 2:
                    pe.wait_ge(sem("og_ev"), i - 1)
                for h in range(H):
                    mm = nc.tensor.transpose(ps[i % 2][:, h * P:h * P + ROWS[i]], hi[0:ROWS[i], i * HW + h * P:i * HW + (h + 1) * P], ident[0:ROWS[i], 0:ROWS[i]])
                mm.then_inc(sem("og_ps"), 1)
            phase_end(pe, 2)
            pe.sem_inc(sem("page_free"), RING)
            pe.wait_ge(sem("oh_in"), 16)
            pe.wait_ge(sem("lam_in"), 1)
            nc.tensor.matmul(ps[7][:, 0:2], ones[0:QK, :], lamv[0:QK, 0:2], start=True, stop=True).then_inc(sem("lam_ps"), 1)
            pe.wait_ge(sem("rb_ready"), 1)
            R = BUCKETS + 1
            for h in range(H):
                pe.wait_ge(sem("rbb"), h + 1)
                nc.tensor.matmul(ps[h][:, 0:384], pT[0][0:R, h * P:(h + 1) * P], oh[0:R, 0:384], start=True, stop=True).then_inc(sem("band_ps"), 1)
            for t in range(NT):
                nc.tensor.matmul(ps[4][:, t * H:(t + 1) * H], oh[0:R, 384 + t * P:384 + (t + 1) * P], rb[0:R, :], start=True, stop=True)
                nc.tensor.matmul(ps[5][0:SMP, t * H:(t + 1) * H], oh[0:R, 1024 + t * SMP:1024 + (t + 1) * SMP], rb[0:R, :], start=True, stop=True)
            nc.tensor.matmul(ps[4][:, 16:16 + H], oh[0:R, 896:1024], rb[0:R, :], start=True, stop=True).then_inc(sem("bias_ps"), 1)
            pe.wait_ge(sem("band_ready"), 1)
            units = [(h, i) for h in range(H) for i in range(8)]

            def scores(n):
                h, i = units[n]
                for m in range(2):
                    if n or m:
                        pe.wait_ge(sem("z_ready"), 2 * n + m - 1) if 2 * n + m - 1 > 0 else None
                    rows = slice(QK * m, QK * m + QK)
                    for j in range(0, i + 1, 4):
                        w = min(4, i + 1 - j) * P
                        mm = nc.tensor.matmul(ps[2 * m + j // 4][:, 0:w], qT[rows, h * TOK + i * P:h * TOK + (i + 1) * P],
                                              kT[rows, h * TOK + j * P:h * TOK + j * P + w], start=True, stop=True)
                    mm.then_inc(sem("s_ps"), 1)

            def weigh(n):
                h, i = units[n]
                pe.wait_ge(sem("a_ready"), n + 1)
                for j in range(i + 1):
                    mm = nc.tensor.transpose(ps[4 + j // 4][:, (j % 4) * P:(j % 4 + 1) * P], zp[n % 2][:, j * P:(j + 1) * P], ident)
                    if j % 4 == 3 or j == i:
                        mm.then_inc(sem("pT_ps"), 1)
                pe.wait_ge(sem("pT"), cumT[(h, i, i // 4 * 4)])
                if n:
                    pe.wait_ge(sem("o_norm"), n)
                for j in range(i + 1):
                    mm = nc.tensor.matmul(ps[6][:, 0:P], pT[n % 2][:, j * P:(j + 1) * P], v_nat[:, j * HW + h * P:j * HW + (h + 1) * P],
                                          start=(j == 0), stop=(j == i))
                mm.then_inc(sem("oa_ps"), 1)

            def turn(n):
                pe.wait_ge(sem("o_norm"), n + 1)
                if n:
                    pe.wait_ge(sem("mix_ev"), n)
                nc.tensor.transpose(ps[7][:, 0:P], o_sb[n % 2], ident).then_inc(sem("ot_ps"), 1)

            scores(0)
            for n in range(len(units)):
                if n + 1 < len(units):
                    scores(n + 1)
                if n:
                    turn(n - 1)
                weigh(n)
            turn(len(units) - 1)
            pe.wait_ge(sem("prompt_gone"), 1)

            pe.wait_ge(sem("qblk"), 1)

            def keys(b, k0):
                def flip(j):
                    pe.wait_ge(sem(f"page{j % RING}"), k0 + (j // RING + 1) * 16)
                    for h in range(H):
                        mm = nc.tensor.transpose(ps[j % 4][:, h * P:(h + 1) * P], pages[j % RING][:, h * P:(h + 1) * P], ident)
                    mm.then_inc(sem("page_free"), 1)

                def multiply(j):
                    pe.wait_ge(sem("kt_even" if j % 2 == 0 else "kt_odd"), b * 16 + j // 2 + 1)
                    for h in range(H):
                        mm = nc.tensor.matmul(ps[4 + j // 16][:, (j % 16) * COLS + h * 8:(j % 16) * COLS + h * 8 + 8],
                                              kTd[j % 4][:, h * P:(h + 1) * P], qcur(b, h), start=True, stop=True)
                    mm.then_inc(sem("qk"), 1)

                flip(0)
                flip(1)
                pe.wait_ge(sem("z_in"), b + 1)
                for h in range(H):
                    nc.tensor.matmul(ps[6][0:SMP, 64 + h * 8:72 + h * 8], knew[:, h * SMP:(h + 1) * SMP], qcur(b, h), start=True, stop=True)
                for j in range(PAGES):
                    if j + 2 < PAGES:
                        flip(j + 2)
                    multiply(j)

            def qcur(b, h):
                if isinstance(b, int):
                    return qblk[:, b * COLS + h * 8:b * COLS + h * 8 + 8]
                return qblk[:, ds(b * COLS + h * 8, 8)]

            def top(b):
                pe.wait_ge(sem("mxc"), b + 1)
                nc.tensor.transpose(ps[7][0:COLS, 0:P], mxc, ident).then_inc(sem("mx_ps"), 1)
                pe.wait_ge(sem("mdg"), b + 1)
                nc.tensor.matmul(ps[7][:, 128:128 + COLS], ones[0:COLS, :], dg[0:COLS, :], start=True, stop=True).then_inc(sem("mb_ps"), 1)

            def values(b, k0):
                pe.wait_ge(sem("psum_s"), b + 1)
                nc.tensor.matmul(ps[7][:, 192:192 + COLS], ones, psums, start=True, stop=True).then_inc(sem("den_ps"), 1)
                first = True
                for j in range(PAGES + 1):
                    if j < PAGES:
                        pe.wait_ge(sem(f"page{j % RING}"), k0 + (j // RING + 1) * 16)
                    for h in range(H):
                        lhs = pages[j % RING][:, h * P:(h + 1) * P] if j < PAGES else v_nat[0:SMP, 8 * HW + h * P:8 * HW + (h + 1) * P]
                        rhs = z[0:(P if j < PAGES else SMP), j * COLS + h * 8:j * COLS + h * 8 + 8]
                        mm = nc.tensor.matmul(ps[6][:, h * 8:h * 8 + 8], lhs, rhs, start=first, stop=(j == PAGES and h == H - 1), skip_group_check=True)
                        first = False
                    if j < PAGES:
                        mm.then_inc(sem("page_free"), 1)
                mm.then_inc(sem("pv_mm"), 1)

            keys(0, 0)
            top(0)
            with pe.Fori(0, NB - 1) as t:
                keys(t + 1, t * 64 + 32)
                values(t, t * 64 + 64)
                top(t + 1)
            values(NB - 1, 7 * 64 + 32)
            pe.wait_ge(sem("fsq"), 1)
            nc.tensor.matmul(ps[0][:, 0:128], ones, fin[:, 128:256], start=True, stop=True).then_inc(sem("fms_ps"), 1)
        @block.vector
        def _(dve):
            V = nc.vector
            ch = Chain(dve, sem("dve"))

            def step(ins):
                ch.step(ins)
                ch.wait()

            def mean_eps(a, n):
                return V.tensor_scalar(a, a, 1.0 / n, EPS, ALU.mult, ALU.add)

            dve.wait_ge(sem("ss"), TILES)
            dve.wait_ge(sem("small0"), 1)
            mean_eps(ss, D).then_inc(sem("ms"), 1)
            dve.wait_ge(sem("rstd"), 1)

            def norm_tile(i):
                r = ROWS[i]
                xi = x_all[0:r, i * D:(i + 1) * D]
                V.tensor_scalar(xi, xi, rstd[0:r, i:i + 1], None, ALU.mult).then_inc(sem("xn"), 1)

            norm_tile(0)
            dve.wait_ge(sem("vecs"), NV_TOTAL)
            for i in range(TILES):
                r = ROWS[i]
                if i + 1 < TILES:
                    norm_tile(i + 1)
                dve.wait_ge(sem("xT_ps"), i + 1)
                for g in range(2):
                    o = head3(hT, TOK)[:, 4 * g:4 * g + 4, i * P:i * P + r]
                    last = V.tensor_tensor(o, head3(ps[(2 * i + g) % 8][:, :], P)[:, :, 0:r],
                                           n1w[:, 4 * g:4 * g + 4].unsqueeze(2).broadcast_to([P, 4, r]), ALU.mult)
                last.then_inc(sem("hT"), 1)
            for g, (s, kind, dst, half, c, n) in enumerate(items):
                if kind != "N":
                    continue
                dve.wait_ge(sem("proj"), g + 1)
                r = ROWS[c]
                V.tensor_copy(dst[0:r, c * HW + half * 256:c * HW + half * 256 + 256], ps[g % 8][0:r, 0:256]).then_inc(sem("ev_N"), 1)
            for i in range(TILES):
                dve.wait_ge(sem("knat_ps"), i + 1)
                if i >= 2:
                    dve.wait_ge(sem(f"knat_out{i % 2}"), 16 * (i // 2))
                V.tensor_copy(knat[i % 2][0:ROWS[i], :], ps[i % 2][0:ROWS[i], :]).then_inc(sem("knat_ready"), 1)
            phase_end(dve, 1)

            dve.wait_ge(sem("pool"), 3)
            V.tensor_tensor(lg1, lg1, lg0, ALU.subtract).then_inc(sem("lbd"), 1)
            dve.wait_ge(sem("lbe"), 1)
            step(V.tensor_scalar(lbT, lbT, 1.0, None, ALU.add))
            step(V.reciprocal(lbT, lbT))
            step(V.tensor_scalar(omlb, lbT, -1.0, 1.0, ALU.mult, ALU.add))
            for h in range(H):
                sl = slice(h * TOK, (h + 1) * TOK)
                g, q, kk = gT[:, sl], hqT[:, sl], kkT[:, sl]
                dve.wait_ge(sem("ef"), h + 1)
                step(V.tensor_scalar(g, g, 1.0, None, ALU.add))
                step(V.reciprocal(g, g))
                ch.step(V.tensor_scalar(g, g, omlb[:, h:h + 1], lbT[:, h:h + 1], ALU.mult, ALU.add))
                ch.wait()
                V.tensor_scalar(kk, g, -1.0, 1.0, ALU.mult, ALU.add).then_inc(sem("f_ready"), 1)
                dve.wait_ge(sem("eq"), h + 1)
                step(V.tensor_scalar(tmp, tmp, 1.0, None, ALU.add))
                step(V.reciprocal(tmp, tmp))
                V.scalar_tensor_tensor(out=q, in0=q, scalar=P ** -0.5, in1=tmp, op0=ALU.mult, op1=ALU.mult).then_inc(sem("q_ready"), 1)
                dve.wait_ge(sem("lnf"), h + 1)
                ch.step(V.tensor_tensor_scan(g, reset, g, 0.0, ALU.mult, ALU.add))
            ch.wait()
            k = 0
            lev = cst("level").bitcast(I32)
            for h in range(H):
                sl = slice(h * TOK, (h + 1) * TOK)
                g, q, kk = gT[:, sl], hqT[:, sl], kkT[:, sl]
                if h:
                    dve.wait_ge(sem("o_ps"), 8 * h)
                    dve.wait_ge(sem("os_ps"), h)
                    dve.wait_ge(sem("snew_out"), 16 * h)
                    dve.wait_ge(sem("state_out"), 16 * h)
                step(V.memset(AT, 0.0))
                step(V.memset(ATs, 0.0))
                step(V.memset(Qpad, 0.0))

                def diff(l):
                    w = LEVELS[l]
                    n = TOK if w < NT else SEQ
                    gg = g[:, 0:n].rearrange("p (b w) -> p b w", w=2 * w)
                    xx = X[l % 2][:, 0:n].rearrange("p (b w) -> p b w", w=2 * w)
                    mid = gg[:, :, w - 1:w].broadcast_to([P, n // (2 * w), w])
                    if l >= 2:
                        dve.wait_ge(sem("lev_ps"), k0 + l - 1)
                    V.tensor_tensor(xx[:, :, 0:w], mid, gg[:, :, 0:w], ALU.subtract)
                    V.tensor_tensor(xx[:, :, w:2 * w], gg[:, :, w:2 * w], mid, ALU.subtract).then_inc(sem("diff"), 1)

                def scale(l):
                    w = LEVELS[l]
                    n = TOK if w < NT else SEQ
                    dve.wait_ge(sem("expd"), NLEV * h + l + 1)
                    xx = X[l % 2][:, 0:n].rearrange("p (b w) -> p b w", w=2 * w)
                    V.tensor_tensor(xx[:, :, 0:w], xx[:, :, 0:w], kk[:, 0:n].rearrange("p (b w) -> p b w", w=2 * w)[:, :, 0:w], ALU.mult)
                    V.tensor_tensor(xx[:, :, w:2 * w], xx[:, :, w:2 * w], q[:, 0:n].rearrange("p (b w) -> p b w", w=2 * w)[:, :, w:2 * w], ALU.mult).then_inc(sem("xl_ready"), 1)

                def collect(l):
                    dve.wait_ge(sem("lev_ps"), k0 + l + 1)
                    if l:
                        dve.wait_ge(sem("lev_ev"), k0 + l)
                    for c in range(2):
                        last = V.copy_predicated(AT[:, c * 512:(c + 1) * 512].rearrange("p (a b) -> p a b", b=P),
                                                 lev[:, l * P:(l + 1) * P].unsqueeze(1).broadcast_to([P, 4, P]),
                                                 ps[2 * (l % 2) + c][:, :].rearrange("p (a b) -> p a b", b=P))
                    if l >= NLEV - 2:
                        last = V.copy_predicated(ATs[0:SMP, :], lev[0:SMP, l * P:l * P + SMP], ps[6 + l % 2][0:SMP, 0:SMP])
                    last.then_inc(sem("lev_ev"), 1)

                k0 = (NLEV + 1) * h
                diff(0)
                diff(1)
                scale(0)
                for l in range(NLEV):
                    if l + 1 < NLEV:
                        scale(l + 1)
                    collect(l)
                    if l + 2 < NLEV:
                        diff(l + 2)
                collect(NLEV)
                k += NLEV + 1
                gp, gs = head3(g[:, 0:SEQ], P), head3(g[:, SEQ:TOK], NT)
                x1p, x1s = head3(X[1][:, 0:SEQ], P), head3(X[1][:, SEQ:TOK], NT)
                V.tensor_tensor(x1p, gp[:, :, P - 1:P].broadcast_to([P, 8, P]), gp, ALU.subtract)
                V.tensor_tensor(x1s, gs[:, :, NT - 1:NT].broadcast_to([P, NB, NT]), gs, ALU.subtract).then_inc(sem("tails"), 1)
                dve.wait_ge(sem("etail"), 2 * h + 2)
                V.tensor_tensor(kk, kk, X[1], ALU.mult).then_inc(sem("kd_ready"), 1)
                step(V.tensor_tensor(q, q, X[0], ALU.mult))
                step(V.tensor_copy(bass.AP(tensor=Qpad.tensor, offset=Qpad.offset, ap=[list(Qpad.ap[0]), [SMP + NT, NB], [1, NT]]),
                                   head3(q[:, SEQ:TOK], NT)))
                ch.step(V.memset(S[:, 0:P], 0.0))
                ch.wait()
                dve.sem_inc(sem("state"), 1)
                for c in range(8):
                    dve.wait_ge(sem("ds_ps"), 8 * h + c + 1)
                    V.scalar_tensor_tensor(out=S[:, (c + 1) * P:(c + 2) * P], in0=S[:, c * P:(c + 1) * P],
                                           scalar=X[0][:, c * P + P - 1:c * P + P], in1=ps[6 + c % 2][:, 0:P],
                                           op0=ALU.mult, op1=ALU.add).then_inc(sem("state"), 1)
                    dve.wait_ge(sem("state"), 9 * h + c + 2)
                dve.sem_inc(sem("state_ready"), 1)
                dve.wait_ge(sem("kdns_ps"), h + 1)
                dve.wait_ge(sem("o_ps"), 8 * h + 8)
                dve.sem_inc(sem("s0_free"), 1)
                for b in range(NB):
                    ch.step(V.tensor_scalar(KdM[0:SMP, b * P:(b + 1) * P], ps[1][0:SMP, 0:P], cst("own", SMP)[:, b:b + 1], None, ALU.mult))
                ch.wait()
                dve.sem_inc(sem("smp_ready"), 1)
                dve.wait_ge(sem("dss_ps"), h + 1)
                dve.wait_ge(sem("os_ps"), h + 1)
                for b in range(NB):
                    c = SEQ + b * NT + NT - 1
                    ch.step(V.scalar_tensor_tensor(out=S0[:, b * P:(b + 1) * P], in0=S0[:, b * P:(b + 1) * P], scalar=X[0][:, c:c + 1],
                                                   in1=ps[2 + b // 4][:, (b % 4) * P:(b % 4 + 1) * P], op0=ALU.mult, op1=ALU.add))
                ch.wait()
                dve.sem_inc(sem("snew_ready"), 1)
            dve.wait_ge(sem("sq"), 4)
            step(V.memset(ss2, 1.0))
            step(V.tensor_reduce(ss2[:, 0:32], head3(kkT[:, 0:4096], P), AX, ALU.add))
            step(V.tensor_reduce(ss2[0:SMP, 32:36], head3(gT[0:SMP, 0:512], P), AX, ALU.add))
            mean_eps(ss2, P).then_inc(sem("ms2"), 1)
            eg, egs = hqT[:, 0:4096], gT[0:SMP, 512:1024]
            for e, gg in ((eg, gate[:, 0:4096]), (egs, gate[0:SMP, 4096:4608])):
                step(V.tensor_scalar(e, e, 1.0, None, ALU.add))
                step(V.reciprocal(e, e))
                step(V.tensor_tensor(e, e, gg, ALU.mult))
            dve.wait_ge(sem("rstd2"), 1)
            for o, r2, e in ((hi[:, 0:4096], rstd2[:, 0:32], eg), (hi[0:SMP, 4096:4608], rstd2[0:SMP, 32:36], egs)):
                n = r2.shape[1]
                step(V.tensor_tensor(head3(o, P), head3(o, P), r2.unsqueeze(2).broadcast_to([o.shape[0], n, P]), ALU.mult))
                step(V.tensor_tensor(o, o, e, ALU.mult))
            dve.sem_inc(sem("og_ready"), 1)
            for i in range(TILES):
                dve.wait_ge(sem("og_ps"), i + 1)
                r = ROWS[i]
                V.tensor_scalar(head3(mixT, TOK)[:, 4:8, i * P:i * P + r], head3(ps[i % 2][:, :], P)[:, :, 0:r], hgw, None, ALU.mult).then_inc(sem("og_ev"), 1)
            phase_end(dve, 2)

            step(V.tensor_tensor(lamv[0:QK, 0:2], lamv[0:QK, 0:2], lamv[0:QK, 2:4], ALU.mult))
            dve.sem_inc(sem("lam_in"), 1)
            dve.sem_inc(sem("rb_ready"), 1)
            for h in range(H):
                V.tensor_copy(pT[0][0:BUCKETS + 1, h * P:(h + 1) * P], rb[0:BUCKETS + 1, h:h + 1].broadcast_to([BUCKETS + 1, P])).then_inc(sem("rbb"), 1)
            dve.wait_ge(sem("lam_e"), 1)
            step(V.tensor_tensor(nlam, lamp[:, 1:2], lamp[:, 0:1], ALU.subtract))
            step(V.tensor_scalar(nlam, nlam, -LAM_INIT, None, ALU.add))
            step(V.tensor_scalar(daw, daw, 1.0 - LAM_INIT, None, ALU.mult))
            for h in range(H):
                dve.wait_ge(sem("band_ps"), h + 1)
                if h:
                    dve.wait_ge(sem("band_out"), 16 * h)
                V.tensor_copy(rowb, ps[h][:, 0:384]).then_inc(sem("rowb"), 1)
            dve.wait_ge(sem("bias_ps"), 1)
            step(V.tensor_copy(bnew[0:SMP, :], ps[5][0:SMP, 0:16]))
            for m in range(2):
                hm = lambda a: a.rearrange("p (h m t) -> p h m t", h=H, m=2)[:, :, m, :]
                step(V.tensor_copy(hm(last_), ps[4][:, 0:16].rearrange("p (t h) -> p h t", h=H)))
                step(V.tensor_copy(hm(far), ps[4][:, 16:20].unsqueeze(2).broadcast_to([P, H, NT])))
                for b in range(NB):
                    step(V.tensor_scalar(hm(biasn[0:SMP, b * COLS:(b + 1) * COLS]), bnew[0:SMP, :].rearrange("p (t h) -> p h t", h=H),
                                         cst("other", SMP)[:, b:b + 1], None, ALU.add))
            for h in range(H):
                step(V.tensor_copy(band[:, h * 1152:h * 1152 + 896], ps[4][:, 16 + h:17 + h].broadcast_to([P, 896])))
            dve.wait_ge(sem("band_in"), 16 * H)
            step(V.memset(qblk, 0.0))
            for h in range(H):
                for m in range(2):
                    o = qblk[QK * m:QK * m + QK, :].rearrange("p (b h m t) -> p b h m t", b=NB, h=H, m=2)[:, :, h, m, :]
                    step(V.tensor_copy(o, head3(qT[QK * m:QK * m + QK, h * TOK + SEQ:(h + 1) * TOK], NT)))
                step(V.tensor_copy(knew[:, h * SMP:(h + 1) * SMP], kT[:, h * TOK + SEQ:(h + 1) * TOK]))
            dve.sem_inc(sem("qblk"), 1)
            dve.sem_inc(sem("band_ready"), 1)

            units = [(h, i) for h in range(H) for i in range(8)]

            def bias_max(n):
                h, i = units[n]
                w = (i + 1) * P
                a = att[:, 8 * (n % 2):8 * (n % 2) + 8]
                for m in range(2):
                    dve.wait_ge(sem("s_ps"), 2 * n + m + 1)
                    if n >= 2 and m == 0:
                        dve.wait_ge(sem("oa_ps"), n - 1)
                        dve.wait_ge(sem("orstd"), n - 1)
                    for j in range(0, i + 1, 4):
                        ww = min(4, i + 1 - j) * P
                        last = V.tensor_tensor(zp[n % 2][:, m * 1024 + j * P:m * 1024 + j * P + ww], ps[2 * m + j // 4][:, 0:ww],
                                               band[:, h * 1152 + 1152 - w + j * P:h * 1152 + 1152 - w + j * P + ww], ALU.add)
                    step(last)
                    step(V.tensor_reduce(a[:, m:m + 1], zp[n % 2][:, m * 1024:m * 1024 + w], AX, ALU.max, negate=True))
                    dve.sem_inc(sem("z_ready"), 1)

            def combine(n):
                h, i = units[n]
                w = (i + 1) * P
                a = att[:, 8 * (n % 2):8 * (n % 2) + 8]
                zb = zp[n % 2]
                dve.wait_ge(sem("p_ready"), 2 * n + 2)
                step(V.reciprocal(a[:, 4:6], a[:, 2:4]))
                step(V.tensor_tensor(a[:, 5:6], a[:, 5:6], nlam, ALU.mult))
                step(V.tensor_scalar(zb[:, 0:w], zb[:, 0:w], a[:, 4:5], None, ALU.mult))
                V.scalar_tensor_tensor(out=zb[:, 0:w], in0=zb[:, 1024:1024 + w], scalar=a[:, 5:6], in1=zb[:, 0:w],
                                       op0=ALU.mult, op1=ALU.add).then_inc(sem("a_ready"), 1)

            def finish(n):
                h, i = units[n]
                a = att[:, 8 * (n % 2):8 * (n % 2) + 8]
                dve.wait_ge(sem("oss"), n + 1)
                mean_eps(a[:, 6:7], P).then_inc(sem("oms"), 1)
                dve.wait_ge(sem("orstd"), n + 1)
                V.tensor_scalar(o_sb[n % 2], ps[6][:, 0:P], a[:, 7:8], None, ALU.mult).then_inc(sem("o_norm"), 1)

            def place(n):
                h, i = units[n]
                dve.wait_ge(sem("ot_ps"), n + 1)
                V.tensor_scalar(mixT[:, h * TOK + i * P:h * TOK + (i + 1) * P], ps[7][:, 0:P], daw, None, ALU.mult).then_inc(sem("mix_ev"), 1)

            bias_max(0)
            for n in range(len(units)):
                combine(n)
                if n + 1 < len(units):
                    bias_max(n + 1)
                if n:
                    place(n - 1)
                finish(n)
            place(len(units) - 1)
            dve.wait_ge(sem("prompt_left"), 1)
            dve.wait_ge(sem("mix_ev"), len(units))
            dve.sem_inc(sem("prompt_done"), 1)
            dve.sem_inc(sem("prompt_gone"), 2)

            step(V.memset(z[:, PAGES * COLS:], NEG))
            dve.sem_inc(sem("z_in"), 1)

            def evacuate(b, k0):
                for j in range(1, PAGES, 2):
                    dve.wait_ge(sem("page_free"), k0 + RING + j + 1)
                    V.tensor_copy(kTd[j % 4], ps[j % 4][:, :]).then_inc(sem("kt_odd"), 1)

            z3 = head3(z, COLS)

            def take_scores(b):
                dve.wait_ge(sem("qk"), b * PAGES + PAGES)
                ch.wait()
                fb = far.unsqueeze(1)
                ch.step(V.tensor_tensor(z3[:, 0:16, :], head3(ps[4][:, :], COLS), fb.broadcast_to([P, 16, COLS]), ALU.add))
                ch.step(V.tensor_tensor(z3[:, 16:31, :], head3(ps[5][:, 0:480], COLS), fb.broadcast_to([P, 15, COLS]), ALU.add))
                ch.step(V.tensor_tensor(z3[:, 31, :], ps[5][:, 480:512], last_, ALU.add))
                bn = biasn[0:SMP, ds(b * COLS, COLS)] if not isinstance(b, int) else biasn[0:SMP, b * COLS:(b + 1) * COLS]
                ch.step(V.tensor_tensor(z3[0:SMP, 32, :], ps[6][0:SMP, 64:64 + COLS], bn, ALU.add))
                ch.wait()
                dve.sem_inc(sem("z_in"), 1)
                V.tensor_reduce(mxc, z.rearrange("p (j c) -> p c j", c=COLS), AX, ALU.max).then_inc(sem("mxc"), 1)
                dve.wait_ge(sem("mx_ps"), b + 1)
                ch.step(V.tensor_reduce(mxr[0:COLS, :], ps[7][0:COLS, 0:P], AX, ALU.max))
                ch.wait()
                V.tensor_scalar(dg[0:COLS, :], ident[0:COLS, 0:COLS], mxr[0:COLS, :], None, ALU.mult).then_inc(sem("mdg"), 1)
                dve.wait_ge(sem("mb_ps"), b + 1)
                V.tensor_tensor(z3, z3, ps[7][:, 128:128 + COLS].unsqueeze(1).broadcast_to([P, PAGES + 1, COLS]), ALU.subtract).then_inc(sem("z_shift"), 1)

            def sums(b):
                dve.wait_ge(sem("z_exp"), b + 1)
                V.tensor_reduce(psums, z.rearrange("p (j c) -> p c j", c=COLS), AX, ALU.add).then_inc(sem("psum_s"), 1)

            def results(b):
                at_b = (lambda a: a[:, ds(b * COLS, COLS)]) if not isinstance(b, int) else (lambda a: a[:, b * COLS:(b + 1) * COLS])
                dve.wait_ge(sem("den_ps"), b + 1)
                ch.step(V.tensor_copy(at_b(sum_all), ps[7][:, 192:192 + COLS]))
                dve.wait_ge(sem("pv_mm"), b + 1)
                ch.step(V.tensor_copy(at_b(oT_all), ps[6][:, 0:COLS]))
                ch.step(V.memset(z[:, PAGES * COLS:], NEG))

            evacuate(0, 0)
            take_scores(0)
            with dve.Fori(0, NB - 1) as t:
                ch.enter(t, 8)
                sums(t)
                evacuate(t + 1, t * 64 + 32)
                results(t)
                take_scores(t + 1)
            ch.leave(NB - 1)
            sums(NB - 1)
            results(NB - 1)
            ch.wait()
            step(V.reciprocal(sum_all, sum_all))
            step(V.tensor_tensor(oT_all, oT_all, sum_all, ALU.mult))
            om = oT_all.rearrange("p (b h m t) -> p (b h) m t", b=NB, h=H, m=2)
            f0 = fin[:, 0:128].rearrange("p (a t) -> p a t", t=NT)
            step(V.scalar_tensor_tensor(out=f0, in0=om[:, :, 1, :], scalar=nlam, in1=om[:, :, 0, :], op0=ALU.mult, op1=ALU.add))
            V.tensor_tensor(fin[:, 128:256], fin[:, 0:128], fin[:, 0:128], ALU.mult).then_inc(sem("fsq"), 1)
            dve.wait_ge(sem("fms_ps"), 1)
            V.tensor_scalar(fin[:, 128:256], ps[0][:, 0:128], 1.0 / P, EPS, ALU.mult, ALU.add).then_inc(sem("dms"), 1)
            dve.wait_ge(sem("drstd"), 1)
            step(V.tensor_tensor(fin[:, 0:128], fin[:, 0:128], fin[:, 256:384], ALU.mult))
            for h in range(H):
                o = head3(mixT[:, h * TOK + SEQ:(h + 1) * TOK], NT)
                step(V.tensor_scalar(o, fin[:, 0:128].rearrange("p (b h t) -> p b h t", b=NB, h=H)[:, :, h, :], daw, None, ALU.mult))
        block_a.__exit__(None, None, None)
        nc.all_engine_barrier()
        nc.clear_and_free_semaphores(list(sems.values()))
        sems.clear()
        part[0] = "_b"
        nc.all_engine_barrier()

        block = ctx.enter_context(nc.Block())

        @block.sync
        def _(sp):
            for g in range(4):
                sp.dma_start(head3(x1, D)[:, 2 * g:2 * g + 2, :],
                             xp_v[:, 2 * g:2 * g + 2, :]).then_inc(sem(f"x1_in{g}"), 16)
            sp.dma_start(x1[0:SMP, 8 * D:9 * D], xs_v).then_inc(sem("x1_in4"), 16)
            for i in range(TILES):
                sp.wait_ge(sem("xh_ready"), i + 1)
                sp.dma_start(rows_d[i * P:i * P + ROWS[i], :], xh[i % 2][0:ROWS[i], :]).then_inc(sem(f"xh_out{i % 2}"), 16)
            phase_end(sp, 1)
            sp.wait_ge(sem("routed"), 1)
            nit = sp.value_load(nit_i[0:1, 0:1], min_val=1, max_val=PAIRS)
            with sp.Fori(0, nit) as t:
                for s in range(2):
                    e = sp.value_load(eid[0:1, ds(t * 2 + s, 1)], min_val=0, max_val=NE - 1)
                    sp.wait_ge(sem("ye_ps"), t * 2 + s + 1)
                    w13 = wslot[s][:, 0:4096].rearrange("p (k f) -> p k f", k=KC)
                    sp.dma_start(w13[:, :, 0:FF], w1_v[ds(e * D, D), :].rearrange("(k p) f -> p k f", p=P)).then_inc(sem(f"wexp{s}"), 16)
                    sp.dma_start(w13[:, :, FF:2 * FF], w3_v[ds(e * D, D), :].rearrange("(k p) f -> p k f", p=P)).then_inc(sem(f"wexp{s}"), 16)
                    sp.dma_start(wslot[s][:, 4096:6144].rearrange("p (k f) -> p k f", k=2),
                                 w2_v[ds(e * FF, FF), :].rearrange("(k p) f -> p k f", p=P)).then_inc(sem(f"wexp{s}"), 16)
            phase_end(sp, 2)
            for i in range(TILES):
                sp.wait_ge(sem("y_ready"), i + 1)
                dst = ys_v if i == TILES - 1 else yp_v[:, i, :]
                sp.dma_start(dst, ya[i % 2][0:ROWS[i], :]).then_inc(sem(f"y_out{i % 2}"), 16)
            sp.wait_ge(sem("y_out0"), 16 * 5)
            sp.wait_ge(sem("y_out1"), 16 * 4)

        @block.gpsimd
        def _(pool):
            nc.gpsimd.memset(zero_rows, 0.0).then_inc(sem("zeros"), 1)
            pool.wait_ge(sem("zeros"), 1)
            for j in range(SURE, CAP):
                pool.dma_start(ye_d[j * P:(j + 1) * P, :], zero_rows).then_inc(sem("zeros_out"), 16)
            nc.gpsimd.memset(ids_sb, 0).then_inc(sem("ids0"), 1)
            pool.wait_ge(sem("ids0"), 1)
            pool.dma_start(ids_d.rearrange("(p j) c -> p (j c)", p=P), ids_sb).then_inc(sem("ids0_out"), 16)
            nc.gpsimd.iota(payload.rearrange("p (i c) -> p i c", c=16), [[P, TILES], [0, 16]], base=0, channel_multiplier=1).then_inc(sem("payload"), 1)
            pool.wait_ge(sem("ids0_out"), 16)
            pool.wait_ge(sem("payload"), 1)
            pool.wait_ge(sem("slots_ready"), 1)
            for c in range(2):
                for i in range(TILES):
                    pool.indirect_dma_start(
                        out=ids_d, out_offset=bass.IndirectOffsetOnAxis(ap=row_i[0:ROWS[i], c * TILES + i:c * TILES + i + 1], axis=0),
                        in_=payload[0:ROWS[i], i * 16:(i + 1) * 16], in_offset=None).then_inc(sem("ids_out"), 16)
            pool.wait_ge(sem("ids_out"), 16 * 2 * TILES)
            pool.dma_start(ids_sb, ids_d.rearrange("(p j) c -> p (j c)", p=P)).then_inc(sem("ids_in"), 16)
            pool.wait_ge(sem("ids_in"), 16)
            pool.wait_ge(sem("xh_out0"), 16 * 5)
            pool.wait_ge(sem("xh_out1"), 16 * 4)
            pool.wait_ge(sem("zeros_out"), 16 * (CAP - SURE))
            phase_end(pool, 1)
            nit = pool.value_load(nit_i[0:1, 0:1], min_val=1, max_val=PAIRS)
            with pool.Fori(0, nit) as t:
                for s in range(2):
                    pool.wait_ge(sem("xgT_ps"), t * 2 + s + 1)
                    nc.gpsimd.tensor_copy(idx_cur[:, s:s + 1], ids_sb[:, ds((t * 2 + s) * 16, 1)]).then_inc(sem("idx"), 1)
                    pool.wait_ge(sem("idx"), t * 2 + s + 1)
                    pool.sem_inc(sem("idx_seen"), 1)
                    pool.indirect_dma_start(out=xg[s], out_offset=None, in_=rows_d,
                                            in_offset=bass.IndirectOffsetOnAxis(ap=idx_cur[:, s:s + 1], axis=0)).then_inc(sem(f"xg_in{s}"), 16)
            phase_end(pool, 2)
            for i in range(TILES):
                if i >= 2:
                    pool.wait_ge(sem("yb_free"), i - 1)
                    pool.wait_ge(sem(f"y_out{i % 2}"), 16 * (i // 2))
                for c, buf in enumerate((ya, yb)):
                    pool.indirect_dma_start(out=buf[i % 2][0:ROWS[i], :], out_offset=None, in_=ye_d,
                                            in_offset=bass.IndirectOffsetOnAxis(ap=slot_i[0:ROWS[i], c * TILES + i:c * TILES + i + 1], axis=0)).then_inc(sem(f"yg{c}{i % 2}"), 16)

        @block.scalar
        def _(act):
            ch = Chain(act, sem("act"))
            for i in range(TILES):
                r = ROWS[i]
                act.wait_ge(sem("x1_ready"), i + 1)
                if i:
                    act.wait_ge(sem("ss1"), i)
                nc.scalar.activation(sqj[0:r, :], x1[0:r, i * D:(i + 1) * D], ACT.Square,
                                     accum_out=ss[0:r, i:i + 1]).then_inc(sem("ss1"), 1)
                act.wait_ge(sem("ms1"), i + 1)
                ch.step(nc.scalar.activation(rstd[0:r, i:i + 1], ss[0:r, i:i + 1], ACT.Ln))
                ch.wait()
                nc.scalar.activation(rstd[0:r, i:i + 1], rstd[0:r, i:i + 1], ACT.Exp, scale=-0.5).then_inc(sem("rstd1"), 1)
            act.wait_ge(sem("gshift"), 1)
            nc.scalar.activation(gexp, gexp, ACT.Exp).then_inc(sem("gexp"), 1)
            act.wait_ge(sem("eshift"), 1)
            nc.scalar.activation(gate2, gate2, ACT.Exp).then_inc(sem("eexp"), 1)
            phase_end(act, 1)
            nit = act.value_load(nit_i[0:1, 0:1], min_val=1, max_val=PAIRS)
            with act.Fori(0, nit) as t:
                for s in range(2):
                    act.wait_ge(sem("h_ps"), t * 2 + s + 1)
                    nc.scalar.activation(he[s][:, 0:FF], ps[4 + s][:, 0:FF], ACT.Exp, scale=-1.0).then_inc(sem("h_exp"), 1)
                for s in range(2):
                    act.wait_ge(sem("heT_ps"), t * 2 + s + 1)
                    nc.scalar.activation(heT[s], ps[6][:, s * FF:(s + 1) * FF], ACT.Copy).then_inc(sem("heT"), 1)
                for s in range(2):
                    act.wait_ge(sem("ye_ps"), t * 2 + s + 3)
                    act.wait_ge(sem(f"ye_out{s}"), t * 16 + 16)
                    nc.scalar.activation(ysb[s][:, 0:512], ps[2 * s][:, :], ACT.Copy).then_inc(sem("ye_a"), 1)
                    act.wait_ge(sem("ye_a"), t * 2 + s + 1)
                    act.wait_ge(sem("ye_v"), t * 2 + s + 1)
                    act.dma_start(ye_d[ds((t * 2 + s) * P, P), :], ysb[s]).then_inc(sem(f"ye_out{s}"), 16)
            act.wait_ge(sem("ye_out0"), nit * 16 + 16)
            act.wait_ge(sem("ye_out1"), nit * 16 + 16)
            act.sem_inc(sem("ye_seen"), 1)
            phase_end(act, 2)
            act.dma_start(fw, final_norm_w.rearrange("(a n) -> a n", a=1).broadcast_to([P, D])).then_inc(sem("fw"), 16)
            for i in range(TILES):
                r = ROWS[i]
                act.wait_ge(sem("x2_ready"), i + 1)
                nc.scalar.activation(yb[i % 2][0:r, :], ya[i % 2][0:r, :], ACT.Square,
                                     accum_out=ss[0:r, i:i + 1]).then_inc(sem("ssf"), 1)
                act.wait_ge(sem("msf"), i + 1)
                ch.step(nc.scalar.activation(rstd[0:r, i:i + 1], ss[0:r, i:i + 1], ACT.Ln))
                ch.wait()
                nc.scalar.activation(rstd[0:r, i:i + 1], rstd[0:r, i:i + 1], ACT.Exp, scale=-0.5).then_inc(sem("rstdf"), 1)

        @block.tensor
        def _(pe):

            def project(i):
                r = ROWS[i]
                if i >= 2:
                    pe.wait_ge(sem("x1_ready"), i - 1)
                for n in range(2):
                    for k in range(KC):
                        mm = nc.tensor.matmul(ps[2 * (i % 2) + n][0:r, :], tok(mixT, k, i), wout[:, k * D + n * 512:k * D + (n + 1) * 512],
                                              start=(k == 0), stop=(k == KC - 1))
                    mm.then_inc(sem("x1_ps"), 1)

            def router(i):
                r = ROWS[i]
                pe.wait_ge(sem("xh_ready"), i + 1)
                if i:
                    pe.wait_ge(sem("h2T"), 2 * i)
                for k in range(KC):
                    mm = nc.tensor.transpose(ps[4 + k // 4][:, (k % 4) * P:(k % 4) * P + r], xh[i % 2][0:r, k * P:(k + 1) * P], ident[0:r, 0:r])
                    if k % 4 == 3:
                        mm.then_inc(sem("h2T_ps"), 1)
                pe.wait_ge(sem("h2T"), 2 * i + 2)
                if i:
                    pe.wait_ge(sem("lg"), i)
                for k in range(KC):
                    mm = nc.tensor.matmul(ps[6][0:r, 0:20], h2T[i % 2][:, k * P:k * P + r], wr[:, k * 20:(k + 1) * 20], start=(k == 0), stop=(k == KC - 1))
                mm.then_inc(sem("lg_ps"), 1)

            project(0)
            for i in range(TILES):
                if i + 1 < TILES:
                    project(i + 1)
                router(i)
            pe.wait_ge(sem("counts_in"), 1)
            nc.tensor.matmul(ps[7][:, 0:TILES * 16], cst("tri"), Mx, start=True, stop=False)
            nc.tensor.matmul(ps[7][:, 0:TILES * 16], ones, cum, start=False, stop=True)
            nc.tensor.matmul(ps[6][:, 64:80], ones, rk[:, 0:16], start=True, stop=True).then_inc(sem("rank_ps"), 1)
            phase_end(pe, 1)
            pe.sem_inc(sem("ye_ps"), 2)
            pe.sem_inc(sem("xgT_ps"), 2)
            nit = pe.value_load(nit_i[0:1, 0:1], min_val=1, max_val=PAIRS)

            def hidden(t, s, k0, k1):
                w13 = wslot[s][:, 0:4096].rearrange("p (k f) -> p k f", k=KC)
                for k in range(k0, k1):
                    mm = nc.tensor.matmul(ps[4 + s][:, :], xT[s][:, k * P:(k + 1) * P], w13[:, k, :], start=(k == 0), stop=(k == KC - 1))
                if k1 == KC:
                    mm.then_inc(sem("h_ps"), 1)

            def flip_hidden(t, s):
                pe.wait_ge(sem("he_ready"), t * 2 + s + 1)
                for k in range(2):
                    mm = nc.tensor.transpose(ps[6][:, s * FF + k * P:s * FF + (k + 1) * P], he[s][:, k * P:(k + 1) * P], ident)
                mm.then_inc(sem("heT_ps"), 1)

            def down(t, s):
                pe.wait_ge(sem("heT"), t * 2 + s + 1)
                w2 = wslot[s][:, 4096:6144]
                for n in range(2):
                    for k in range(2):
                        mm = nc.tensor.matmul(ps[2 * s + n][:, :], heT[s][:, k * P:(k + 1) * P], w2[:, k * D + n * 512:k * D + (n + 1) * 512], start=(k == 0), stop=(k == 1))
                mm.then_inc(sem("ye_ps"), 1)

            with pe.Fori(0, nit) as t:
                for s in range(2):
                    pe.wait_ge(sem("xbank_free"), t * 4 + 2 * s + 2)
                    pe.wait_ge(sem(f"xg_in{s}"), t * 16 + 16)
                    for k in range(KC):
                        mm = nc.tensor.transpose(ps[2 * s + k // 4][:, (k % 4) * P:(k % 4 + 1) * P], xg[s][:, k * P:(k + 1) * P], ident)
                    mm.then_inc(sem("xgT_ps"), 1)
                for s in range(2):
                    pe.wait_ge(sem("xT_s"), t * 4 + 2 * s + 2)
                    pe.wait_ge(sem(f"wexp{s}"), t * 48 + 48)
                    if s == 0:
                        hidden(t, 0, 0, KC)
                    else:
                        hidden(t, 1, 0, 6)
                        flip_hidden(t, 0)
                        hidden(t, 1, 6, KC)
                down(t, 0)
                flip_hidden(t, 1)
                down(t, 1)
            phase_end(pe, 2)

        @block.vector
        def _(dve):
            V = nc.vector
            ch = Chain(dve, sem("dve"))

            def step(ins):
                ch.step(ins)
                ch.wait()

            def mean_eps(a, n):
                return V.tensor_scalar(a, a, 1.0 / n, EPS, ALU.mult, ALU.add)


            def residual(i):
                r = ROWS[i]
                dve.wait_ge(sem(f"x1_in{i // 2}"), 16)
                dve.wait_ge(sem("x1_ps"), 2 * i + 2)
                for n in range(2):
                    xx = x1[0:r, i * D + n * 512:i * D + (n + 1) * 512]
                    last = V.tensor_tensor(xx, ps[2 * (i % 2) + n][0:r, :], xx, ALU.add)
                last.then_inc(sem("x1_ready"), 1)

            def norm2(i):
                r = ROWS[i]
                dve.wait_ge(sem("ss1"), i + 1)
                mean_eps(ss[0:r, i:i + 1], D).then_inc(sem("ms1"), 1)
                dve.wait_ge(sem("rstd1"), i + 1)
                if i >= 2:
                    dve.wait_ge(sem(f"xh_out{i % 2}"), 16 * (i // 2))
                V.tensor_scalar(xh[i % 2][0:r, :], x1[0:r, i * D:(i + 1) * D], rstd[0:r, i:i + 1], None, ALU.mult).then_inc(sem("xh_ready"), 1)

            def logits(i):
                r = ROWS[i]
                for g in range(2):
                    dve.wait_ge(sem("h2T_ps"), 2 * i + g + 1)
                    V.tensor_tensor(h2T[i % 2][:, 512 * g:512 * g + 512].rearrange("p (a b) -> p a b", b=P)[:, :, 0:r],
                                    head3(ps[4 + g][:, :], P)[:, :, 0:r],
                                    n2w[:, 4 * g:4 * g + 4].unsqueeze(2).broadcast_to([P, 4, r]), ALU.mult).then_inc(sem("h2T"), 1)
                dve.wait_ge(sem("lg_ps"), i + 1)
                V.tensor_tensor(lgall[0:r, i * 20:(i + 1) * 20], ps[6][0:r, 0:20], rbias[0:r, :], ALU.add).then_inc(sem("lg"), 1)

            residual(0)
            for i in range(TILES):
                norm2(i)
                if i + 1 < TILES:
                    residual(i + 1)
                logits(i)

            dve.wait_ge(sem("lg"), TILES)
            lg3 = head3(lgall, 20)
            step(V.memset(gpad, -3e38))
            step(V.tensor_copy(head3(gpad, 8)[:, :, 0:NG], lg3[:, :, 0:NG]))
            for i in range(TILES):
                step(V.max(g8, gpad[:, i * 8:(i + 1) * 8]))
                step(V.max_index(gi, g8, gpad[:, i * 8:(i + 1) * 8]))
                step(V.tensor_copy(gidx[:, i:i + 1], gi[:, 0:1]))
                step(V.tensor_scalar(gexp[:, i * 4:(i + 1) * 4], lgall[:, i * 20:i * 20 + 4], g8[:, 0:1], None, ALU.subtract))
            dve.sem_inc(sem("gshift"), 1)
            ohg = head3(oh1[:, 0:36], NG)
            step(V.tensor_tensor(ohg, cst("iota")[:, 0:NG].unsqueeze(1).broadcast_to([P, TILES, NG]),
                                 gidx.unsqueeze(2).broadcast_to([P, TILES, NG]), ALU.is_equal))
            off = head3(oh2[:, 0:36], NG)
            step(V.tensor_scalar(off, ohg, -NEG, NEG, ALU.mult, ALU.add))
            for i in range(TILES):
                lmi = lm[:, i * 16:(i + 1) * 16].rearrange("p (g e) -> p g e", e=EG)
                lei = lgall[:, i * 20 + NG:(i + 1) * 20].rearrange("p (g e) -> p g e", e=EG)
                step(V.tensor_tensor(lmi, lei, ohg[:, i, :].unsqueeze(2).broadcast_to([P, NG, EG]), ALU.mult))
                step(V.tensor_tensor(lmi, lmi, off[:, i, :].unsqueeze(2).broadcast_to([P, NG, EG]), ALU.add))
                step(V.max(e8, lm[:, i * 16:(i + 1) * 16]))
                step(V.max_index(ei, e8, lm[:, i * 16:(i + 1) * 16]))
                step(V.tensor_copy(v12[:, 2 * i:2 * i + 2], e8[:, 0:2]))
                step(V.tensor_copy(i12[:, 2 * i:2 * i + 2], ei[:, 0:2]))
            v3, i3 = head3(v12, 2), head3(i12, 2)
            V.tensor_tensor(gate2.unsqueeze(2), v3[:, :, 1:2], v3[:, :, 0:1], ALU.subtract).then_inc(sem("eshift"), 1)
            iot = cst("iota")[:, 0:NE].unsqueeze(1).broadcast_to([P, TILES, NE])
            o1, o2, M3, c3, r3 = (head3(a, NE) for a in (oh1, oh2, Mx, cum, rk))
            step(V.tensor_tensor(o1, iot, i3[:, :, 0:1].broadcast_to([P, TILES, NE]), ALU.is_equal))
            step(V.tensor_tensor(o2, iot, i3[:, :, 1:2].broadcast_to([P, TILES, NE]), ALU.is_equal))
            step(V.tensor_tensor(Mx, oh1, oh2, ALU.add))
            step(V.tensor_scalar(M3[:, 8, :], M3[:, 8, :], cst("valid"), None, ALU.mult))
            step(V.memset(c3[:, 0, :], 0.0))
            for i in range(1, TILES):
                step(V.tensor_tensor(c3[:, i, :], c3[:, i - 1, :], M3[:, i - 1, :], ALU.add))
            step(V.tensor_tensor(rk[:, 0:16], c3[:, 8, :], M3[:, 8, :], ALU.add))
            dve.sem_inc(sem("counts_in"), 1)
            dve.wait_ge(sem("gexp"), 1)
            step(V.tensor_reduce(ptop, head3(gexp, 4), AX, ALU.add))
            step(V.reciprocal(ptop, ptop))
            dve.wait_ge(sem("eexp"), 1)
            step(V.tensor_scalar(gate1, gate2, 1.0, None, ALU.add))
            step(V.reciprocal(gate1, gate1))
            step(V.tensor_tensor(gate1, gate1, ptop, ALU.mult))
            step(V.tensor_tensor(gate2, gate2, gate1, ALU.mult))
            dve.wait_ge(sem("rank_ps"), 1)
            step(V.tensor_scalar(cnt_i, ps[6][:, 64:80], 127.0, None, ALU.add))
            step(V.tensor_scalar(cnt_i, cnt_i, 7, None, ALU.logical_shift_right))
            step(V.tensor_copy(ntl, cnt_i))
            step(V.tensor_tensor_scan(endt, ones[:, 0:NE], ntl, 0.0, ALU.mult, ALU.add))
            step(V.tensor_tensor(base, endt, ntl, ALU.subtract))
            step(V.tensor_scalar(base, base, float(P), None, ALU.mult))
            step(V.tensor_tensor(r3, head3(ps[7][:, 0:TILES * 16], NE), base.unsqueeze(1).broadcast_to([P, TILES, NE]), ALU.add))
            for c, o in ((0, oh1), (1, oh2)):
                step(V.tensor_tensor(o, o, rk, ALU.mult))
                step(V.tensor_reduce(slotf[:, c * TILES:(c + 1) * TILES], head3(o, NE), AX, ALU.add))
            step(V.tensor_copy(slot_i, slotf))
            step(V.tensor_scalar(row_i, slot_i, P - 1, 5, ALU.bitwise_and, ALU.logical_shift_left))
            step(V.tensor_scalar(row_j, slot_i, 7, None, ALU.logical_shift_right))
            step(V.tensor_tensor(row_i, row_i, row_j, ALU.bitwise_or))
            dve.sem_inc(sem("slots_ready"), 1)
            c3_ = cmp.rearrange("p (j e) -> p j e", e=NE)
            step(V.tensor_tensor(c3_, endt.unsqueeze(1).broadcast_to([P, CAP, NE]), cst("iota").unsqueeze(2).broadcast_to([P, CAP, NE]), ALU.is_le))
            step(V.tensor_reduce(eid_f, c3_, AX, ALU.add))
            step(V.tensor_scalar(eid, eid_f, float(NE - 1), None, ALU.min))
            step(V.tensor_scalar(base[:, 0:1].bitcast(I32), endt[:, NE - 1:NE], 1.0, None, ALU.add))
            step(V.tensor_scalar(nit_i, base[:, 0:1].bitcast(I32), 1, None, ALU.logical_shift_right))
            dve.sem_inc(sem("routed"), 1)
            phase_end(dve, 1)

            dve.sem_inc(sem("xbank_free"), 4)
            dve.sem_inc(sem("ye_out0"), 16)
            dve.sem_inc(sem("ye_out1"), 16)
            nit = dve.value_load(nit_i[0:1, 0:1], min_val=1, max_val=PAIRS)
            with dve.Fori(0, nit) as t:
                ch.enter(t, 6)
                for s in range(2):
                    dve.wait_ge(sem("xgT_ps"), t * 2 + s + 3)
                    for g in range(2):
                        V.tensor_tensor(head3(xT[s][:, g * 512:(g + 1) * 512], P), head3(ps[2 * s + g][:, :], P),
                                        n2w[:, 4 * g:4 * g + 4].unsqueeze(2).broadcast_to([P, 4, P]), ALU.mult).then_inc(sem("xT_s"), 1)
                for s in range(2):
                    dve.wait_ge(sem("h_exp"), t * 2 + s + 1)
                    hx, hy = he[s][:, 0:FF], he[s][:, FF:2 * FF]
                    step(V.tensor_scalar(hx, hx, 1.0, None, ALU.add))
                    step(V.reciprocal(hx, hx))
                    step(V.tensor_tensor(hx, hx, ps[4 + s][:, 0:FF], ALU.mult))
                    V.tensor_tensor(hx, hx, ps[4 + s][:, FF:2 * FF], ALU.mult).then_inc(sem("he_ready"), 1)
                for s in range(2):
                    dve.wait_ge(sem("ye_ps"), t * 2 + s + 3)
                    dve.wait_ge(sem(f"ye_out{s}"), t * 16 + 16)
                    V.tensor_copy(ysb[s][:, 512:1024], ps[2 * s + 1][:, :]).then_inc(sem("ye_v"), 1)
                    dve.wait_ge(sem("ye_a"), t * 2 + s + 1)
                    dve.wait_ge(sem("ye_v"), t * 2 + s + 1)
                    dve.sem_inc(sem("xbank_free"), 2)
                assert ch.n == ch.per
            phase_end(dve, 2)

            dve.wait_ge(sem("fw"), 16)
            ch2 = Chain(dve, sem("dve_last"))
            for i in range(TILES):
                r = ROWS[i]
                xi = x1[0:r, i * D:(i + 1) * D]
                for c in range(2):
                    dve.wait_ge(sem(f"yg{c}{i % 2}"), 16 * (i // 2 + 1))
                a_, b_ = ya[i % 2][0:r, :], yb[i % 2][0:r, :]
                ch2.step(V.scalar_tensor_tensor(out=a_, in0=a_, scalar=gate1[0:r, i:i + 1], in1=xi, op0=ALU.mult, op1=ALU.add))
                ch2.wait()
                V.scalar_tensor_tensor(out=a_, in0=b_, scalar=gate2[0:r, i:i + 1], in1=a_, op0=ALU.mult, op1=ALU.add).then_inc(sem("x2_ready"), 1)
                dve.wait_ge(sem("ssf"), i + 1)
                dve.sem_inc(sem("yb_free"), 1)
                mean_eps(ss[0:r, i:i + 1], D).then_inc(sem("msf"), 1)
                dve.wait_ge(sem("rstdf"), i + 1)
                V.scalar_tensor_tensor(out=a_, in0=a_, scalar=rstd[0:r, i:i + 1], in1=fw[0:r, :], op0=ALU.mult, op1=ALU.mult).then_inc(sem("y_ready"), 1)



_INS = ['x_prompt', 'x_sample', 'cache_k', 'cache_v', 'state_hgrn', 'page_table', 'norm1_w', 'w_in', 'rel_bias',
        'lambda_q1', 'lambda_k1', 'lambda_q2', 'lambda_k2', 'da_subln_w', 'hg_lb_logits', 'hg_norm_w', 'w_out',
        'norm2_w', 'router_g_w', 'router_g_b', 'router_e_w', 'router_e_b', 'expert_w1', 'expert_w3', 'expert_w2',
        'final_norm_w']
_OUTS = [((1, SEQ, D), 'float32'), ((NB, NT, D), 'float32'), ((1, 1, SEQ, H, P), 'float32'), ((1, 1, SEQ, H, P), 'float32'),
         ((1, 1, H, P, P), 'float32'), ((1, NB, NT, H, P), 'float32'), ((1, NB, NT, H, P), 'float32'), ((1, NB, H, P, P), 'float32')]


def kernel(**inputs):
    import numpy as _np
    import concourse.bacc as _bacc
    from concourse import mybir as _mybir
    from concourse.bass_utils import run_bass_kernel_spmd as _run

    nc = _bacc.Bacc("TRN2", target_bir_lowering=False, num_devices=1)
    arrays, args = {}, []
    for name in _INS:
        a = _np.ascontiguousarray(inputs[name])
        arrays[f"in_{name}_dram"] = a
        args.append(nc.dram_tensor(f"in_{name}_dram", a.shape, _mybir.dt.from_np(a.dtype), kind="ExternalInput").ap())
    arrays["in_table_dram"] = TABLE
    args.append(nc.dram_tensor("in_table_dram", TABLE.shape, F32, kind="ExternalInput").ap())
    for i, (shape, dtype) in enumerate(_OUTS):
        dt = _mybir.dt.from_np(_np.dtype(dtype))
        args.append(nc.dram_tensor(f"out_{i}_dram", shape, dt, kind="ExternalOutput").ap())
    build(nc, *args)
    r = _run(nc, [arrays], core_ids=[0])
    return tuple(r.results[0][f"out_{i}_dram"] for i in range(len(_OUTS)))
```

```python
import math
from contextlib import ExitStack

import numpy as np
import concourse.bass as bass
from concourse import mybir

F32 = mybir.dt.float32
I32 = mybir.dt.int32
U32 = mybir.dt.uint32
ALU = mybir.AluOpType
ACT = mybir.ActivationFunctionType
AX = mybir.AxisListType.X
ds = bass.ds

P = 128
D = 1024
KC = D // P
SEQ = 1024
NB, NT = 8, 4
SMP = NB * NT
TOK = SEQ + SMP
TILES = SEQ // P + 1
ROWS = [P] * (SEQ // P) + [SMP]
H = 4
QK = 64
HW = H * P
PAGES = 32
COLS = H * 2 * NT
NE, NG, EG, FF = 16, 4, 4, 256
CAP = 32
PAIRS = CAP // 2
SURE = -(-(2 * TOK // P + 1) // 2) * 2
LEVELS = [64, 32, 16, 8, 4, 2, 1]
NLEV = len(LEVELS)
BUCKETS = 32
EPS = 1e-6
NEG = -1e30
LAM_INIT = 0.8 - 0.6 * math.exp(-0.3 * 0)

CP = {}


def constants():
    parts = []

    def put(name, a):
        full = np.zeros((P, a.shape[1]), np.float32)
        full[:a.shape[0]] = a
        CP[name] = (sum(x.shape[1] for x in parts), a.shape[1])
        parts.append(full)

    def bucket(n):
        n = np.maximum(n, 0)
        nf = np.maximum(n, 16).astype(np.float32)
        large = 16 + (np.log(nf / np.float32(16)) / np.float32(math.log(8.0)) * 16).astype(np.int32)
        return np.where(n < 16, n, np.minimum(large, 31))

    def onehot(dist):
        a = np.zeros((BUCKETS + 1, dist.size), np.float32)
        dist = dist.reshape(-1)
        ok = dist >= 0
        a[bucket(dist)[ok], np.nonzero(ok)[0]] = 1.0
        a[BUCKETS, ~ok] = NEG
        return a

    t = np.arange(P)
    put("ident", np.eye(P))
    put("tri", (t[:, None] < t[None, :]) * 1.0)
    lv = []
    for w in LEVELS:
        same = t[:, None] // (2 * w) == t[None, :] // (2 * w)
        lv.append(same & (t[:, None] % (2 * w) < w) & (t[None, :] % (2 * w) >= w))
    lv.append(t[:, None] == t[None, :])
    put("level", np.concatenate(lv, 1) * 1.0)
    put("own", (np.arange(SMP)[:, None] // NT == np.arange(NB)[None, :]) * 1.0)
    put("valid", (t[:, None] < SMP) * 1.0)
    put("iota", np.broadcast_to(np.arange(CAP)[None, :], (P, CAP)) * 1.0)
    row = np.arange(P)
    c32 = np.arange(COLS)
    put("rowsum", ((row[:, None] // 32 == c32[None, :] // 8) & (row[:, None] % 8 == c32[None, :] % 8)) * 1.0)
    c16 = np.arange(H * NT)
    same = (c32[:, None] // 8 == c16[None, :] // NT) & (c32[:, None] % NT == c16[None, :] % NT)
    put("map1", (same & (c32[:, None] // NT % 2 == 0)) * 1.0)
    put("map2", (same & (c32[:, None] // NT % 2 == 1)) * 1.0)
    put("head", (c32[:, None] // 8 == np.arange(H)[None, :]) * 1.0)
    small = sum(x.shape[1] for x in parts)
    put("oh_band", onehot(255 - np.arange(384)))
    return np.concatenate(parts, 1).astype(np.float32), small


TABLE, SMALL = constants()


class Chain:

    def __init__(self, eng, sem):
        self.eng, self.sem, self.n, self.base = eng, sem, 0, 0

    def step(self, ins):
        ins.then_inc(self.sem, 1)
        self.n += 1

    def wait(self):
        self.eng.wait_ge(self.sem, self.base + self.n)

    def enter(self, turn, per_turn):
        self.n0, self.per = self.n, per_turn
        self.base, self.n = turn * per_turn + self.n0, 0

    def leave(self, turns):
        assert self.n == self.per, (self.n, self.per)
        self.base, self.n = 0, self.n0 + turns * self.per


def build(nc, x_prompt, x_sample, cache_k, cache_v, state_hgrn, page_table,
          norm1_w, w_in, rel_bias, lambda_q1, lambda_k1, lambda_q2, lambda_k2,
          da_subln_w, hg_lb_logits, hg_norm_w, w_out, norm2_w,
          router_g_w, router_g_b, router_e_w, router_e_b,
          expert_w1, expert_w3, expert_w2, final_norm_w, table,
          y_prompt, y_sample, k_prompt, v_prompt, s_prompt, k_sample, v_sample, s_sample):

    band_d = nc.dram_tensor("band_scratch", (H * P, 384), F32, kind="Internal").ap()
    rows_d = nc.dram_tensor("rows_scratch", (TOK, D), F32, kind="Internal").ap()
    ids_d = nc.dram_tensor("ids_scratch", (P * CAP, 16), I32, kind="Internal").ap()
    ye_d = nc.dram_tensor("expert_scratch", (CAP * P, D), F32, kind="Internal").ap()

    POOL = cache_k.shape[1]
    xp_v = x_prompt.rearrange("b (i p) d -> p (b i) d", p=P)
    xs_v = x_sample.rearrange("b t d -> (b t) d")
    win_v = w_in.rearrange("l (k p) n -> p (l k) n", p=P)
    wout_v = w_out.rearrange("l (k p) n -> p (l k) n", p=P)
    ck_v = cache_k.rearrange("l n p h d -> (l n p) (h d)")
    cv_v = cache_v.rearrange("l n p h d -> (l n p) (h d)")
    st_v = state_hgrn.rearrange("l b h k v -> (l h) k b v")
    so_v = s_sample.rearrange("l b h k v -> (l h) k b v")
    kp_v = k_prompt.rearrange("l b (i p) h d -> p (l b i) (h d)", p=P)
    vp_v = v_prompt.rearrange("l b (i p) h d -> p (l b i) (h d)", p=P)
    ks_v = k_sample.rearrange("l b t h d -> (l b t) (h d)")
    vs_v = v_sample.rearrange("l b t h d -> (l b t) (h d)")
    yp_v = y_prompt.rearrange("b (i p) d -> p (b i) d", p=P)
    ys_v = y_sample.rearrange("b t d -> (b t) d")
    w1_v = expert_w1.rearrange("l e d f -> (l e d) f")
    w3_v = expert_w3.rearrange("l e d f -> (l e d) f")
    w2_v = expert_w2.rearrange("l e f d -> (l e f) d")

    with ExitStack() as ctx:
        def sb(name, cols, dt=F32, rows=P):
            return ctx.enter_context(nc.sbuf_tensor(name, [rows, cols], dt))

        sems = {}
        part = [""]

        def sem(name):
            if name not in sems:
                sems[name] = nc.alloc_semaphore(name=name + part[0])
            return sems[name]

        arena = sb("arena", 8448 + 13056 + 21888 + 6144)
        at = [0]

        def take(cols, start=None):
            if start is None:
                start = at[0]
                at[0] += cols
            return arena[:, start:start + cols]

        A0 = 0
        hT = take(KC * TOK)
        B0 = at[0]
        qT, kT = take(H * TOK), take(H * TOK)
        v_nat = take(TILES * HW)
        C0 = at[0]
        hqT, gT, kkT = take(H * TOK), take(H * TOK), take(H * TOK)
        hi, gate = take(TILES * HW), take(TILES * HW)
        W0 = at[0]
        wring = [take(2048) for _ in range(3)]
        mixT = take(KC * TOK, A0)
        reset = take(TOK, A0)
        x_all = take(TILES * D, C0)
        knat = [take(HW, W0), take(HW, W0 + HW)]
        X = [take(TOK, W0), take(TOK, W0 + TOK)]
        tmp = take(TOK, W0)
        AT = take(1024, W0 + 2112)
        KdN = take(1024, W0 + 3136)
        S = take(9 * P, W0 + 4160)
        ATs = take(SMP, W0 + 5312)
        Qpad = take(NB * SMP, W0 + 5344)
        KdM = take(NB * P, W0 + 3136)
        S0 = take(NB * P, W0 + 2112)
        band = take(H * 1152, C0)
        zp = [take(2048, C0 + 4608), take(2048, C0 + 6656)]
        pT = [take(1024, C0 + 8704), take(1024, C0 + 9728)]
        o_sb = [take(P, C0 + 10752), take(P, C0 + 10880)]
        oh = take(384, W0)
        rowb = take(384, W0 + 1200)
        R0 = C0 + 11264
        RING = 16
        ring = take(RING * HW, R0)
        kt = [take(8 * HW, C0), take(8 * HW, C0 + 8 * HW)]
        z = take(PAGES * 32 + SMP, W0)
        PT = take(9 * P, W0 + 1056)
        qcur = [take(HW, W0 + 2208), take(HW, W0 + 2720)]
        o_all = take(NB * P, W0 + 3232)
        kn = take(HW, W0 + 4256)
        o_sel = take(P, W0 + 4768)
        o16 = take(NB * P, W0 + 4896)
        osq = take(NB * P, W0)
        qd = take(NB * HW, B0 + 2 * H * TOK)
        vnew = v_nat[0:SMP, 8 * HW:9 * HW]
        wout = take(KC * D, B0)
        x1 = take(TILES * D, C0)
        xh = [take(D, W0), take(D, W0 + D)]
        h2T = [take(D, W0 + 2 * D), take(D, W0 + 3 * D)]
        sqj = take(D, W0 + 4 * D)
        wslot = [take(6144, A0), take(6144, R0)]
        xg = [take(D, B0), take(D, B0 + D)]
        xT = [take(D, B0 + 2 * D), take(D, B0 + 3 * D)]
        he = [take(2 * FF, B0 + 4 * D), take(2 * FF, B0 + 4 * D + 512)]
        heT = [take(FF, B0 + 5 * D), take(FF, B0 + 5 * D + 256)]
        ysb = [take(D, B0 + 6 * D), take(D, B0 + 7 * D)]
        zero_rows = take(D, R0)
        ya = [take(D, B0), take(D, B0 + D)]
        yb = [take(D, B0 + 2 * D), take(D, B0 + 3 * D)]
        fw = take(D, B0 + 4 * D)

        tab = sb("tab", SMALL)

        def cst(name, rows=P):
            a, n = CP[name]
            return tab[0:rows, a:a + n]

        ident = cst("ident")
        ones = sb("ones", P)[:, :]
        small = sb("small", 768)
        sat = [0]

        def sm(n, dt=F32):
            a = small[:, sat[0]:sat[0] + n]
            sat[0] += n
            return a if dt == F32 else a.bitcast(dt)

        n1w, n2w, lbT, omlb = sm(KC), sm(KC), sm(H), sm(H)
        lg0, lg1 = sm(H), sm(H)
        daw, hgw = sm(1), sm(1)
        ss, rstd = sm(TILES), sm(TILES)
        ss2, rstd2 = sm(TILES * H), sm(TILES * H)
        lamv, lamp, nlam = sm(4), sm(2), sm(1)
        rb = sm(H)
        farc, blast, bias4, biasn = sm(1), sm(SMP), sm(NT), sm(NB * SMP)
        att = sm(16)
        mxc, nmx, mcol = sm(1), sm(1), sm(1)
        mall, m32 = sm(P), sm(COLS)
        sumc, sum_all, rsum = sm(1), sm(NB), sm(NB)
        comb = sm(H * NT)
        oms = sm(NB)
        ptab = sb("ptab", NB * PAGES, I32, 1)
        rbias = sm(20)
        wr = sb("wr", KC * 20)
        route = sb("route", 624)
        rat = [0]

        def rt(n, dt=F32):
            a = route[:, rat[0]:rat[0] + n]
            rat[0] += n
            return a if dt == F32 else a.bitcast(dt)

        lgall, gpad = rt(TILES * 20), rt(TILES * 8)
        g8, gi, e8, ei = rt(8), rt(8, U32), rt(8), rt(8, U32)
        gidx, v12, i12 = rt(TILES), rt(TILES * 2), rt(TILES * 2)
        gate1, gate2, ptop = rt(TILES), rt(TILES), rt(TILES)
        gexp = rt(TILES * 4)
        slotf, slot_i, row_i, row_j = rt(2 * TILES), rt(2 * TILES, I32), rt(2 * TILES, I32), rt(2 * TILES, I32)
        cnt_i, ntl, endt, base = rt(NE, I32), rt(NE), rt(NE), rt(NE)
        eid_f, eid = rt(CAP), rt(CAP, I32)
        nit_i = rt(1, I32)
        idx_cur = rt(2, I32)
        ids_sb = take(CAP * 16, R0 + 6144).bitcast(I32)
        payload = take(TILES * 16, R0 + 6656).bitcast(I32)
        lm = take(TILES * 16, R0 + 6800)
        oh1, oh2, Mx, cum, rk = (take(TILES * 16, W0 + 4 * D + 144 * i) for i in range(5))
        cmp = take(CAP * 16, W0 + 4 * D + 720)

        ps = [ctx.enter_context(nc.psum_tensor(f"bank{i}", [P, 512], F32)) for i in range(8)]

        Q0, K0, V0, HQ0, HF0, HI0, GA0 = (i * HW for i in range(7))
        slots = []
        for kind, dst, c0 in (("T", hqT, HQ0), ("T", gT, HF0), ("N", hi, HI0), ("N", gate, GA0),
                              ("T", qT, Q0), ("T", kT, K0), ("N", v_nat, V0)):
            for half in range(2):
                slots.append((kind, dst, c0 + half * 256, half))
        items = []
        for s, (kind, dst, c0, half) in enumerate(slots):
            if kind == "T":
                items += [(s, kind, dst, half, c, n) for c in range(2) for n in range(3)]
            else:
                items += [(s, kind, dst, half, i, 0) for i in range(TILES)]
        N3 = TOK // 3
        upto = {"T": [0], "N": [0]}
        for it in items:
            for k in upto:
                upto[k].append(upto[k][-1] + (it[1] == k))

        def tok(t, c, i):
            return t[:, c * TOK + i * P:c * TOK + i * P + ROWS[i]]

        def head3(a, n, **kw):
            return a.rearrange("p (a b) -> p a b", b=n)

        NPH = [0]

        def phase_end(eng, k):
            eng.drain().then_inc(sem("phase"), 1)
            eng.wait_ge(sem("phase"), 5 * k)

        cumT, n = {}, 0
        for h in range(H):
            for i in range(8):
                for j in range(0, i + 1, 4):
                    n += 1
                    cumT[(h, i, j)] = n

        NV_TOTAL = 16 * 11
        block_a = nc.Block()
        block = block_a.__enter__()

        @block.sync
        def _(sp):
            for g in range(4):
                sp.dma_start(head3(x_all, D)[:, 2 * g:2 * g + 2, :],
                             xp_v[:, 2 * g:2 * g + 2, :]).then_inc(sem(f"x_in{g}"), 16)
            sp.dma_start(x_all[0:SMP, 8 * D:9 * D], xs_v).then_inc(sem("x_in4"), 16)
            for s, (kind, dst, c0, half) in enumerate(slots):
                if s >= 3:
                    sp.wait_ge(sem("proj"), sum(it[0] <= s - 3 for it in items))
                sp.dma_start(head3(wring[s % 3], 256), win_v[:, :, c0:c0 + 256]).then_inc(sem(f"w_in{s % 3}"), 16)
            for i in range(TILES):
                sp.wait_ge(sem("knat_ready"), i + 1)
                dst = ks_v if i == TILES - 1 else kp_v[:, i, :]
                sp.dma_start(dst, knat[i % 2][0:ROWS[i], :]).then_inc(sem(f"knat_out{i % 2}"), 16)
            sp.dma_start(vp_v, head3(v_nat, HW)[:, 0:8, :]).then_inc(sem("out"), 16)
            sp.dma_start(vs_v, v_nat[0:SMP, 8 * HW:9 * HW]).then_inc(sem("out"), 16)
            sp.wait_ge(sem("knat_out0"), 16 * 5)
            sp.wait_ge(sem("knat_out1"), 16 * 4)
            phase_end(sp, 1)
            for h in range(H):
                sp.wait_ge(sem("s0_free"), h + 1)
                sp.dma_start(head3(S0, P), st_v[h]).then_inc(sem("s0_in"), 16)
                sp.wait_ge(sem("state_ready"), h + 1)
                sp.dma_start(s_prompt[0, 0, h], S[:, 8 * P:9 * P]).then_inc(sem("state_out"), 16)
                sp.wait_ge(sem("snew_ready"), h + 1)
                sp.dma_start(so_v[h], head3(S0, P)).then_inc(sem("snew_out"), 16)
            phase_end(sp, 2)
            sp.dma_start(oh, table[:, SMALL:]).then_inc(sem("oh_in"), 16)
            for h in range(H):
                sp.wait_ge(sem("rowb"), h + 1)
                sp.dma_start(band_d[h * P:(h + 1) * P, :], rowb).then_inc(sem("band_out"), 16)
                sp.wait_ge(sem("band_out"), 16 * (h + 1))
                skew = bass.AP(tensor=band_d.tensor, offset=h * P * 384 + 127, ap=[[383, P], [1, 256]])
                sp.dma_start(band[:, h * 1152 + 896:(h + 1) * 1152], skew).then_inc(sem("band_in"), 16)
            for h in range(H):
                base_h = h * P * 384
                rows_h = slice(32 * h, 32 * h + 32)
                for q4 in range(4):
                    for m in range(2):
                        r4 = slice(32 * h + 8 * q4 + 4 * m, 32 * h + 8 * q4 + 4 * m + 4)
                        sp.dma_start(blast[r4, :], bass.AP(tensor=band_d.tensor, offset=base_h + 127 + 32 * q4, ap=[[383, NT], [1, SMP]])).then_inc(sem("dbias"), 16)
                        sp.dma_start(bias4[r4, :], bass.AP(tensor=band_d.tensor, offset=base_h + 255 + 40 * q4, ap=[[383, NT], [1, NT]])).then_inc(sem("dbias"), 16)
                with nc.allow_non_contiguous_dma("one value a partition"):
                    sp.dma_start(farc[rows_h, :], bass.AP(tensor=band_d.tensor, offset=base_h, ap=[[384, 32], [1, 1]])).then_inc(sem("dbias"), 16)
            sp.wait_ge(sem("ptab_in"), 16)

            def stream(b, view, free, put):
                for j in range(0, PAGES, 8):
                    _, numbers = nc.values_load_multi_w_load_instructions(
                        ptab[0:1, ds(b * PAGES + j, 8)], engines=[mybir.EngineType.SP], min_val=0, max_val=POOL - 1,
                        skip_runtime_bounds_check_because="the page table names pages of the pool")
                    for i, e in enumerate(numbers):
                        free(j + i)
                        put(j + i, view[ds(e * P, P), :])

            def keys(b, first=False):
                def free(j):
                    if j >= RING:
                        sp.wait_ge(sem("k_used"), b * PAGES + j - RING + 1)
                    elif not first and j % 4 == 0:
                        sp.wait_ge(sem("k_used"), b * PAGES)
                        sp.sem_inc(sem("sp_held"), 1)
                        sp.wait_ge(sem("v_used"), b * PAGES + RING + j + 4)

                def put(j, src):
                    sp.dma_start(ring[:, (j % RING) * HW:(j % RING + 1) * HW], src).then_inc(sem(f"page{j % RING}"), 16)

                stream(b, ck_v, free, put)

            def values(b, last_one=False):
                def free(j):
                    if j % 4:
                        return
                    if j >= RING:
                        sp.wait_ge(sem("v_used"), 64 + b * PAGES + j - RING + 4)
                    elif last_one:
                        sp.wait_ge(sem("v_used"), 64 + b * PAGES - RING + j + 4)
                    else:
                        sp.wait_ge(sem("k_used"), b * PAGES + PAGES + RING + j + 4)

                def put(j, src):
                    g, q4 = j // 4 % 4, j % 4
                    dst = ring[32 * q4:32 * q4 + 32, g * 4 * HW:(g + 1) * 4 * HW].rearrange("p (i d) -> p i d", i=4)
                    sp.dma_start(dst, src.rearrange("(i b) d -> b i d", b=32)).then_inc(sem(f"page{j % RING}"), 16)

                stream(b, cv_v, free, put)

            keys(0, True)
            with sp.Fori(0, NB - 1) as t:
                keys(t + 1)
                values(t)
            values(NB - 1, True)
            sp.wait_ge(sem("prompt_done"), 1)
            sp.dma_start(head3(wout, D), wout_v).then_inc(sem("wout_in"), 16)
            sp.wait_ge(sem("wout_in"), 16)
            sp.wait_ge(sem("out"), 32)
            sp.wait_ge(sem("state_out"), 16 * H)
            sp.wait_ge(sem("snew_out"), 16 * H)
        @block.gpsimd
        def _(pool):
            nc.gpsimd.memset(ones[:, :], 1.0).then_inc(sem("ones"), 1)
            nc.gpsimd.memset(small[:, :], 1.0).then_inc(sem("small0"), 1)
            nc.gpsimd.memset(route[:, :], 0.0).then_inc(sem("route0"), 1)
            phase_end(pool, 1)
            nc.gpsimd.memset(reset, 1.0).then_inc(sem("pool"), 1)
            pool.wait_ge(sem("pool"), 1)
            nc.gpsimd.memset(head3(reset[:, 0:SEQ], P)[:, :, 0:1], 0.0).then_inc(sem("pool"), 1)
            nc.gpsimd.memset(head3(reset[:, SEQ:TOK], NT)[:, :, 0:1], 0.0).then_inc(sem("pool"), 1)
            phase_end(pool, 2)
        @block.scalar
        def _(act):
            ch = Chain(act, sem("act"))
            act.dma_start(tab[:, :], table[:, 0:SMALL]).then_inc(sem("tab"), 16)
            act.wait_ge(sem("small0"), 1)
            loads = [(n1w, norm1_w.rearrange("l (k p) -> p (l k)", p=P)),
                     (n2w, norm2_w.rearrange("l (k p) -> p (l k)", p=P)),
                     (lg0, hg_lb_logits[0:1].rearrange("a (h p) -> p (a h)", p=P)),
                     (lg1, hg_lb_logits[1:2].rearrange("a (h p) -> p (a h)", p=P)),
                     (daw, da_subln_w.rearrange("l p -> p l")),
                     (hgw, hg_norm_w.rearrange("l p -> p l")),
                     (lamv[0:QK, 0:1], lambda_q1.rearrange("l p -> p l")),
                     (lamv[0:QK, 1:2], lambda_q2.rearrange("l p -> p l")),
                     (lamv[0:QK, 2:3], lambda_k1.rearrange("l p -> p l")),
                     (lamv[0:QK, 3:4], lambda_k2.rearrange("l p -> p l")),
                     (rb[0:BUCKETS, :], rel_bias)]
            for dst, src in loads:
                with nc.allow_non_contiguous_dma("one column a partition"):
                    act.dma_start(dst, src).then_inc(sem("vecs"), 16)
            assert 16 * len(loads) == NV_TOTAL
            act.dma_start(ptab[:, :], page_table.rearrange("(a b) n -> a (b n)", a=1)).then_inc(sem("ptab_in"), 16)
            act.dma_start(rbias[:, 0:NG], router_g_b.broadcast_to([P, NG])).then_inc(sem("rw"), 16)
            act.dma_start(rbias[:, NG:20], router_e_b.broadcast_to([P, NE])).then_inc(sem("rw"), 16)
            wr3 = wr[:, :].rearrange("p (k n) -> p k n", n=20)
            act.dma_start(wr3[:, :, 0:NG], router_g_w.rearrange("l (k p) n -> p (l k) n", p=P)).then_inc(sem("rw"), 16)
            act.dma_start(wr3[:, :, NG:20], router_e_w.rearrange("l (k p) n -> p (l k) n", p=P)).then_inc(sem("rw"), 16)
            for i in range(TILES):
                act.wait_ge(sem(f"x_in{i // 2}"), 16)
                r = ROWS[i]
                nc.scalar.activation(take(D, A0 + i * D)[0:r, :], x_all[0:r, i * D:(i + 1) * D], ACT.Square,
                                     accum_out=ss[0:r, i:i + 1]).then_inc(sem("ss"), 1)
            act.wait_ge(sem("ms"), 1)
            ch.step(nc.scalar.activation(rstd, ss, ACT.Ln))
            ch.wait()
            nc.scalar.activation(rstd, rstd, ACT.Exp, scale=-0.5).then_inc(sem("rstd"), 1)
            for g, (s, kind, dst, half, c, n) in enumerate(items):
                if kind != "T":
                    continue
                act.wait_ge(sem("proj"), g + 1)
                col = (half * 2 + c) * TOK + n * N3
                nc.scalar.activation(dst[:, col:col + N3], ps[g % 8][:, 0:N3], ACT.Copy,
                                     scale=QK ** -0.5 if dst is qT else 1.0).then_inc(sem("ev_T"), 1)
            phase_end(act, 1)
            act.wait_ge(sem("lbd"), 1)
            nc.scalar.activation(lbT, lg1, ACT.Exp).then_inc(sem("lbe"), 1)
            for h in range(H):
                sl = slice(h * TOK, (h + 1) * TOK)
                nc.scalar.activation(gT[:, sl], gT[:, sl], ACT.Exp, scale=-1.0).then_inc(sem("ef"), 1)
                if h:
                    act.wait_ge(sem("q_ready"), h)
                nc.scalar.activation(tmp, hqT[:, sl], ACT.Exp, scale=-1.0).then_inc(sem("eq"), 1)
                act.wait_ge(sem("f_ready"), h + 1)
                nc.scalar.activation(gT[:, sl], gT[:, sl], ACT.Ln).then_inc(sem("lnf"), 1)
            k = 0
            for h in range(H):
                for l in range(NLEV):
                    k += 1
                    act.wait_ge(sem("diff"), k)
                    n = TOK if LEVELS[l] < NT else SEQ
                    x = X[l % 2]
                    nc.scalar.activation(x[:, 0:n], x[:, 0:n], ACT.Exp).then_inc(sem("expd"), 1)
                act.wait_ge(sem("tails"), h + 1)
                sl = slice(h * TOK, (h + 1) * TOK)
                nc.scalar.activation(X[0], gT[:, sl], ACT.Exp).then_inc(sem("etail"), 1)
                nc.scalar.activation(X[1], X[1], ACT.Exp).then_inc(sem("etail"), 1)
                for c in range(8):
                    if c % 4 == 0:
                        act.wait_ge(sem("kdn_ps"), 2 * h + c // 4 + 1)
                        nc.scalar.activation(KdN[:, (c // 4) * 512:(c // 4 + 1) * 512], ps[2 + c // 4][:, :], ACT.Copy).then_inc(sem("kdn"), 1)
                for c in range(8):
                    act.wait_ge(sem("o_ps"), 8 * h + c + 1)
                    nc.scalar.activation(hi[:, c * HW + h * P:c * HW + (h + 1) * P], ps[4 + c % 2][:, 0:P], ACT.Copy).then_inc(sem("o_ev"), 1)
                act.wait_ge(sem("os_ps"), h + 1)
                nc.scalar.activation(hi[0:SMP, 8 * HW + h * P:8 * HW + (h + 1) * P], ps[0][0:SMP, 0:P], ACT.Copy).then_inc(sem("o_ev"), 1)
            act.wait_ge(sem("o_ev"), 9 * H)
            nc.scalar.activation(kkT[:, 0:4096], hi[:, 0:4096], ACT.Square).then_inc(sem("sq"), 1)
            nc.scalar.activation(gT[0:SMP, 0:512], hi[0:SMP, 4096:4608], ACT.Square).then_inc(sem("sq"), 1)
            nc.scalar.activation(hqT[:, 0:4096], gate[:, 0:4096], ACT.Exp, scale=-1.0).then_inc(sem("sq"), 1)
            nc.scalar.activation(gT[0:SMP, 512:1024], gate[0:SMP, 4096:4608], ACT.Exp, scale=-1.0).then_inc(sem("sq"), 1)
            act.wait_ge(sem("ms2"), 1)
            ch.step(nc.scalar.activation(rstd2, ss2, ACT.Ln))
            ch.wait()
            nc.scalar.activation(rstd2, rstd2, ACT.Exp, scale=-0.5).then_inc(sem("rstd2"), 1)
            phase_end(act, 2)
            act.wait_ge(sem("lam_ps"), 1)
            nc.scalar.activation(lamp, ps[7][:, 0:2], ACT.Exp).then_inc(sem("lam_e"), 1)
            n = 0
            for h in range(H):
                for i in range(8):
                    zb = zp[n % 2]
                    for m in range(2):
                        act.wait_ge(sem("z_ready"), 2 * n + m + 1)
                        sl = slice(m * 1024, m * 1024 + (i + 1) * P)
                        a = att[:, 8 * (n % 2):8 * (n % 2) + 8]
                        nc.scalar.activation(zb[:, sl], zb[:, sl], ACT.Exp, bias=a[:, m:m + 1],
                                             accum_out=a[:, 2 + m:3 + m]).then_inc(sem("p_ready"), 1)
                    for j in range(0, i + 1, 4):
                        act.wait_ge(sem("pT_ps"), cumT[(h, i, j)])
                        w = min(4, i + 1 - j) * P
                        nc.scalar.activation(pT[n % 2][:, j * P:j * P + w], ps[4 + (j // 4)][:, 0:w], ACT.Copy).then_inc(sem("pT"), 1)
                    act.wait_ge(sem("oa_ps"), n + 1)
                    ch.step(nc.scalar.activation(o_sb[n % 2], ps[6][:, 0:P], ACT.Square, accum_out=a[:, 6:7]))
                    ch.wait()
                    act.sem_inc(sem("oss"), 1)
                    act.wait_ge(sem("oms"), n + 1)
                    ch.step(nc.scalar.activation(a[:, 7:8], a[:, 6:7], ACT.Ln))
                    ch.wait()
                    nc.scalar.activation(a[:, 7:8], a[:, 7:8], ACT.Exp, scale=-0.5).then_inc(sem("orstd"), 1)
                    n += 1
            act.drain().then_inc(sem("prompt_left"), 1)

            def soft(b):
                act.wait_ge(sem("s_done"), b + 1)
                act.wait_ge(sem("z_free"), b + 1)
                nc.scalar.activation(z[:, 0:512], ps[0][:, :], ACT.Copy).then_inc(sem("z_act"), 1)
                act.wait_ge(sem("nmx"), b + 1)
                nc.scalar.activation(z, z, ACT.Exp, bias=nmx, accum_out=sumc).then_inc(sem("z_exp"), 1)

            def move_probs(b):
                for g in range(3):
                    act.wait_ge(sem("PT_ps"), b * 3 + g + 1)
                    n = 512 if g < 2 else P
                    r = P if g < 2 else SMP
                    o = PT[0:r, :].rearrange("p (i k c) -> p i k c", i=4, c=8)[:, :, g * 16:g * 16 + n // 32, :]
                    nc.scalar.activation(o, ps[3 + g % 2][0:r, 0:n].rearrange("p (k i c) -> p i k c", i=4, c=8), ACT.Copy).then_inc(sem("PT"), 1)

            act.wait_ge(sem("prompt_gone"), 1)
            soft(0)
            with act.Fori(0, NB - 1) as t:
                move_probs(t)
                soft(t + 1)
            move_probs(NB - 1)
            act.wait_ge(sem("dss"), 1)
            nc.scalar.activation(osq[0:16, :], o16[0:16, :], ACT.Square).then_inc(sem("dsq"), 1)
            act.wait_ge(sem("dms"), 1)
            ch.step(nc.scalar.activation(oms[0:16, :], oms[0:16, :], ACT.Ln))
            ch.wait()
            nc.scalar.activation(oms[0:16, :], oms[0:16, :], ACT.Exp, scale=-0.5).then_inc(sem("drstd"), 1)
            act.wait_ge(sem("rw"), 64)
        @block.tensor
        def _(pe):
            pe.wait_ge(sem("tab"), 16)
            pe.wait_ge(sem("ones"), 1)
            for i in range(TILES):
                r = ROWS[i]
                pe.wait_ge(sem("xn"), i + 1)
                if i >= 4:
                    pe.wait_ge(sem("hT"), i - 3)
                for k in range(KC):
                    b = ps[(2 * i + k // 4) % 8]
                    last_mm = nc.tensor.transpose(b[:, (k % 4) * P:(k % 4) * P + r], x_all[0:r, i * D + k * P:i * D + (k + 1) * P], ident[0:r, 0:r])
                last_mm.then_inc(sem("xT_ps"), 1)
            pe.wait_ge(sem("hT"), TILES)
            for g, (s, kind, dst, half, c, n) in enumerate(items):
                if g == 0 or items[g - 1][0] != s:
                    pe.wait_ge(sem(f"w_in{s % 3}"), 16 * (s // 3 + 1))
                if g >= 8:
                    for q in ("T", "N"):
                        if items[g - 8][1] == q:
                            pe.wait_ge(sem(f"ev_{q}"), upto[q][g - 7])
                w = head3(wring[s % 3], 256)
                for k in range(KC):
                    if kind == "T":
                        mm = nc.tensor.matmul(ps[g % 8][:, 0:N3], w[:, k, c * P:(c + 1) * P],
                                              hT[:, k * TOK + n * N3:k * TOK + (n + 1) * N3], start=(k == 0), stop=(k == KC - 1))
                    else:
                        mm = nc.tensor.matmul(ps[g % 8][0:ROWS[c], 0:256], tok(hT, k, c), w[:, k, :],
                                              start=(k == 0), stop=(k == KC - 1))
                mm.then_inc(sem("proj"), 1)
            pe.wait_ge(sem("ev_T"), upto["T"][-1])
            pe.wait_ge(sem("ev_N"), upto["N"][-1])
            for i in range(TILES):
                r = ROWS[i]
                if i >= 2:
                    pe.wait_ge(sem("knat_ready"), i - 1)
                for h in range(H):
                    mm = nc.tensor.transpose(ps[i % 2][0:r, h * P:(h + 1) * P], tok(kT, h, i), ident)
                mm.then_inc(sem("knat_ps"), 1)
            phase_end(pe, 1)
            k = 0
            for h in range(H):
                if h:
                    pe.wait_ge(sem("o_ev"), 9 * h)
                for l in range(NLEV + 1):
                    if l < NLEV:
                        pe.wait_ge(sem("xl_ready"), NLEV * h + l + 1)
                    else:
                        pe.wait_ge(sem("q_ready"), H)
                    bb = 2 * (l % 2)
                    if k >= 2:
                        pe.wait_ge(sem("lev_ev"), k - 1)
                    for c in range(8):
                        if l < NLEV:
                            a = b_ = X[l % 2][:, c * P:(c + 1) * P]
                        else:
                            a = tok(kkT, h, c)
                            b_ = tok(hqT, h, c)
                        mm = nc.tensor.matmul(ps[bb + c // 4][:, (c % 4) * P:(c % 4 + 1) * P], a, b_, start=True, stop=True)
                    if l >= NLEV - 2:
                        a = X[l % 2][:, SEQ:TOK] if l < NLEV else tok(kkT, h, 8)
                        b_ = X[l % 2][:, SEQ:TOK] if l < NLEV else tok(hqT, h, 8)
                        mm = nc.tensor.matmul(ps[6 + l % 2][0:SMP, 0:SMP], a, b_, start=True, stop=True)
                    mm.then_inc(sem("lev_ps"), 1)
                    k += 1
                pe.wait_ge(sem("kd_ready"), h + 1)
                pe.wait_ge(sem("lev_ev"), k)
                for c in range(9):
                    b = ps[2 + c // 4] if c < 8 else ps[1]
                    mm = nc.tensor.transpose(b[0:ROWS[c], (c % 4) * P:(c % 4 + 1) * P], tok(kkT, h, c), ident)
                    if c in (3, 7):
                        mm.then_inc(sem("kdn_ps"), 1)
                mm.then_inc(sem("kdns_ps"), 1)
                pe.wait_ge(sem("kdn"), 2 * h + 2)
                for c in range(8):
                    vv = hi[:, c * HW + h * P:c * HW + (h + 1) * P]
                    nc.tensor.matmul(ps[6 + c % 2][:, 0:P], KdN[:, c * P:(c + 1) * P], vv, start=True, stop=True).then_inc(sem("ds_ps"), 1)
                    if c >= 2:
                        pe.wait_ge(sem("o_ev"), 9 * h + c - 1)
                    nc.tensor.matmul(ps[4 + c % 2][:, 0:P], AT[:, c * P:(c + 1) * P], vv, start=True, stop=False)
                    pe.wait_ge(sem("state"), 9 * h + c + 1)
                    nc.tensor.matmul(ps[4 + c % 2][:, 0:P], tok(hqT, h, c), S[:, c * P:(c + 1) * P], start=False, stop=True).then_inc(sem("o_ps"), 1)
                pe.wait_ge(sem("state"), 9 * h + 9)
                pe.wait_ge(sem("smp_ready"), h + 1)
                pe.wait_ge(sem("s0_in"), 16 * (h + 1))
                vs = hi[0:SMP, 8 * HW + h * P:8 * HW + (h + 1) * P]
                for b in range(NB):
                    mm = nc.tensor.matmul(ps[2 + b // 4][:, (b % 4) * P:(b % 4 + 1) * P], KdM[0:SMP, b * P:(b + 1) * P], vs, start=True, stop=True)
                mm.then_inc(sem("dss_ps"), 1)
                nc.tensor.matmul(ps[0][0:SMP, 0:P], ATs[0:SMP, :], vs, start=True, stop=False)
                for b in range(NB):
                    mm = nc.tensor.matmul(ps[0][0:SMP, 0:P], Qpad[:, b * SMP:(b + 1) * SMP], S0[:, b * P:(b + 1) * P], start=False, stop=(b == NB - 1))
                mm.then_inc(sem("os_ps"), 1)
            pe.wait_ge(sem("og_ready"), 1)
            for i in range(TILES):
                if i >= 2:
                    pe.wait_ge(sem("og_ev"), i - 1)
                for h in range(H):
                    mm = nc.tensor.transpose(ps[i % 2][:, h * P:h * P + ROWS[i]], hi[0:ROWS[i], i * HW + h * P:i * HW + (h + 1) * P], ident[0:ROWS[i], 0:ROWS[i]])
                mm.then_inc(sem("og_ps"), 1)
            phase_end(pe, 2)
            pe.sem_inc(sem("v_used"), 64)
            pe.wait_ge(sem("oh_in"), 16)
            pe.wait_ge(sem("lam_in"), 1)
            nc.tensor.matmul(ps[7][:, 0:2], ones[0:QK, :], lamv[0:QK, 0:2], start=True, stop=True).then_inc(sem("lam_ps"), 1)
            pe.wait_ge(sem("rb_ready"), 1)
            R = BUCKETS + 1
            for h in range(H):
                pe.wait_ge(sem("rbb"), h + 1)
                nc.tensor.matmul(ps[h][:, 0:384], pT[0][0:R, h * P:(h + 1) * P], oh[0:R, 0:384], start=True, stop=True).then_inc(sem("band_ps"), 1)
            pe.wait_ge(sem("band_ready"), 1)
            units = [(h, i) for h in range(H) for i in range(8)]

            def scores(n):
                h, i = units[n]
                for m in range(2):
                    if n or m:
                        pe.wait_ge(sem("z_ready"), 2 * n + m - 1) if 2 * n + m - 1 > 0 else None
                    rows = slice(QK * m, QK * m + QK)
                    for j in range(0, i + 1, 4):
                        w = min(4, i + 1 - j) * P
                        mm = nc.tensor.matmul(ps[2 * m + j // 4][:, 0:w], qT[rows, h * TOK + i * P:h * TOK + (i + 1) * P],
                                              kT[rows, h * TOK + j * P:h * TOK + j * P + w], start=True, stop=True)
                    mm.then_inc(sem("s_ps"), 1)

            def weigh(n):
                h, i = units[n]
                pe.wait_ge(sem("a_ready"), n + 1)
                for j in range(i + 1):
                    mm = nc.tensor.transpose(ps[4 + j // 4][:, (j % 4) * P:(j % 4 + 1) * P], zp[n % 2][:, j * P:(j + 1) * P], ident)
                    if j % 4 == 3 or j == i:
                        mm.then_inc(sem("pT_ps"), 1)
                pe.wait_ge(sem("pT"), cumT[(h, i, i // 4 * 4)])
                if n:
                    pe.wait_ge(sem("o_norm"), n)
                for j in range(i + 1):
                    mm = nc.tensor.matmul(ps[6][:, 0:P], pT[n % 2][:, j * P:(j + 1) * P], v_nat[:, j * HW + h * P:j * HW + (h + 1) * P],
                                          start=(j == 0), stop=(j == i))
                mm.then_inc(sem("oa_ps"), 1)

            def turn(n):
                pe.wait_ge(sem("o_norm"), n + 1)
                if n:
                    pe.wait_ge(sem("mix_ev"), n)
                nc.tensor.transpose(ps[7][:, 0:P], o_sb[n % 2], ident).then_inc(sem("ot_ps"), 1)

            scores(0)
            for n in range(len(units)):
                if n + 1 < len(units):
                    scores(n + 1)
                if n:
                    turn(n - 1)
                weigh(n)
            turn(len(units) - 1)
            pe.wait_ge(sem("prompt_gone"), 1)

            pe.sem_inc(sem("kt_used"), 2)
            pe.wait_ge(sem("kn_ready"), 1)

            def keys(b, s):
                pe.wait_ge(sem("qcur"), b + 1)
                pe.wait_ge(sem("s_free"), b + 1)
                q = qcur[s]
                for g in range(4):
                    pe.wait_ge(sem("k_used"), b * PAGES + 8 * g + 8)
                    k8 = kt[g % 2].rearrange("p (n c w) -> p n c w", n=8, w=32)
                    for h in range(H):
                        for j in range(4):
                            c = h * 4 + j
                            mm = nc.tensor.matmul(ps[g // 2][32 * h:32 * h + 32, (g % 2) * 256:(g % 2) * 256 + 256],
                                                  q[:, c * 32:(c + 1) * 32], k8[:, :, c, :], start=(j == 0), stop=(j == 3))
                    mm.then_inc(sem("kt_used"), 1)
                for h in range(H):
                    for j in range(4):
                        c = h * 4 + j
                        mm = nc.tensor.matmul(ps[2][32 * h:32 * h + 32, 0:SMP], q[0:32, c * 32:(c + 1) * 32], kn[0:32, c * 32:(c + 1) * 32],
                                              start=(j == 0), stop=(j == 3))
                mm.then_inc(sem("s_done"), 1)

            def flip(b):
                pe.wait_ge(sem("z_exp"), b + 1)
                for g in range(9):
                    if g == 8:
                        pe.wait_ge(sem("PT"), b * 3 + 1)
                    n = P if g < 8 else SMP
                    mm = nc.tensor.transpose(ps[3 + g // 4 % 2][0:n, (g % 4) * P:(g % 4 + 1) * P], z[:, g * P:g * P + n], ident)
                    if g in (3, 7, 8):
                        mm.then_inc(sem("PT_ps"), 1)

            def values(b, k0):
                pe.wait_ge(sem("o_free"), b + 1)
                for g in range(8):
                    pe.wait_ge(sem("PT"), b * 3 + g // 4 + 1)
                    for q4 in range(4):
                        slot = (4 * g + q4) % RING
                        pe.wait_ge(sem(f"page{slot}"), k0 + (g // 4 + 1) * 16)
                    for i in range(4):
                        lhs = PT[:, (i * 9 + g) * COLS:(i * 9 + g + 1) * COLS]
                        mm = nc.tensor.matmul(ps[5][0:COLS, :], lhs, ring[:, (g % 4 * 4 + i) * HW:(g % 4 * 4 + i + 1) * HW],
                                              start=(g == 0 and i == 0), stop=False)
                    mm.then_inc(sem("v_groups"), 1)
                    pe.wait_ge(sem("v_groups"), b * 8 + g + 1)
                    pe.sem_inc(sem("v_used"), 4)
                pe.wait_ge(sem("PT"), b * 3 + 3)
                pe.sem_inc(sem("pe_held"), 1)
                lhs = PT[0:SMP, 8 * COLS:9 * COLS]
                nc.tensor.matmul(ps[5][0:COLS, :], lhs, vnew, start=False, stop=True).then_inc(sem("pv"), 1)

            def top(b):
                pe.wait_ge(sem("mxc"), b + 1)
                nc.tensor.transpose(ps[6][0:1, 0:P], mxc, ident).then_inc(sem("mx_ps"), 1)
                pe.wait_ge(sem("mall"), b + 1)
                nc.tensor.matmul(ps[7][:, 0:1], mall[0:1, :], ones[0:1, 0:1], start=True, stop=True).then_inc(sem("mb_ps"), 1)

            keys(0, 0)
            top(0)
            flip(0)
            with pe.Fori(0, NB - 1) as t:
                keys(t + 1, 0)
                top(t + 1)
                values(t, t * 64 + 64)
                flip(t + 1)
            values(NB - 1, 7 * 64 + 32)
            pe.wait_ge(sem("dsum_in"), 1)
            nc.tensor.matmul(ps[0][0:COLS, 0:NB], cst("rowsum"), sum_all, start=True, stop=True).then_inc(sem("dsum_ps"), 1)
            pe.wait_ge(sem("dnorm"), 1)
            for n in range(2):
                mm = nc.tensor.matmul(ps[1 + n][0:16, :], comb[0:COLS, :], o_all[0:COLS, n * 512:(n + 1) * 512], start=True, stop=True)
            mm.then_inc(sem("dmix_ps"), 1)
            pe.wait_ge(sem("d_ready"), 1)
            for b in range(NB):
                mm = nc.tensor.transpose(ps[3][:, b * 16:(b + 1) * 16], o16[0:16, b * P:(b + 1) * P], ident[0:16, 0:16])
            mm.then_inc(sem("dT_ps"), 1)
        @block.vector
        def _(dve):
            V = nc.vector
            ch = Chain(dve, sem("dve"))

            def step(ins):
                ch.step(ins)
                ch.wait()

            def mean_eps(a, n):
                return V.tensor_scalar(a, a, 1.0 / n, EPS, ALU.mult, ALU.add)

            dve.wait_ge(sem("ss"), TILES)
            dve.wait_ge(sem("small0"), 1)
            mean_eps(ss, D).then_inc(sem("ms"), 1)
            dve.wait_ge(sem("rstd"), 1)

            def norm_tile(i):
                r = ROWS[i]
                xi = x_all[0:r, i * D:(i + 1) * D]
                V.tensor_scalar(xi, xi, rstd[0:r, i:i + 1], None, ALU.mult).then_inc(sem("xn"), 1)

            norm_tile(0)
            dve.wait_ge(sem("vecs"), NV_TOTAL)
            for i in range(TILES):
                r = ROWS[i]
                if i + 1 < TILES:
                    norm_tile(i + 1)
                dve.wait_ge(sem("xT_ps"), i + 1)
                for g in range(2):
                    o = head3(hT, TOK)[:, 4 * g:4 * g + 4, i * P:i * P + r]
                    last = V.tensor_tensor(o, head3(ps[(2 * i + g) % 8][:, :], P)[:, :, 0:r],
                                           n1w[:, 4 * g:4 * g + 4].unsqueeze(2).broadcast_to([P, 4, r]), ALU.mult)
                last.then_inc(sem("hT"), 1)
            for g, (s, kind, dst, half, c, n) in enumerate(items):
                if kind != "N":
                    continue
                dve.wait_ge(sem("proj"), g + 1)
                r = ROWS[c]
                V.tensor_copy(dst[0:r, c * HW + half * 256:c * HW + half * 256 + 256], ps[g % 8][0:r, 0:256]).then_inc(sem("ev_N"), 1)
            for i in range(TILES):
                dve.wait_ge(sem("knat_ps"), i + 1)
                if i >= 2:
                    dve.wait_ge(sem(f"knat_out{i % 2}"), 16 * (i // 2))
                V.tensor_copy(knat[i % 2][0:ROWS[i], :], ps[i % 2][0:ROWS[i], :]).then_inc(sem("knat_ready"), 1)
            phase_end(dve, 1)

            dve.wait_ge(sem("pool"), 3)
            V.tensor_tensor(lg1, lg1, lg0, ALU.subtract).then_inc(sem("lbd"), 1)
            dve.wait_ge(sem("lbe"), 1)
            step(V.tensor_scalar(lbT, lbT, 1.0, None, ALU.add))
            step(V.reciprocal(lbT, lbT))
            step(V.tensor_scalar(omlb, lbT, -1.0, 1.0, ALU.mult, ALU.add))
            for h in range(H):
                sl = slice(h * TOK, (h + 1) * TOK)
                g, q, kk = gT[:, sl], hqT[:, sl], kkT[:, sl]
                dve.wait_ge(sem("ef"), h + 1)
                step(V.tensor_scalar(g, g, 1.0, None, ALU.add))
                step(V.reciprocal(g, g))
                ch.step(V.tensor_scalar(g, g, omlb[:, h:h + 1], lbT[:, h:h + 1], ALU.mult, ALU.add))
                ch.wait()
                V.tensor_scalar(kk, g, -1.0, 1.0, ALU.mult, ALU.add).then_inc(sem("f_ready"), 1)
                dve.wait_ge(sem("eq"), h + 1)
                step(V.tensor_scalar(tmp, tmp, 1.0, None, ALU.add))
                step(V.reciprocal(tmp, tmp))
                V.scalar_tensor_tensor(out=q, in0=q, scalar=P ** -0.5, in1=tmp, op0=ALU.mult, op1=ALU.mult).then_inc(sem("q_ready"), 1)
                dve.wait_ge(sem("lnf"), h + 1)
                ch.step(V.tensor_tensor_scan(g, reset, g, 0.0, ALU.mult, ALU.add))
            ch.wait()
            k = 0
            lev = cst("level").bitcast(I32)
            for h in range(H):
                sl = slice(h * TOK, (h + 1) * TOK)
                g, q, kk = gT[:, sl], hqT[:, sl], kkT[:, sl]
                if h:
                    dve.wait_ge(sem("o_ps"), 8 * h)
                    dve.wait_ge(sem("os_ps"), h)
                    dve.wait_ge(sem("snew_out"), 16 * h)
                    dve.wait_ge(sem("state_out"), 16 * h)
                step(V.memset(AT, 0.0))
                step(V.memset(ATs, 0.0))
                step(V.memset(Qpad, 0.0))

                def diff(l):
                    w = LEVELS[l]
                    n = TOK if w < NT else SEQ
                    gg = g[:, 0:n].rearrange("p (b w) -> p b w", w=2 * w)
                    xx = X[l % 2][:, 0:n].rearrange("p (b w) -> p b w", w=2 * w)
                    mid = gg[:, :, w - 1:w].broadcast_to([P, n // (2 * w), w])
                    if l >= 2:
                        dve.wait_ge(sem("lev_ps"), k0 + l - 1)
                    V.tensor_tensor(xx[:, :, 0:w], mid, gg[:, :, 0:w], ALU.subtract)
                    V.tensor_tensor(xx[:, :, w:2 * w], gg[:, :, w:2 * w], mid, ALU.subtract).then_inc(sem("diff"), 1)

                def scale(l):
                    w = LEVELS[l]
                    n = TOK if w < NT else SEQ
                    dve.wait_ge(sem("expd"), NLEV * h + l + 1)
                    xx = X[l % 2][:, 0:n].rearrange("p (b w) -> p b w", w=2 * w)
                    V.tensor_tensor(xx[:, :, 0:w], xx[:, :, 0:w], kk[:, 0:n].rearrange("p (b w) -> p b w", w=2 * w)[:, :, 0:w], ALU.mult)
                    V.tensor_tensor(xx[:, :, w:2 * w], xx[:, :, w:2 * w], q[:, 0:n].rearrange("p (b w) -> p b w", w=2 * w)[:, :, w:2 * w], ALU.mult).then_inc(sem("xl_ready"), 1)

                def collect(l):
                    dve.wait_ge(sem("lev_ps"), k0 + l + 1)
                    if l:
                        dve.wait_ge(sem("lev_ev"), k0 + l)
                    for c in range(2):
                        last = V.copy_predicated(AT[:, c * 512:(c + 1) * 512].rearrange("p (a b) -> p a b", b=P),
                                                 lev[:, l * P:(l + 1) * P].unsqueeze(1).broadcast_to([P, 4, P]),
                                                 ps[2 * (l % 2) + c][:, :].rearrange("p (a b) -> p a b", b=P))
                    if l >= NLEV - 2:
                        last = V.copy_predicated(ATs[0:SMP, :], lev[0:SMP, l * P:l * P + SMP], ps[6 + l % 2][0:SMP, 0:SMP])
                    last.then_inc(sem("lev_ev"), 1)

                k0 = (NLEV + 1) * h
                diff(0)
                diff(1)
                scale(0)
                for l in range(NLEV):
                    if l + 1 < NLEV:
                        scale(l + 1)
                    collect(l)
                    if l + 2 < NLEV:
                        diff(l + 2)
                collect(NLEV)
                k += NLEV + 1
                gp, gs = head3(g[:, 0:SEQ], P), head3(g[:, SEQ:TOK], NT)
                x1p, x1s = head3(X[1][:, 0:SEQ], P), head3(X[1][:, SEQ:TOK], NT)
                V.tensor_tensor(x1p, gp[:, :, P - 1:P].broadcast_to([P, 8, P]), gp, ALU.subtract)
                V.tensor_tensor(x1s, gs[:, :, NT - 1:NT].broadcast_to([P, NB, NT]), gs, ALU.subtract).then_inc(sem("tails"), 1)
                dve.wait_ge(sem("etail"), 2 * h + 2)
                V.tensor_tensor(kk, kk, X[1], ALU.mult).then_inc(sem("kd_ready"), 1)
                step(V.tensor_tensor(q, q, X[0], ALU.mult))
                step(V.tensor_copy(bass.AP(tensor=Qpad.tensor, offset=Qpad.offset, ap=[list(Qpad.ap[0]), [SMP + NT, NB], [1, NT]]),
                                   head3(q[:, SEQ:TOK], NT)))
                ch.step(V.memset(S[:, 0:P], 0.0))
                ch.wait()
                dve.sem_inc(sem("state"), 1)
                for c in range(8):
                    dve.wait_ge(sem("ds_ps"), 8 * h + c + 1)
                    V.scalar_tensor_tensor(out=S[:, (c + 1) * P:(c + 2) * P], in0=S[:, c * P:(c + 1) * P],
                                           scalar=X[0][:, c * P + P - 1:c * P + P], in1=ps[6 + c % 2][:, 0:P],
                                           op0=ALU.mult, op1=ALU.add).then_inc(sem("state"), 1)
                    dve.wait_ge(sem("state"), 9 * h + c + 2)
                dve.sem_inc(sem("state_ready"), 1)
                dve.wait_ge(sem("kdns_ps"), h + 1)
                dve.wait_ge(sem("o_ps"), 8 * h + 8)
                dve.sem_inc(sem("s0_free"), 1)
                for b in range(NB):
                    ch.step(V.tensor_scalar(KdM[0:SMP, b * P:(b + 1) * P], ps[1][0:SMP, 0:P], cst("own", SMP)[:, b:b + 1], None, ALU.mult))
                ch.wait()
                dve.sem_inc(sem("smp_ready"), 1)
                dve.wait_ge(sem("dss_ps"), h + 1)
                dve.wait_ge(sem("os_ps"), h + 1)
                for b in range(NB):
                    c = SEQ + b * NT + NT - 1
                    ch.step(V.scalar_tensor_tensor(out=S0[:, b * P:(b + 1) * P], in0=S0[:, b * P:(b + 1) * P], scalar=X[0][:, c:c + 1],
                                                   in1=ps[2 + b // 4][:, (b % 4) * P:(b % 4 + 1) * P], op0=ALU.mult, op1=ALU.add))
                ch.wait()
                dve.sem_inc(sem("snew_ready"), 1)
            dve.wait_ge(sem("sq"), 4)
            step(V.memset(ss2, 1.0))
            step(V.tensor_reduce(ss2[:, 0:32], head3(kkT[:, 0:4096], P), AX, ALU.add))
            step(V.tensor_reduce(ss2[0:SMP, 32:36], head3(gT[0:SMP, 0:512], P), AX, ALU.add))
            mean_eps(ss2, P).then_inc(sem("ms2"), 1)
            eg, egs = hqT[:, 0:4096], gT[0:SMP, 512:1024]
            for e, gg in ((eg, gate[:, 0:4096]), (egs, gate[0:SMP, 4096:4608])):
                step(V.tensor_scalar(e, e, 1.0, None, ALU.add))
                step(V.reciprocal(e, e))
                step(V.tensor_tensor(e, e, gg, ALU.mult))
            dve.wait_ge(sem("rstd2"), 1)
            for o, r2, e in ((hi[:, 0:4096], rstd2[:, 0:32], eg), (hi[0:SMP, 4096:4608], rstd2[0:SMP, 32:36], egs)):
                n = r2.shape[1]
                step(V.tensor_tensor(head3(o, P), head3(o, P), r2.unsqueeze(2).broadcast_to([o.shape[0], n, P]), ALU.mult))
                step(V.tensor_tensor(o, o, e, ALU.mult))
            dve.sem_inc(sem("og_ready"), 1)
            for i in range(TILES):
                dve.wait_ge(sem("og_ps"), i + 1)
                r = ROWS[i]
                V.tensor_scalar(head3(mixT, TOK)[:, 4:8, i * P:i * P + r], head3(ps[i % 2][:, :], P)[:, :, 0:r], hgw, None, ALU.mult).then_inc(sem("og_ev"), 1)
            phase_end(dve, 2)

            step(V.tensor_tensor(lamv[0:QK, 0:2], lamv[0:QK, 0:2], lamv[0:QK, 2:4], ALU.mult))
            dve.sem_inc(sem("lam_in"), 1)
            dve.sem_inc(sem("rb_ready"), 1)
            for h in range(H):
                V.tensor_copy(pT[0][0:BUCKETS + 1, h * P:(h + 1) * P], rb[0:BUCKETS + 1, h:h + 1].broadcast_to([BUCKETS + 1, P])).then_inc(sem("rbb"), 1)
            dve.wait_ge(sem("lam_e"), 1)
            step(V.tensor_tensor(nlam, lamp[:, 1:2], lamp[:, 0:1], ALU.subtract))
            step(V.tensor_scalar(nlam, nlam, -LAM_INIT, None, ALU.add))
            step(V.tensor_scalar(daw, daw, 1.0 - LAM_INIT, None, ALU.mult))
            for h in range(H):
                dve.wait_ge(sem("band_ps"), h + 1)
                if h:
                    dve.wait_ge(sem("band_out"), 16 * h)
                V.tensor_copy(rowb, ps[h][:, 0:384]).then_inc(sem("rowb"), 1)
            for h in range(H):
                dve.wait_ge(sem("band_in"), 16 * H)
                step(V.tensor_copy(band[:, h * 1152:h * 1152 + 896], band[:, h * 1152 + 896:h * 1152 + 897].broadcast_to([P, 896])))
            dve.wait_ge(sem("dbias"), 16 * (16 * 4 + H))
            step(V.tensor_scalar(blast, blast, farc, None, ALU.subtract))
            step(V.tensor_scalar(bias4, bias4, farc, None, ALU.subtract))
            step(V.memset(biasn, NEG))
            step(V.tensor_copy(bass.AP(tensor=biasn.tensor, offset=biasn.offset, ap=[list(biasn.ap[0]), [SMP + NT, NB], [1, NT]]),
                               bias4.unsqueeze(1).broadcast_to([P, NB, NT])))
            dve.sem_inc(sem("band_ready"), 1)

            units = [(h, i) for h in range(H) for i in range(8)]

            def bias_max(n):
                h, i = units[n]
                w = (i + 1) * P
                a = att[:, 8 * (n % 2):8 * (n % 2) + 8]
                for m in range(2):
                    dve.wait_ge(sem("s_ps"), 2 * n + m + 1)
                    if n >= 2 and m == 0:
                        dve.wait_ge(sem("oa_ps"), n - 1)
                        dve.wait_ge(sem("orstd"), n - 1)
                    for j in range(0, i + 1, 4):
                        ww = min(4, i + 1 - j) * P
                        last = V.tensor_tensor(zp[n % 2][:, m * 1024 + j * P:m * 1024 + j * P + ww], ps[2 * m + j // 4][:, 0:ww],
                                               band[:, h * 1152 + 1152 - w + j * P:h * 1152 + 1152 - w + j * P + ww], ALU.add)
                    step(last)
                    step(V.tensor_reduce(a[:, m:m + 1], zp[n % 2][:, m * 1024:m * 1024 + w], AX, ALU.max, negate=True))
                    dve.sem_inc(sem("z_ready"), 1)

            def combine(n):
                h, i = units[n]
                w = (i + 1) * P
                a = att[:, 8 * (n % 2):8 * (n % 2) + 8]
                zb = zp[n % 2]
                dve.wait_ge(sem("p_ready"), 2 * n + 2)
                step(V.reciprocal(a[:, 4:6], a[:, 2:4]))
                step(V.tensor_tensor(a[:, 5:6], a[:, 5:6], nlam, ALU.mult))
                step(V.tensor_scalar(zb[:, 0:w], zb[:, 0:w], a[:, 4:5], None, ALU.mult))
                V.scalar_tensor_tensor(out=zb[:, 0:w], in0=zb[:, 1024:1024 + w], scalar=a[:, 5:6], in1=zb[:, 0:w],
                                       op0=ALU.mult, op1=ALU.add).then_inc(sem("a_ready"), 1)

            def finish(n):
                h, i = units[n]
                a = att[:, 8 * (n % 2):8 * (n % 2) + 8]
                dve.wait_ge(sem("oss"), n + 1)
                mean_eps(a[:, 6:7], P).then_inc(sem("oms"), 1)
                dve.wait_ge(sem("orstd"), n + 1)
                V.tensor_scalar(o_sb[n % 2], ps[6][:, 0:P], a[:, 7:8], None, ALU.mult).then_inc(sem("o_norm"), 1)

            def place(n):
                h, i = units[n]
                dve.wait_ge(sem("ot_ps"), n + 1)
                V.tensor_scalar(mixT[:, h * TOK + i * P:h * TOK + (i + 1) * P], ps[7][:, 0:P], daw, None, ALU.mult).then_inc(sem("mix_ev"), 1)

            bias_max(0)
            for n in range(len(units)):
                combine(n)
                if n + 1 < len(units):
                    bias_max(n + 1)
                if n:
                    place(n - 1)
                finish(n)
            place(len(units) - 1)
            dve.wait_ge(sem("prompt_left"), 1)
            dve.wait_ge(sem("mix_ev"), len(units))
            dve.sem_inc(sem("prompt_gone"), 2)

            step(V.memset(qd, 0.0))
            for i in range(4):
                for j in range(4):
                    for h in range(H):
                        o = qd[32 * i:32 * i + 32, :].rearrange("p (b h j i m t) -> p b h j i m t", b=NB, h=H, j=4, i=4, m=2)[:, :, h, j, i, j // 2, :]
                        ch.step(V.tensor_copy(o, head3(qT[32 * j:32 * j + 32, h * TOK + SEQ:(h + 1) * TOK], NT)))
            for j in range(4):
                ch.step(V.tensor_copy(kn[0:32, :].rearrange("p (h j w) -> p h j w", h=H, j=4)[:, :, j, :], head3(kT[32 * j:32 * j + 32, :], TOK)[:, :, SEQ:TOK]))
            step(V.scalar_tensor_tensor(out=comb[0:COLS, :], in0=cst("map2", COLS), scalar=nlam[0:COLS, :], in1=cst("map1", COLS), op0=ALU.mult, op1=ALU.add))
            dve.sem_inc(sem("kn_ready"), 1)
            dve.sem_inc(sem("prompt_done"), 1)
            dve.sem_inc(sem("s_free"), 1)
            dve.sem_inc(sem("z_free"), 1)
            dve.sem_inc(sem("o_free"), 1)

            def flip_keys(b, s):
                if s is None:
                    pass
                dve.wait_ge(sem("s_done0"), b + 1)
                V.tensor_scalar(qcur[0], qd[:, ds(b * HW, HW)] if not isinstance(b, int) else qd[:, b * HW:(b + 1) * HW], 1.0, None, ALU.mult).then_inc(sem("qcur"), 1)
                for j in range(PAGES):
                    if j % 8 == 0:
                        dve.wait_ge(sem("kt_used"), b * 4 + j // 8 + 1)
                    k0 = 0 if isinstance(b, int) else b * 64 - 32
                    dve.wait_ge(sem(f"page{j % RING}"), k0 + (j // RING + 1) * 16)
                    V.transpose(kt[j // 8 % 2][:, (j % 8) * HW:(j % 8 + 1) * HW], ring[:, (j % RING) * HW:(j % RING + 1) * HW]).then_inc(sem("k_used"), 1)

            def take_scores(b):
                dve.wait_ge(sem("s_done"), b + 1)
                dve.wait_ge(sem("z_free"), b + 1)
                ch.step(V.tensor_copy(z[:, 512:992], ps[1][:, 0:480]))
                ch.step(V.tensor_tensor(z[:, 992:1024], ps[1][:, 480:512], blast, ALU.add))
                bn = biasn[:, ds(b * SMP, SMP)] if not isinstance(b, int) else biasn[:, b * SMP:(b + 1) * SMP]
                ch.step(V.tensor_tensor(z[:, 1024:1056], ps[2][:, 0:SMP], bn, ALU.add))
                ch.wait()
                dve.wait_ge(sem("z_act"), b + 1)
                dve.sem_inc(sem("s_free"), 1)
                dve.sem_inc(sem("s_done0"), 1)
                V.tensor_reduce(mxc, z, AX, ALU.max).then_inc(sem("mxc"), 1)
                dve.wait_ge(sem("mx_ps"), b + 1)
                ch.step(V.tensor_reduce(m32[0:1, :].rearrange("p (h c) -> p h c", h=H), ps[6][0:1, 0:P].rearrange("p (h i c) -> p h c i", h=H, i=4), AX, ALU.max))
                ch.wait()
                V.tensor_copy(mall[0:1, :].rearrange("p (h i c) -> p h i c", h=H, i=4),
                              m32[0:1, :].rearrange("p (h c) -> p h c", h=H).unsqueeze(2).broadcast_to([1, H, 4, 8])).then_inc(sem("mall"), 1)
                dve.wait_ge(sem("mb_ps"), b + 1)
                V.tensor_scalar(nmx, ps[7][:, 0:1], -1.0, None, ALU.mult).then_inc(sem("nmx"), 1)

            def keep_sums(b):
                dve.wait_ge(sem("z_exp"), b + 1)
                dve.wait_ge(sem("PT_ps"), b * 3 + 3)
                sa = sum_all[:, ds(b, 1)] if not isinstance(b, int) else sum_all[:, b:b + 1]
                ch.step(V.tensor_scalar(sa, sumc, 1.0, None, ALU.mult))
                ch.wait()
                dve.sem_inc(sem("z_free"), 1)

            def keep_output(b):
                dve.wait_ge(sem("pv"), b + 1)
                ch.step(V.tensor_scalar(o_sel[0:COLS, :], ps[5][0:COLS, 0:P], cst("head", COLS)[:, 0:1], None, ALU.mult))
                for h in range(1, H):
                    ch.wait()
                    last = h == H - 1
                    o = o_sel[0:COLS, :] if not last else (o_all[0:COLS, ds(b * P, P)] if not isinstance(b, int) else o_all[0:COLS, b * P:(b + 1) * P])
                    ch.step(V.scalar_tensor_tensor(out=o, in0=ps[5][0:COLS, h * P:(h + 1) * P], scalar=cst("head", COLS)[:, h:h + 1],
                                                   in1=o_sel[0:COLS, :], op0=ALU.mult, op1=ALU.add))
                ch.wait()
                dve.sem_inc(sem("o_free"), 1)

            dve.sem_inc(sem("s_done0"), 1)
            flip_keys(0, 0)
            take_scores(0)
            keep_sums(0)
            with dve.Fori(0, NB - 1) as t:
                ch.enter(t, 9)
                flip_keys(t + 1, None)
                take_scores(t + 1)
                keep_output(t)
                keep_sums(t + 1)
            ch.leave(NB - 1)
            keep_output(NB - 1)
            dve.sem_inc(sem("dsum_in"), 1)
            dve.wait_ge(sem("dsum_ps"), 1)
            step(V.reciprocal(rsum[0:COLS, :], ps[0][0:COLS, 0:NB]))
            step(V.tensor_tensor(head3(o_all[0:COLS, :], P), head3(o_all[0:COLS, :], P), rsum[0:COLS, :].unsqueeze(2).broadcast_to([COLS, NB, P]), ALU.mult))
            dve.sem_inc(sem("dnorm"), 1)
            dve.wait_ge(sem("dmix_ps"), 1)
            for n in range(2):
                ch.step(V.tensor_copy(o16[0:16, n * 512:(n + 1) * 512], ps[1 + n][0:16, :]))
            ch.wait()
            dve.sem_inc(sem("dss"), 1)
            dve.wait_ge(sem("dsq"), 1)
            step(V.tensor_reduce(oms[0:16, :], head3(osq[0:16, :], P), AX, ALU.add))
            mean_eps(oms[0:16, :], P).then_inc(sem("dms"), 1)
            dve.wait_ge(sem("drstd"), 1)
            step(V.tensor_tensor(head3(o16[0:16, :], P), head3(o16[0:16, :], P), oms[0:16, :].unsqueeze(2).broadcast_to([16, NB, P]), ALU.mult))
            dve.sem_inc(sem("d_ready"), 1)
            dve.wait_ge(sem("dT_ps"), 1)
            for h in range(H):
                ch.step(V.tensor_scalar(head3(mixT[:, h * TOK + SEQ:(h + 1) * TOK], NT),
                                        ps[3][:, 0:128].rearrange("p (b h t) -> p b h t", b=NB, h=H)[:, :, h, :], daw, None, ALU.mult))
            ch.wait()
        block_a.__exit__(None, None, None)
        nc.all_engine_barrier()
        nc.clear_and_free_semaphores(list(sems.values()))
        sems.clear()
        part[0] = "_b"
        nc.all_engine_barrier()

        block = ctx.enter_context(nc.Block())

        @block.sync
        def _(sp):
            for g in range(4):
                sp.dma_start(head3(x1, D)[:, 2 * g:2 * g + 2, :],
                             xp_v[:, 2 * g:2 * g + 2, :]).then_inc(sem(f"x1_in{g}"), 16)
            sp.dma_start(x1[0:SMP, 8 * D:9 * D], xs_v).then_inc(sem("x1_in4"), 16)
            for i in range(TILES):
                sp.wait_ge(sem("xh_ready"), i + 1)
                sp.dma_start(rows_d[i * P:i * P + ROWS[i], :], xh[i % 2][0:ROWS[i], :]).then_inc(sem(f"xh_out{i % 2}"), 16)
            phase_end(sp, 1)
            sp.wait_ge(sem("routed"), 1)
            nit = sp.value_load(nit_i[0:1, 0:1], min_val=1, max_val=PAIRS)
            with sp.Fori(0, nit) as t:
                for s in range(2):
                    e = sp.value_load(eid[0:1, ds(t * 2 + s, 1)], min_val=0, max_val=NE - 1)
                    sp.wait_ge(sem("ye_ps"), t * 2 + s + 1)
                    w13 = wslot[s][:, 0:4096].rearrange("p (k f) -> p k f", k=KC)
                    sp.dma_start(w13[:, :, 0:FF], w1_v[ds(e * D, D), :].rearrange("(k p) f -> p k f", p=P)).then_inc(sem(f"wexp{s}"), 16)
                    sp.dma_start(w13[:, :, FF:2 * FF], w3_v[ds(e * D, D), :].rearrange("(k p) f -> p k f", p=P)).then_inc(sem(f"wexp{s}"), 16)
                    sp.dma_start(wslot[s][:, 4096:6144].rearrange("p (k f) -> p k f", k=2),
                                 w2_v[ds(e * FF, FF), :].rearrange("(k p) f -> p k f", p=P)).then_inc(sem(f"wexp{s}"), 16)
            phase_end(sp, 2)
            for i in range(TILES):
                sp.wait_ge(sem("y_ready"), i + 1)
                dst = ys_v if i == TILES - 1 else yp_v[:, i, :]
                sp.dma_start(dst, ya[i % 2][0:ROWS[i], :]).then_inc(sem(f"y_out{i % 2}"), 16)
            sp.wait_ge(sem("y_out0"), 16 * 5)
            sp.wait_ge(sem("y_out1"), 16 * 4)

        @block.gpsimd
        def _(pool):
            nc.gpsimd.memset(zero_rows, 0.0).then_inc(sem("zeros"), 1)
            pool.wait_ge(sem("zeros"), 1)
            for j in range(SURE, CAP):
                pool.dma_start(ye_d[j * P:(j + 1) * P, :], zero_rows).then_inc(sem("zeros_out"), 16)
            nc.gpsimd.memset(ids_sb, 0).then_inc(sem("ids0"), 1)
            pool.wait_ge(sem("ids0"), 1)
            pool.dma_start(ids_d.rearrange("(p j) c -> p (j c)", p=P), ids_sb).then_inc(sem("ids0_out"), 16)
            nc.gpsimd.iota(payload.rearrange("p (i c) -> p i c", c=16), [[P, TILES], [0, 16]], base=0, channel_multiplier=1).then_inc(sem("payload"), 1)
            pool.wait_ge(sem("ids0_out"), 16)
            pool.wait_ge(sem("payload"), 1)
            pool.wait_ge(sem("slots_ready"), 1)
            for c in range(2):
                for i in range(TILES):
                    pool.indirect_dma_start(
                        out=ids_d, out_offset=bass.IndirectOffsetOnAxis(ap=row_i[0:ROWS[i], c * TILES + i:c * TILES + i + 1], axis=0),
                        in_=payload[0:ROWS[i], i * 16:(i + 1) * 16], in_offset=None).then_inc(sem("ids_out"), 16)
            pool.wait_ge(sem("ids_out"), 16 * 2 * TILES)
            pool.dma_start(ids_sb, ids_d.rearrange("(p j) c -> p (j c)", p=P)).then_inc(sem("ids_in"), 16)
            pool.wait_ge(sem("ids_in"), 16)
            pool.wait_ge(sem("xh_out0"), 16 * 5)
            pool.wait_ge(sem("xh_out1"), 16 * 4)
            pool.wait_ge(sem("zeros_out"), 16 * (CAP - SURE))
            phase_end(pool, 1)
            nit = pool.value_load(nit_i[0:1, 0:1], min_val=1, max_val=PAIRS)
            with pool.Fori(0, nit) as t:
                for s in range(2):
                    pool.wait_ge(sem("xgT_ps"), t * 2 + s + 1)
                    nc.gpsimd.tensor_copy(idx_cur[:, s:s + 1], ids_sb[:, ds((t * 2 + s) * 16, 1)]).then_inc(sem("idx"), 1)
                    pool.wait_ge(sem("idx"), t * 2 + s + 1)
                    pool.sem_inc(sem("idx_seen"), 1)
                    pool.indirect_dma_start(out=xg[s], out_offset=None, in_=rows_d,
                                            in_offset=bass.IndirectOffsetOnAxis(ap=idx_cur[:, s:s + 1], axis=0)).then_inc(sem(f"xg_in{s}"), 16)
            phase_end(pool, 2)
            for i in range(TILES):
                if i >= 2:
                    pool.wait_ge(sem("yb_free"), i - 1)
                    pool.wait_ge(sem(f"y_out{i % 2}"), 16 * (i // 2))
                for c, buf in enumerate((ya, yb)):
                    pool.indirect_dma_start(out=buf[i % 2][0:ROWS[i], :], out_offset=None, in_=ye_d,
                                            in_offset=bass.IndirectOffsetOnAxis(ap=slot_i[0:ROWS[i], c * TILES + i:c * TILES + i + 1], axis=0)).then_inc(sem(f"yg{c}{i % 2}"), 16)

        @block.scalar
        def _(act):
            ch = Chain(act, sem("act"))
            for i in range(TILES):
                r = ROWS[i]
                act.wait_ge(sem("x1_ready"), i + 1)
                if i:
                    act.wait_ge(sem("ss1"), i)
                nc.scalar.activation(sqj[0:r, :], x1[0:r, i * D:(i + 1) * D], ACT.Square,
                                     accum_out=ss[0:r, i:i + 1]).then_inc(sem("ss1"), 1)
                act.wait_ge(sem("ms1"), i + 1)
                ch.step(nc.scalar.activation(rstd[0:r, i:i + 1], ss[0:r, i:i + 1], ACT.Ln))
                ch.wait()
                nc.scalar.activation(rstd[0:r, i:i + 1], rstd[0:r, i:i + 1], ACT.Exp, scale=-0.5).then_inc(sem("rstd1"), 1)
            act.wait_ge(sem("gshift"), 1)
            nc.scalar.activation(gexp, gexp, ACT.Exp).then_inc(sem("gexp"), 1)
            act.wait_ge(sem("eshift"), 1)
            nc.scalar.activation(gate2, gate2, ACT.Exp).then_inc(sem("eexp"), 1)
            phase_end(act, 1)
            nit = act.value_load(nit_i[0:1, 0:1], min_val=1, max_val=PAIRS)
            with act.Fori(0, nit) as t:
                for s in range(2):
                    act.wait_ge(sem("h_ps"), t * 2 + s + 1)
                    nc.scalar.activation(he[s][:, 0:FF], ps[4 + s][:, 0:FF], ACT.Exp, scale=-1.0).then_inc(sem("h_exp"), 1)
                for s in range(2):
                    act.wait_ge(sem("heT_ps"), t * 2 + s + 1)
                    nc.scalar.activation(heT[s], ps[6][:, s * FF:(s + 1) * FF], ACT.Copy).then_inc(sem("heT"), 1)
                for s in range(2):
                    act.wait_ge(sem("ye_ps"), t * 2 + s + 3)
                    act.wait_ge(sem(f"ye_out{s}"), t * 16 + 16)
                    nc.scalar.activation(ysb[s][:, 0:512], ps[2 * s][:, :], ACT.Copy).then_inc(sem("ye_a"), 1)
                    act.wait_ge(sem("ye_a"), t * 2 + s + 1)
                    act.wait_ge(sem("ye_v"), t * 2 + s + 1)
                    act.dma_start(ye_d[ds((t * 2 + s) * P, P), :], ysb[s]).then_inc(sem(f"ye_out{s}"), 16)
            act.wait_ge(sem("ye_out0"), nit * 16 + 16)
            act.wait_ge(sem("ye_out1"), nit * 16 + 16)
            act.sem_inc(sem("ye_seen"), 1)
            phase_end(act, 2)
            act.dma_start(fw, final_norm_w.rearrange("(a n) -> a n", a=1).broadcast_to([P, D])).then_inc(sem("fw"), 16)
            for i in range(TILES):
                r = ROWS[i]
                act.wait_ge(sem("x2_ready"), i + 1)
                nc.scalar.activation(yb[i % 2][0:r, :], ya[i % 2][0:r, :], ACT.Square,
                                     accum_out=ss[0:r, i:i + 1]).then_inc(sem("ssf"), 1)
                act.wait_ge(sem("msf"), i + 1)
                ch.step(nc.scalar.activation(rstd[0:r, i:i + 1], ss[0:r, i:i + 1], ACT.Ln))
                ch.wait()
                nc.scalar.activation(rstd[0:r, i:i + 1], rstd[0:r, i:i + 1], ACT.Exp, scale=-0.5).then_inc(sem("rstdf"), 1)

        @block.tensor
        def _(pe):

            def project(i):
                r = ROWS[i]
                if i >= 2:
                    pe.wait_ge(sem("x1_ready"), i - 1)
                for n in range(2):
                    for k in range(KC):
                        mm = nc.tensor.matmul(ps[2 * (i % 2) + n][0:r, :], tok(mixT, k, i), wout[:, k * D + n * 512:k * D + (n + 1) * 512],
                                              start=(k == 0), stop=(k == KC - 1))
                    mm.then_inc(sem("x1_ps"), 1)

            def router(i):
                r = ROWS[i]
                pe.wait_ge(sem("xh_ready"), i + 1)
                if i:
                    pe.wait_ge(sem("h2T"), 2 * i)
                for k in range(KC):
                    mm = nc.tensor.transpose(ps[4 + k // 4][:, (k % 4) * P:(k % 4) * P + r], xh[i % 2][0:r, k * P:(k + 1) * P], ident[0:r, 0:r])
                    if k % 4 == 3:
                        mm.then_inc(sem("h2T_ps"), 1)
                pe.wait_ge(sem("h2T"), 2 * i + 2)
                if i:
                    pe.wait_ge(sem("lg"), i)
                for k in range(KC):
                    mm = nc.tensor.matmul(ps[6][0:r, 0:20], h2T[i % 2][:, k * P:k * P + r], wr[:, k * 20:(k + 1) * 20], start=(k == 0), stop=(k == KC - 1))
                mm.then_inc(sem("lg_ps"), 1)

            project(0)
            for i in range(TILES):
                if i + 1 < TILES:
                    project(i + 1)
                router(i)
            pe.wait_ge(sem("counts_in"), 1)
            nc.tensor.matmul(ps[7][:, 0:TILES * 16], cst("tri"), Mx, start=True, stop=False)
            nc.tensor.matmul(ps[7][:, 0:TILES * 16], ones, cum, start=False, stop=True)
            nc.tensor.matmul(ps[6][:, 64:80], ones, rk[:, 0:16], start=True, stop=True).then_inc(sem("rank_ps"), 1)
            phase_end(pe, 1)
            pe.sem_inc(sem("ye_ps"), 2)
            pe.sem_inc(sem("xgT_ps"), 2)
            nit = pe.value_load(nit_i[0:1, 0:1], min_val=1, max_val=PAIRS)

            def hidden(t, s, k0, k1):
                w13 = wslot[s][:, 0:4096].rearrange("p (k f) -> p k f", k=KC)
                for k in range(k0, k1):
                    mm = nc.tensor.matmul(ps[4 + s][:, :], xT[s][:, k * P:(k + 1) * P], w13[:, k, :], start=(k == 0), stop=(k == KC - 1))
                if k1 == KC:
                    mm.then_inc(sem("h_ps"), 1)

            def flip_hidden(t, s):
                pe.wait_ge(sem("he_ready"), t * 2 + s + 1)
                for k in range(2):
                    mm = nc.tensor.transpose(ps[6][:, s * FF + k * P:s * FF + (k + 1) * P], he[s][:, k * P:(k + 1) * P], ident)
                mm.then_inc(sem("heT_ps"), 1)

            def down(t, s):
                pe.wait_ge(sem("heT"), t * 2 + s + 1)
                w2 = wslot[s][:, 4096:6144]
                for n in range(2):
                    for k in range(2):
                        mm = nc.tensor.matmul(ps[2 * s + n][:, :], heT[s][:, k * P:(k + 1) * P], w2[:, k * D + n * 512:k * D + (n + 1) * 512], start=(k == 0), stop=(k == 1))
                mm.then_inc(sem("ye_ps"), 1)

            with pe.Fori(0, nit) as t:
                for s in range(2):
                    pe.wait_ge(sem("xbank_free"), t * 4 + 2 * s + 2)
                    pe.wait_ge(sem(f"xg_in{s}"), t * 16 + 16)
                    for k in range(KC):
                        mm = nc.tensor.transpose(ps[2 * s + k // 4][:, (k % 4) * P:(k % 4 + 1) * P], xg[s][:, k * P:(k + 1) * P], ident)
                    mm.then_inc(sem("xgT_ps"), 1)
                for s in range(2):
                    pe.wait_ge(sem("xT_s"), t * 4 + 2 * s + 2)
                    pe.wait_ge(sem(f"wexp{s}"), t * 48 + 48)
                    if s == 0:
                        hidden(t, 0, 0, KC)
                    else:
                        hidden(t, 1, 0, 6)
                        flip_hidden(t, 0)
                        hidden(t, 1, 6, KC)
                down(t, 0)
                flip_hidden(t, 1)
                down(t, 1)
            phase_end(pe, 2)

        @block.vector
        def _(dve):
            V = nc.vector
            ch = Chain(dve, sem("dve"))

            def step(ins):
                ch.step(ins)
                ch.wait()

            def mean_eps(a, n):
                return V.tensor_scalar(a, a, 1.0 / n, EPS, ALU.mult, ALU.add)


            def residual(i):
                r = ROWS[i]
                dve.wait_ge(sem(f"x1_in{i // 2}"), 16)
                dve.wait_ge(sem("x1_ps"), 2 * i + 2)
                for n in range(2):
                    xx = x1[0:r, i * D + n * 512:i * D + (n + 1) * 512]
                    last = V.tensor_tensor(xx, ps[2 * (i % 2) + n][0:r, :], xx, ALU.add)
                last.then_inc(sem("x1_ready"), 1)

            def norm2(i):
                r = ROWS[i]
                dve.wait_ge(sem("ss1"), i + 1)
                mean_eps(ss[0:r, i:i + 1], D).then_inc(sem("ms1"), 1)
                dve.wait_ge(sem("rstd1"), i + 1)
                if i >= 2:
                    dve.wait_ge(sem(f"xh_out{i % 2}"), 16 * (i // 2))
                V.tensor_scalar(xh[i % 2][0:r, :], x1[0:r, i * D:(i + 1) * D], rstd[0:r, i:i + 1], None, ALU.mult).then_inc(sem("xh_ready"), 1)

            def logits(i):
                r = ROWS[i]
                for g in range(2):
                    dve.wait_ge(sem("h2T_ps"), 2 * i + g + 1)
                    V.tensor_tensor(h2T[i % 2][:, 512 * g:512 * g + 512].rearrange("p (a b) -> p a b", b=P)[:, :, 0:r],
                                    head3(ps[4 + g][:, :], P)[:, :, 0:r],
                                    n2w[:, 4 * g:4 * g + 4].unsqueeze(2).broadcast_to([P, 4, r]), ALU.mult).then_inc(sem("h2T"), 1)
                dve.wait_ge(sem("lg_ps"), i + 1)
                V.tensor_tensor(lgall[0:r, i * 20:(i + 1) * 20], ps[6][0:r, 0:20], rbias[0:r, :], ALU.add).then_inc(sem("lg"), 1)

            residual(0)
            for i in range(TILES):
                norm2(i)
                if i + 1 < TILES:
                    residual(i + 1)
                logits(i)

            dve.wait_ge(sem("lg"), TILES)
            lg3 = head3(lgall, 20)
            step(V.memset(gpad, -3e38))
            step(V.tensor_copy(head3(gpad, 8)[:, :, 0:NG], lg3[:, :, 0:NG]))
            for i in range(TILES):
                step(V.max(g8, gpad[:, i * 8:(i + 1) * 8]))
                step(V.max_index(gi, g8, gpad[:, i * 8:(i + 1) * 8]))
                step(V.tensor_copy(gidx[:, i:i + 1], gi[:, 0:1]))
                step(V.tensor_scalar(gexp[:, i * 4:(i + 1) * 4], lgall[:, i * 20:i * 20 + 4], g8[:, 0:1], None, ALU.subtract))
            dve.sem_inc(sem("gshift"), 1)
            ohg = head3(oh1[:, 0:36], NG)
            step(V.tensor_tensor(ohg, cst("iota")[:, 0:NG].unsqueeze(1).broadcast_to([P, TILES, NG]),
                                 gidx.unsqueeze(2).broadcast_to([P, TILES, NG]), ALU.is_equal))
            off = head3(oh2[:, 0:36], NG)
            step(V.tensor_scalar(off, ohg, -NEG, NEG, ALU.mult, ALU.add))
            for i in range(TILES):
                lmi = lm[:, i * 16:(i + 1) * 16].rearrange("p (g e) -> p g e", e=EG)
                lei = lgall[:, i * 20 + NG:(i + 1) * 20].rearrange("p (g e) -> p g e", e=EG)
                step(V.tensor_tensor(lmi, lei, ohg[:, i, :].unsqueeze(2).broadcast_to([P, NG, EG]), ALU.mult))
                step(V.tensor_tensor(lmi, lmi, off[:, i, :].unsqueeze(2).broadcast_to([P, NG, EG]), ALU.add))
                step(V.max(e8, lm[:, i * 16:(i + 1) * 16]))
                step(V.max_index(ei, e8, lm[:, i * 16:(i + 1) * 16]))
                step(V.tensor_copy(v12[:, 2 * i:2 * i + 2], e8[:, 0:2]))
                step(V.tensor_copy(i12[:, 2 * i:2 * i + 2], ei[:, 0:2]))
            v3, i3 = head3(v12, 2), head3(i12, 2)
            V.tensor_tensor(gate2.unsqueeze(2), v3[:, :, 1:2], v3[:, :, 0:1], ALU.subtract).then_inc(sem("eshift"), 1)
            iot = cst("iota")[:, 0:NE].unsqueeze(1).broadcast_to([P, TILES, NE])
            o1, o2, M3, c3, r3 = (head3(a, NE) for a in (oh1, oh2, Mx, cum, rk))
            step(V.tensor_tensor(o1, iot, i3[:, :, 0:1].broadcast_to([P, TILES, NE]), ALU.is_equal))
            step(V.tensor_tensor(o2, iot, i3[:, :, 1:2].broadcast_to([P, TILES, NE]), ALU.is_equal))
            step(V.tensor_tensor(Mx, oh1, oh2, ALU.add))
            step(V.tensor_scalar(M3[:, 8, :], M3[:, 8, :], cst("valid"), None, ALU.mult))
            step(V.memset(c3[:, 0, :], 0.0))
            for i in range(1, TILES):
                step(V.tensor_tensor(c3[:, i, :], c3[:, i - 1, :], M3[:, i - 1, :], ALU.add))
            step(V.tensor_tensor(rk[:, 0:16], c3[:, 8, :], M3[:, 8, :], ALU.add))
            dve.sem_inc(sem("counts_in"), 1)
            dve.wait_ge(sem("gexp"), 1)
            step(V.tensor_reduce(ptop, head3(gexp, 4), AX, ALU.add))
            step(V.reciprocal(ptop, ptop))
            dve.wait_ge(sem("eexp"), 1)
            step(V.tensor_scalar(gate1, gate2, 1.0, None, ALU.add))
            step(V.reciprocal(gate1, gate1))
            step(V.tensor_tensor(gate1, gate1, ptop, ALU.mult))
            step(V.tensor_tensor(gate2, gate2, gate1, ALU.mult))
            dve.wait_ge(sem("rank_ps"), 1)
            step(V.tensor_scalar(cnt_i, ps[6][:, 64:80], 127.0, None, ALU.add))
            step(V.tensor_scalar(cnt_i, cnt_i, 7, None, ALU.logical_shift_right))
            step(V.tensor_copy(ntl, cnt_i))
            step(V.tensor_tensor_scan(endt, ones[:, 0:NE], ntl, 0.0, ALU.mult, ALU.add))
            step(V.tensor_tensor(base, endt, ntl, ALU.subtract))
            step(V.tensor_scalar(base, base, float(P), None, ALU.mult))
            step(V.tensor_tensor(r3, head3(ps[7][:, 0:TILES * 16], NE), base.unsqueeze(1).broadcast_to([P, TILES, NE]), ALU.add))
            for c, o in ((0, oh1), (1, oh2)):
                step(V.tensor_tensor(o, o, rk, ALU.mult))
                step(V.tensor_reduce(slotf[:, c * TILES:(c + 1) * TILES], head3(o, NE), AX, ALU.add))
            step(V.tensor_copy(slot_i, slotf))
            step(V.tensor_scalar(row_i, slot_i, P - 1, 5, ALU.bitwise_and, ALU.logical_shift_left))
            step(V.tensor_scalar(row_j, slot_i, 7, None, ALU.logical_shift_right))
            step(V.tensor_tensor(row_i, row_i, row_j, ALU.bitwise_or))
            dve.sem_inc(sem("slots_ready"), 1)
            c3_ = cmp.rearrange("p (j e) -> p j e", e=NE)
            step(V.tensor_tensor(c3_, endt.unsqueeze(1).broadcast_to([P, CAP, NE]), cst("iota").unsqueeze(2).broadcast_to([P, CAP, NE]), ALU.is_le))
            step(V.tensor_reduce(eid_f, c3_, AX, ALU.add))
            step(V.tensor_scalar(eid, eid_f, float(NE - 1), None, ALU.min))
            step(V.tensor_scalar(base[:, 0:1].bitcast(I32), endt[:, NE - 1:NE], 1.0, None, ALU.add))
            step(V.tensor_scalar(nit_i, base[:, 0:1].bitcast(I32), 1, None, ALU.logical_shift_right))
            dve.sem_inc(sem("routed"), 1)
            phase_end(dve, 1)

            dve.sem_inc(sem("xbank_free"), 4)
            dve.sem_inc(sem("ye_out0"), 16)
            dve.sem_inc(sem("ye_out1"), 16)
            nit = dve.value_load(nit_i[0:1, 0:1], min_val=1, max_val=PAIRS)
            with dve.Fori(0, nit) as t:
                ch.enter(t, 6)
                for s in range(2):
                    dve.wait_ge(sem("xgT_ps"), t * 2 + s + 3)
                    for g in range(2):
                        V.tensor_tensor(head3(xT[s][:, g * 512:(g + 1) * 512], P), head3(ps[2 * s + g][:, :], P),
                                        n2w[:, 4 * g:4 * g + 4].unsqueeze(2).broadcast_to([P, 4, P]), ALU.mult).then_inc(sem("xT_s"), 1)
                for s in range(2):
                    dve.wait_ge(sem("h_exp"), t * 2 + s + 1)
                    hx, hy = he[s][:, 0:FF], he[s][:, FF:2 * FF]
                    step(V.tensor_scalar(hx, hx, 1.0, None, ALU.add))
                    step(V.reciprocal(hx, hx))
                    step(V.tensor_tensor(hx, hx, ps[4 + s][:, 0:FF], ALU.mult))
                    V.tensor_tensor(hx, hx, ps[4 + s][:, FF:2 * FF], ALU.mult).then_inc(sem("he_ready"), 1)
                for s in range(2):
                    dve.wait_ge(sem("ye_ps"), t * 2 + s + 3)
                    dve.wait_ge(sem(f"ye_out{s}"), t * 16 + 16)
                    V.tensor_copy(ysb[s][:, 512:1024], ps[2 * s + 1][:, :]).then_inc(sem("ye_v"), 1)
                    dve.wait_ge(sem("ye_a"), t * 2 + s + 1)
                    dve.wait_ge(sem("ye_v"), t * 2 + s + 1)
                    dve.sem_inc(sem("xbank_free"), 2)
                assert ch.n == ch.per
            phase_end(dve, 2)

            dve.wait_ge(sem("fw"), 16)
            ch2 = Chain(dve, sem("dve_last"))
            for i in range(TILES):
                r = ROWS[i]
                xi = x1[0:r, i * D:(i + 1) * D]
                for c in range(2):
                    dve.wait_ge(sem(f"yg{c}{i % 2}"), 16 * (i // 2 + 1))
                a_, b_ = ya[i % 2][0:r, :], yb[i % 2][0:r, :]
                ch2.step(V.scalar_tensor_tensor(out=a_, in0=a_, scalar=gate1[0:r, i:i + 1], in1=xi, op0=ALU.mult, op1=ALU.add))
                ch2.wait()
                V.scalar_tensor_tensor(out=a_, in0=b_, scalar=gate2[0:r, i:i + 1], in1=a_, op0=ALU.mult, op1=ALU.add).then_inc(sem("x2_ready"), 1)
                dve.wait_ge(sem("ssf"), i + 1)
                dve.sem_inc(sem("yb_free"), 1)
                mean_eps(ss[0:r, i:i + 1], D).then_inc(sem("msf"), 1)
                dve.wait_ge(sem("rstdf"), i + 1)
                V.scalar_tensor_tensor(out=a_, in0=a_, scalar=rstd[0:r, i:i + 1], in1=fw[0:r, :], op0=ALU.mult, op1=ALU.mult).then_inc(sem("y_ready"), 1)



_INS = ['x_prompt', 'x_sample', 'cache_k', 'cache_v', 'state_hgrn', 'page_table', 'norm1_w', 'w_in', 'rel_bias',
        'lambda_q1', 'lambda_k1', 'lambda_q2', 'lambda_k2', 'da_subln_w', 'hg_lb_logits', 'hg_norm_w', 'w_out',
        'norm2_w', 'router_g_w', 'router_g_b', 'router_e_w', 'router_e_b', 'expert_w1', 'expert_w3', 'expert_w2',
        'final_norm_w']
_OUTS = [((1, SEQ, D), 'float32'), ((NB, NT, D), 'float32'), ((1, 1, SEQ, H, P), 'float32'), ((1, 1, SEQ, H, P), 'float32'),
         ((1, 1, H, P, P), 'float32'), ((1, NB, NT, H, P), 'float32'), ((1, NB, NT, H, P), 'float32'), ((1, NB, H, P, P), 'float32')]


def kernel(**inputs):
    import numpy as _np
    import concourse.bacc as _bacc
    from concourse import mybir as _mybir
    from concourse.bass_utils import run_bass_kernel_spmd as _run

    nc = _bacc.Bacc("TRN2", target_bir_lowering=False, num_devices=1)
    arrays, args = {}, []
    for name in _INS:
        a = _np.ascontiguousarray(inputs[name])
        arrays[f"in_{name}_dram"] = a
        args.append(nc.dram_tensor(f"in_{name}_dram", a.shape, _mybir.dt.from_np(a.dtype), kind="ExternalInput").ap())
    arrays["in_table_dram"] = TABLE
    args.append(nc.dram_tensor("in_table_dram", TABLE.shape, F32, kind="ExternalInput").ap())
    for i, (shape, dtype) in enumerate(_OUTS):
        dt = _mybir.dt.from_np(_np.dtype(dtype))
        args.append(nc.dram_tensor(f"out_{i}_dram", shape, dt, kind="ExternalOutput").ap())
    build(nc, *args)
    r = _run(nc, [arrays], core_ids=[0])
    return tuple(r.results[0][f"out_{i}_dram"] for i in range(len(_OUTS)))
```

```python
import math
from contextlib import ExitStack

import numpy as np
import concourse.bass as bass
from concourse import mybir

F32 = mybir.dt.float32
I32 = mybir.dt.int32
U32 = mybir.dt.uint32
ALU = mybir.AluOpType
ACT = mybir.ActivationFunctionType
AX = mybir.AxisListType.X
ds = bass.ds

P = 128
D = 1024
KC = D // P
SEQ = 1024
NB, NT = 8, 4
SMP = NB * NT
TOK = SEQ + SMP
TILES = SEQ // P + 1
ROWS = [P] * (SEQ // P) + [SMP]
H = 4
QK = 64
HW = H * P
PAGES = 32
COLS = H * 2 * NT
NE, NG, EG, FF = 16, 4, 4, 256
CAP = 32
PAIRS = CAP // 2
SURE = -(-(2 * TOK // P + 1) // 2) * 2
LEVELS = [64, 32, 16, 8, 4, 2, 1]
NLEV = len(LEVELS)
BUCKETS = 32
EPS = 1e-6
NEG = -1e30
LAM_INIT = 0.8 - 0.6 * math.exp(-0.3 * 0)

CP = {}


def constants():
    parts = []

    def put(name, a):
        full = np.zeros((P, a.shape[1]), np.float32)
        full[:a.shape[0]] = a
        CP[name] = (sum(x.shape[1] for x in parts), a.shape[1])
        parts.append(full)

    def bucket(n):
        n = np.maximum(n, 0)
        nf = np.maximum(n, 16).astype(np.float32)
        large = 16 + (np.log(nf / np.float32(16)) / np.float32(math.log(8.0)) * 16).astype(np.int32)
        return np.where(n < 16, n, np.minimum(large, 31))

    def onehot(dist):
        a = np.zeros((BUCKETS + 1, dist.size), np.float32)
        dist = dist.reshape(-1)
        ok = dist >= 0
        a[bucket(dist)[ok], np.nonzero(ok)[0]] = 1.0
        a[BUCKETS, ~ok] = NEG
        return a

    t = np.arange(P)
    put("ident", np.eye(P))
    put("tri", (t[:, None] < t[None, :]) * 1.0)
    lv = []
    for w in LEVELS:
        same = t[:, None] // (2 * w) == t[None, :] // (2 * w)
        lv.append(same & (t[:, None] % (2 * w) < w) & (t[None, :] % (2 * w) >= w))
    lv.append(t[:, None] == t[None, :])
    put("level", np.concatenate(lv, 1) * 1.0)
    put("own", (np.arange(SMP)[:, None] // NT == np.arange(NB)[None, :]) * 1.0)
    put("valid", (t[:, None] < SMP) * 1.0)
    put("iota", np.broadcast_to(np.arange(CAP)[None, :], (P, CAP)) * 1.0)
    row = np.arange(P)
    c32 = np.arange(COLS)
    put("rowsum", ((row[:, None] // 32 == c32[None, :] // 8) & (row[:, None] % 8 == c32[None, :] % 8)) * 1.0)
    c16 = np.arange(H * NT)
    same = (c32[:, None] // 8 == c16[None, :] // NT) & (c32[:, None] % NT == c16[None, :] % NT)
    put("map1", (same & (c32[:, None] // NT % 2 == 0)) * 1.0)
    put("map2", (same & (c32[:, None] // NT % 2 == 1)) * 1.0)
    put("head", (c32[:, None] // 8 == np.arange(H)[None, :]) * 1.0)
    put("iota128", np.broadcast_to(t[None, :], (P, P)) * 1.0)
    put("token", (t[:, None] + P * np.arange(TILES)[None, :]) * 1.0)
    small = sum(x.shape[1] for x in parts)
    put("oh_band", onehot(255 - np.arange(384)))
    return np.concatenate(parts, 1).astype(np.float32), small


TABLE, SMALL = constants()


class Chain:

    def __init__(self, eng, sem):
        self.eng, self.sem, self.n, self.base = eng, sem, 0, 0

    def step(self, ins):
        ins.then_inc(self.sem, 1)
        self.n += 1

    def wait(self):
        self.eng.wait_ge(self.sem, self.base + self.n)

    def enter(self, turn, per_turn):
        self.n0, self.per = self.n, per_turn
        self.base, self.n = turn * per_turn + self.n0, 0

    def leave(self, turns):
        assert self.n == self.per, (self.n, self.per)
        self.base, self.n = 0, self.n0 + turns * self.per


def build(nc, x_prompt, x_sample, cache_k, cache_v, state_hgrn, page_table,
          norm1_w, w_in, rel_bias, lambda_q1, lambda_k1, lambda_q2, lambda_k2,
          da_subln_w, hg_lb_logits, hg_norm_w, w_out, norm2_w,
          router_g_w, router_g_b, router_e_w, router_e_b,
          expert_w1, expert_w3, expert_w2, final_norm_w, table,
          y_prompt, y_sample, k_prompt, v_prompt, s_prompt, k_sample, v_sample, s_sample):

    band_d = nc.dram_tensor("band_scratch", (H * P, 384), F32, kind="Internal").ap()
    rows_d = nc.dram_tensor("rows_scratch", (TOK, D), F32, kind="Internal").ap()
    ye_d = nc.dram_tensor("expert_scratch", (CAP * P, D), F32, kind="Internal").ap()

    POOL = cache_k.shape[1]
    xp_v = x_prompt.rearrange("b (i p) d -> p (b i) d", p=P)
    xs_v = x_sample.rearrange("b t d -> (b t) d")
    win_v = w_in.rearrange("l (k p) n -> p (l k) n", p=P)
    wout_v = w_out.rearrange("l (k p) n -> p (l k) n", p=P)
    ck_v = cache_k.rearrange("l n p h d -> (l n p) (h d)")
    cv_v = cache_v.rearrange("l n p h d -> (l n p) (h d)")
    st_v = state_hgrn.rearrange("l b h k v -> (l h) k b v")
    so_v = s_sample.rearrange("l b h k v -> (l h) k b v")
    kp_v = k_prompt.rearrange("l b (i p) h d -> p (l b i) (h d)", p=P)
    vp_v = v_prompt.rearrange("l b (i p) h d -> p (l b i) (h d)", p=P)
    ks_v = k_sample.rearrange("l b t h d -> (l b t) (h d)")
    vs_v = v_sample.rearrange("l b t h d -> (l b t) (h d)")
    yp_v = y_prompt.rearrange("b (i p) d -> p (b i) d", p=P)
    ys_v = y_sample.rearrange("b t d -> (b t) d")
    w1_v = expert_w1.rearrange("l e d f -> (l e d) f")
    w3_v = expert_w3.rearrange("l e d f -> (l e d) f")
    w2_v = expert_w2.rearrange("l e f d -> (l e f) d")

    with ExitStack() as ctx:
        def sb(name, cols, dt=F32, rows=P):
            return ctx.enter_context(nc.sbuf_tensor(name, [rows, cols], dt))

        sems = {}
        part = [""]

        def sem(name):
            if name not in sems:
                sems[name] = nc.alloc_semaphore(name=name + part[0])
            return sems[name]

        arena = sb("arena", 8448 + 13056 + 21888 + 6144)
        at = [0]

        def take(cols, start=None):
            if start is None:
                start = at[0]
                at[0] += cols
            return arena[:, start:start + cols]

        A0 = 0
        hT = take(KC * TOK)
        B0 = at[0]
        qT, kT = take(H * TOK), take(H * TOK)
        v_nat = take(TILES * HW)
        C0 = at[0]
        hqT, gT, kkT = take(H * TOK), take(H * TOK), take(H * TOK)
        hi, gate = take(TILES * HW), take(TILES * HW)
        W0 = at[0]
        wring = [take(2048) for _ in range(2)]
        at[0] += 2048
        mixT = take(KC * TOK, A0)
        x_all = take(TILES * D, C0)
        KBUF = 4
        knat = [take(HW, W0 + 4096 + HW * i) for i in range(KBUF)]
        N0 = B0 + 2 * H * TOK
        X = [take(TOK, N0), take(TOK, N0 + TOK)]
        S = take(9 * P, N0 + 2 * TOK)
        Qpad = take(NB * SMP, N0 + 2 * TOK + 9 * P)
        ATs = take(SMP, N0 + 2 * TOK + 9 * P + NB * SMP)
        reset = take(TOK, N0 + 3552)
        AT = take(1024, W0 + 4096)
        KdN = take(1024, W0 + 5120)
        S0 = take(NB * P, N0 + 3552)
        band = take(H * 1152, C0)
        zp = [take(2048, C0 + 4608), take(2048, C0 + 6656)]
        pT = [take(1024, C0 + 8704), take(1024, C0 + 9728)]
        oN = take(H * SEQ, W0)
        osq_p = take(SEQ, W0 + H * SEQ)
        oh = take(384, N0)
        rowb = [take(384, N0 + 384 * (h + 1)) for h in range(H)]
        rbw = take(HW, N0 + 384 * (H + 1))
        R0 = C0 + 11264
        R1 = C0 + 12288
        ring = [take(HW, R1 + j * HW if j < 16 else B0 + (j - 16) * HW) for j in range(PAGES)]
        ring4 = [take(4 * HW, R1 + j * HW if j < 16 else B0 + (j - 16) * HW) for j in range(0, PAGES, 4)]
        kt = [take(8 * HW, a) for a in (C0, C0 + 8 * HW, C0 + 16 * HW, N0)]
        z = take(PAGES * 32 + SMP, W0)
        PT = take(9 * P, W0 + 1056)
        o_all = take(NB * P, W0 + 3232)
        qx, qcur, kn = take(HW, R1 + 16 * HW), take(HW, R1 + 17 * HW), take(HW, W0 + 5120)
        o_sel = take(P, W0 + 4768)
        o16 = take(NB * P, W0 + 2208)
        osq = take(NB * P, W0)
        vnew = v_nat[0:SMP, 8 * HW:9 * HW]
        wout = take(KC * D, R1)
        x1 = take(TILES * D, C0)
        xh = [take(D, B0), take(D, B0 + D)]
        h2T = [take(D, B0 + 2 * D), take(D, B0 + 3 * D)]
        M0 = B0 + 8 * D + 256
        sqj = take(D, M0)
        wslot = [take(6144, A0), take(6144, R0)]
        xg = [take(D, B0), take(D, B0 + D)]
        xT = [take(D, B0 + 2 * D), take(D, B0 + 3 * D)]
        he = [take(FF, B0 + 4 * D), take(FF, B0 + 4 * D + 256)]
        heT = [take(FF, B0 + 5 * D), take(FF, B0 + 5 * D + 256)]
        ysb = [take(D, B0 + 6 * D), take(D, B0 + 7 * D)]
        zero_rows = take(D, M0 + D)
        YBUF = 5
        ya = [take(D, B0 + i * D) for i in range(YBUF)]
        yb = [take(D, B0 + (YBUF + i) * D) for i in range(YBUF)]
        fw = take(D, B0 + 2 * YBUF * D)
        diag2 = take(TILES * P, W0)

        tab = sb("tab", SMALL)

        def cst(name, rows=P):
            a, n = CP[name]
            return tab[0:rows, a:a + n]

        ident = cst("ident")
        ones = sb("ones", P)[:, :]
        small = sb("small", 720)
        sat = [0]

        def sm(n, dt=F32):
            a = small[:, sat[0]:sat[0] + n]
            sat[0] += n
            return a if dt == F32 else a.bitcast(dt)

        n1w, n2w, lbT, omlb = sm(KC), sm(KC), sm(H), sm(H)
        lg0, lg1 = sm(H), sm(H)
        daw, hgw = sm(1), sm(1)
        ss, rstd = sm(TILES), sm(TILES)
        ss2, rstd2 = sm(TILES * H), sm(TILES * H)
        lamv, lamp, nlam = sm(4), sm(2), sm(1)
        rb = sm(H)
        farc, blast, bias4, biasn = sm(1), sm(SMP), sm(NT), sm(NB * SMP)
        att = sm(16)
        mxc, nmx, epsc = sm(1), sm(1), sm(1)
        nwt = sm(TILES * H)
        rs1 = sm(4)
        mall, m32 = sm(P), sm(COLS)
        sumc, sum_all, rsum = sm(1), sm(NB), sm(NB)
        comb = sm(H * NT)
        oms, orms = sm(NB), sm(NB)
        ptab = sb("ptab", NB * PAGES, I32, 1)
        rbias = sm(20)
        wr = sb("wr", KC * 20)
        route = sb("route", 624)
        rat = [0]

        def rt(n, dt=F32):
            a = route[:, rat[0]:rat[0] + n]
            rat[0] += n
            return a if dt == F32 else a.bitcast(dt)

        lgall, gpad = rt(TILES * 20), rt(TILES * 8)
        g8, gi, e8, ei = rt(8), rt(8, U32), rt(8), rt(8, U32)
        gidx, v12, i12 = rt(TILES), rt(TILES * 2), rt(TILES * 2)
        gate1, gate2, ptop = rt(TILES), rt(TILES), rt(TILES)
        gexp = rt(TILES * 4)
        slotf, slot_i, row_i, row_j = rt(2 * TILES), rt(2 * TILES, I32), rt(2 * TILES, I32), rt(2 * TILES, I32)
        cnt_i, ntl, endt, base = rt(NE, I32), rt(NE), rt(NE), rt(NE)
        eid_f, eid = rt(CAP), rt(CAP, I32)
        nit_i, more_i = rt(1, I32), rt(1, I32)
        idx_cur = rt(2, I32)
        ids = take(CAP, M0 + 2 * D).bitcast(I32)
        rowf, tilef = take(2 * TILES, M0 + 2 * D + 64), take(2 * TILES, M0 + 2 * D + 96)
        inrow = take(2 * TILES * P, W0 + TILES * P)
        intile = take(2 * TILES * CAP, W0 + 3 * TILES * P)
        lm = take(TILES * 16, M0 + 2 * D + 656)
        oh1, oh2, Mx, cum, rk = (take(TILES * 16, W0 + 4 * D + 144 * i) for i in range(5))
        cmp = take(CAP * 16, W0 + 4 * D + 720)

        ps = [ctx.enter_context(nc.psum_tensor(f"bank{i}", [P, 512], F32)) for i in range(8)]

        Q0, K0, V0, HQ0, HF0, HI0, GA0 = (i * HW for i in range(7))
        slots = []
        for kind, dst, c0 in (("T", hqT, HQ0), ("T", gT, HF0), ("N", hi, HI0),
                              ("T", qT, Q0), ("T", kT, K0), ("G", gate, GA0), ("N", v_nat, V0)):
            for half in range(2):
                slots.append((kind, dst, c0 + half * 256, half))
        items = []
        for s, (kind, dst, c0, half) in enumerate(slots):
            if kind == "T":
                items += [(s, kind, dst, half, c, n) for c in range(2) for n in range(3)]
            else:
                items += [(s, kind, dst, half, i, 0) for i in range(TILES)]
        N3 = TOK // 3
        upto = {"T": [0], "N": [0], "G": [0]}
        for it in items:
            for k in upto:
                upto[k].append(upto[k][-1] + (it[1] == k))

        G_MIX = sum(it[0] < 6 for it in items)
        G_VAL = sum(it[0] < 12 for it in items)

        SPOTS = [f"level{l}" for l in range(NLEV + 1)] + ["chunk1", "chunk5", "end"]
        spot_item, g = {}, G_MIX
        for h in range(H):
            for spot in SPOTS:
                if spot == "chunk5" and (G_VAL - G_MIX) - len(SPOTS) * H < h + 1 - H:
                    continue
                spot_item[(h, spot)] = g
                g += 1
        assert g == G_VAL

        def bank(g):
            return ps[g % 8] if g < G_MIX else ps[4 + g % 2] if g < G_VAL else ps[(g - G_VAL) % 6]

        def tok(t, c, i):
            return t[:, c * TOK + i * P:c * TOK + i * P + ROWS[i]]

        def head3(a, n, **kw):
            return a.rearrange("p (a b) -> p a b", b=n)

        NPH = [0]

        def phase_end(eng, k):
            eng.drain().then_inc(sem("phase"), 1)
            eng.wait_ge(sem("phase"), 5 * k)

        cumT, n = {}, 0
        for h in range(H):
            for i in range(8):
                for j in range(0, i + 1, 4):
                    n += 1
                    cumT[(h, i, j)] = n

        NV_TOTAL = 16 * 11
        block_a = nc.Block()
        block = block_a.__enter__()

        @block.sync
        def _(sp):
            for g in range(4):
                sp.dma_start(head3(x_all, D)[:, 2 * g:2 * g + 2, :],
                             xp_v[:, 2 * g:2 * g + 2, :]).then_inc(sem(f"x_in{g}"), 16)
            sp.dma_start(x_all[0:SMP, 8 * D:9 * D], xs_v).then_inc(sem("x_in4"), 16)
            sp.dma_start(oh, table[:, SMALL:]).then_inc(sem("oh_in"), 16)
            def weights(s):
                c0 = slots[s][2]
                if s >= 2:
                    sp.wait_ge(sem("proj"), sum(it[0] <= s - 2 for it in items))
                sp.dma_start(head3(wring[s % 2], 256), win_v[:, :, c0:c0 + 256]).then_inc(sem(f"w_in{s % 2}"), 16)

            for s in range(4):
                weights(s)
            for h in range(H):
                sp.wait_ge(sem("rowb"), h + 1)
                sp.dma_start(band_d[h * P:(h + 1) * P, :], rowb[h]).then_inc(sem("band_out"), 16)
            sp.wait_ge(sem("band_out"), 16 * H)
            for h in range(H):
                base_h = h * P * 384
                rows_h = slice(32 * h, 32 * h + 32)
                for q4 in range(4):
                    for m in range(2):
                        r4 = slice(32 * h + 8 * q4 + 4 * m, 32 * h + 8 * q4 + 4 * m + 4)
                        sp.dma_start(blast[r4, :], bass.AP(tensor=band_d.tensor, offset=base_h + 127 + 32 * q4, ap=[[383, NT], [1, SMP]])).then_inc(sem("dbias"), 16)
                        sp.dma_start(bias4[r4, :], bass.AP(tensor=band_d.tensor, offset=base_h + 255 + 40 * q4, ap=[[383, NT], [1, NT]])).then_inc(sem("dbias"), 16)
                with nc.allow_non_contiguous_dma("one value a partition"):
                    sp.dma_start(farc[rows_h, :], bass.AP(tensor=band_d.tensor, offset=base_h, ap=[[384, 32], [1, 1]])).then_inc(sem("dbias"), 16)
            for s in range(4, 8):
                weights(s)
            for h in range(H):
                if h:
                    sp.wait_ge(sem("snew_out"), 16 * h)
                else:
                    sp.wait_ge(sem("s0_free"), 1)
                if h == 2:
                    weights(10)
                sp.dma_start(head3(S0, P), st_v[h]).then_inc(sem("s0_in"), 16)
                weights((8, 9, 11, 12)[h])
                sp.wait_ge(sem("state_ready"), h + 1)
                sp.dma_start(s_prompt[0, 0, h], S[:, 8 * P:9 * P]).then_inc(sem("state_out"), 16)
                sp.wait_ge(sem("snew_ready"), h + 1)
                sp.dma_start(so_v[h], head3(S0, P)).then_inc(sem("snew_out"), 16)
            weights(13)
            sp.wait_ge(sem("snew_out"), 16 * H)
            sp.wait_ge(sem("state_out"), 16 * H)
            sp.sem_inc(sem("hgrn_out"), 2)
            sp.wait_ge(sem("o_ev"), 9 * H)
            for h in range(H):
                skew = bass.AP(tensor=band_d.tensor, offset=h * P * 384 + 127, ap=[[383, P], [1, 256]])
                sp.dma_start(band[:, h * 1152 + 896:(h + 1) * 1152], skew).then_inc(sem("band_in"), 16)
            for i in range(TILES):
                sp.wait_ge(sem("knat_ready"), i + 1)
                dst = ks_v if i == TILES - 1 else kp_v[:, i, :]
                sp.dma_start(dst, knat[i % KBUF][0:ROWS[i], :]).then_inc(sem(f"knat_out{i % KBUF}"), 16)
            sp.wait_ge(sem("ev_N"), upto["N"][-1])
            sp.dma_start(vp_v, head3(v_nat, HW)[:, 0:8, :]).then_inc(sem("out"), 16)
            sp.dma_start(vs_v, v_nat[0:SMP, 8 * HW:9 * HW]).then_inc(sem("out"), 16)
            for i in range(KBUF):
                sp.wait_ge(sem(f"knat_out{i}"), 16 * len(range(i, TILES, KBUF)))
            phase_end(sp, 1)
            sp.wait_ge(sem("ptab_in"), 16)

            def stream(b, view, free, put):
                for j in range(0, PAGES, 8):
                    _, numbers = nc.values_load_multi_w_load_instructions(
                        ptab[0:1, ds(b * PAGES + j, 8)], engines=[mybir.EngineType.SP], min_val=0, max_val=POOL - 1,
                        skip_runtime_bounds_check_because="the page table names pages of the pool")
                    for i, e in enumerate(numbers):
                        free(j + i)
                        put(j + i, view[ds(e * P, P), :])

            def keys(b, first=False):
                def free(j):
                    if first:
                        if j == 16:
                            sp.wait_ge(sem("prompt_done"), 1)
                        return
                    sp.wait_ge(sem("k_used"), b * PAGES - PAGES + j + 1)
                    if j % 4 == 0:
                        sp.sem_inc(sem("sp_held"), 1)
                        sp.wait_ge(sem("v_used"), b * PAGES - PAGES + j + 4)

                def put(j, src):
                    sp.dma_start(ring[j], src).then_inc(sem(f"pages{j // 4}"), 16)

                stream(b, ck_v, free, put)

            def values(b, last_one=False):
                def free(j):
                    if j % 4:
                        return
                    if last_one:
                        sp.wait_ge(sem("v_used"), b * PAGES + j + 4)
                    else:
                        sp.wait_ge(sem("k_used"), b * PAGES + PAGES + j + 4)

                def put(j, src):
                    q4 = j % 4
                    dst = ring4[j // 4][32 * q4:32 * q4 + 32, :].rearrange("p (i d) -> p i d", i=4)
                    sp.dma_start(dst, src.rearrange("(i b) d -> b i d", b=32)).then_inc(sem(f"pages{j // 4}"), 16)

                stream(b, cv_v, free, put)

            keys(0, True)
            with sp.Fori(0, NB - 1) as t:
                keys(t + 1)
                values(t)
            values(NB - 1, True)
            sp.wait_ge(sem("s_done"), NB)
            sp.dma_start(head3(x1, D)[:, 0:8, :], xp_v).then_inc(sem("wout_in"), 16)
            sp.dma_start(x1[0:SMP, 8 * D:9 * D], xs_v).then_inc(sem("wout_in"), 16)
            sp.wait_ge(sem("v_used"), PAGES + (NB - 1) * PAGES + 16)
            sp.dma_start(head3(wout, D), wout_v).then_inc(sem("wout_in"), 16)
            sp.wait_ge(sem("wout_in"), 48)
            sp.wait_ge(sem("out"), 32)
        @block.gpsimd
        def _(pool):
            nc.gpsimd.memset(ones[:, :], 1.0).then_inc(sem("ones"), 1)
            nc.gpsimd.memset(small[:, :], 1.0).then_inc(sem("small_ones"), 1)
            pool.wait_ge(sem("small_ones"), 1)
            nc.gpsimd.memset(epsc, EPS).then_inc(sem("small0"), 1)
            nc.gpsimd.memset(route[:, :], 0.0).then_inc(sem("route0"), 1)
            nc.gpsimd.memset(reset, 1.0).then_inc(sem("pool"), 1)
            pool.wait_ge(sem("pool"), 1)
            nc.gpsimd.memset(head3(reset[:, 0:SEQ], P)[:, :, 0:1], 0.0).then_inc(sem("pool"), 1)
            nc.gpsimd.memset(head3(reset[:, SEQ:TOK], NT)[:, :, 0:1], 0.0).then_inc(sem("pool"), 1)
            phase_end(pool, 1)
            nc.gpsimd.memset(qcur, 0.0).then_inc(sem("qx"), 1)
            for j in range(4):
                for i in range(4):
                    pool.wait_ge(sem("qx"), 5 * j + i + 1)
                    nc.gpsimd.tensor_copy(qx[32 * i:32 * i + 32, :].rearrange("p (b h j t) -> p h j b t", b=NB, h=H, j=4)[:, :, j, :, :],
                                          head3(qT[32 * j:32 * j + 32, :], TOK)[:, :, SEQ:TOK].rearrange("p h (b t) -> p h b t", t=NT)).then_inc(sem("qx"), 1)
                pool.wait_ge(sem("qx"), 5 * j + 5)
                nc.gpsimd.tensor_copy(kn[0:32, :].rearrange("p (h j w) -> p h j w", h=H, j=4)[:, :, j, :],
                                      head3(kT[32 * j:32 * j + 32, :], TOK)[:, :, SEQ:TOK]).then_inc(sem("qx"), 1)
        @block.scalar
        def _(act):
            ch = Chain(act, sem("act"))
            act.dma_start(tab[:, :], table[:, 0:SMALL]).then_inc(sem("tab"), 16)
            act.wait_ge(sem("small0"), 1)
            loads = [(n1w, norm1_w.rearrange("l (k p) -> p (l k)", p=P)),
                     (n2w, norm2_w.rearrange("l (k p) -> p (l k)", p=P)),
                     (lg0, hg_lb_logits[0:1].rearrange("a (h p) -> p (a h)", p=P)),
                     (lg1, hg_lb_logits[1:2].rearrange("a (h p) -> p (a h)", p=P)),
                     (daw, da_subln_w.rearrange("l p -> p l")),
                     (hgw, hg_norm_w.rearrange("l p -> p l")),
                     (lamv[0:QK, 0:1], lambda_q1.rearrange("l p -> p l")),
                     (lamv[0:QK, 1:2], lambda_q2.rearrange("l p -> p l")),
                     (lamv[0:QK, 2:3], lambda_k1.rearrange("l p -> p l")),
                     (lamv[0:QK, 3:4], lambda_k2.rearrange("l p -> p l")),
                     (rb[0:BUCKETS, :], rel_bias)]
            for dst, src in loads:
                with nc.allow_non_contiguous_dma("one column a partition"):
                    act.dma_start(dst, src).then_inc(sem("vecs"), 16)
            assert 16 * len(loads) == NV_TOTAL
            act.dma_start(ptab[:, :], page_table.rearrange("(a b) n -> a (b n)", a=1)).then_inc(sem("ptab_in"), 16)
            act.dma_start(rbias[:, 0:NG], router_g_b.broadcast_to([P, NG])).then_inc(sem("rw"), 16)
            act.dma_start(rbias[:, NG:20], router_e_b.broadcast_to([P, NE])).then_inc(sem("rw"), 16)
            wr3 = wr[:, :].rearrange("p (k n) -> p k n", n=20)
            act.dma_start(wr3[:, :, 0:NG], router_g_w.rearrange("l (k p) n -> p (l k) n", p=P)).then_inc(sem("rw"), 16)
            act.dma_start(wr3[:, :, NG:20], router_e_w.rearrange("l (k p) n -> p (l k) n", p=P)).then_inc(sem("rw"), 16)
            def tiles_of(g):
                return range(2 * g, min(2 * g + 2, TILES))

            def squares_of(g):
                act.wait_ge(sem(f"x_in{g}"), 16)
                for i in tiles_of(g):
                    r = ROWS[i]
                    ch.wait() if i else None
                    ch.step(nc.scalar.activation(take(D, W0 + 4 * D)[0:r, :], x_all[0:r, i * D:(i + 1) * D], ACT.Square,
                                                 accum_out=ss[0:r, i:i + 1]))
                ch.wait()
                c = slice(2 * g, tiles_of(g)[-1] + 1)
                nc.scalar.activation(rstd[0:r, c], ss[0:r, c], ACT.Sqrt, scale=1.0 / D, bias=epsc[0:r, :]).then_inc(sem("rms"), 1)

            def scale_tokens(g):
                act.wait_ge(sem("rstd"), g + 1)
                for i in tiles_of(g):
                    xi = x_all[0:ROWS[i], i * D:(i + 1) * D]
                    nc.scalar.activation(xi, xi, ACT.Copy, scale=rstd[0:ROWS[i], i:i + 1]).then_inc(sem("xn"), 1)

            squares_of(0)
            for g in range(5):
                if g < 4:
                    squares_of(g + 1)
                scale_tokens(g)
            def evacuate(g):
                s, kind, dst, half, c, n = items[g]
                act.wait_ge(sem("proj"), g + 1)
                if kind == "T":
                    col = (half * 2 + c) * TOK + n * N3
                    fn = ACT.Silu if dst is hqT else ACT.Sigmoid if dst is gT else ACT.Copy
                    nc.scalar.activation(dst[:, col:col + N3], bank(g)[:, 0:N3], fn,
                                         scale=QK ** -0.5 if dst is qT else 1.0).then_inc(sem("ev_T"), 1)
                else:
                    r = ROWS[c]
                    nc.scalar.activation(dst[0:r, c * HW + half * 256:c * HW + half * 256 + 256], bank(g)[0:r, 0:256],
                                         ACT.Copy).then_inc(sem("ev_G"), 1)

            act.wait_ge(sem("lam_ps"), 1)
            nc.scalar.activation(lamp, ps[3][:, 0:2], ACT.Exp).then_inc(sem("lam_e"), 1)
            act.wait_ge(sem("lbd"), 1)
            nc.scalar.activation(lbT, lg1, ACT.Sigmoid).then_inc(sem("lbe"), 1)
            for g in range(G_MIX):
                if items[g][1] == "T":
                    evacuate(g)
            for h in range(H):
                act.wait_ge(sem("f_ready"), h + 1)
                sl = slice(h * TOK, (h + 1) * TOK)
                nc.scalar.activation(gT[:, sl], gT[:, sl], ACT.Ln).then_inc(sem("lnf"), 1)
            def evacuate_spot(h, spot):
                if (h, spot) in spot_item:
                    evacuate(spot_item[(h, spot)])

            k = 0
            for h in range(H):
                for l in range(NLEV):
                    k += 1
                    act.wait_ge(sem("diff"), k)
                    n = TOK if LEVELS[l] < NT else SEQ
                    x = X[l % 2]
                    nc.scalar.activation(x[:, 0:n], x[:, 0:n], ACT.Exp).then_inc(sem("expd"), 1)
                    if l:
                        evacuate_spot(h, f"level{l - 1}")
                evacuate_spot(h, f"level{NLEV - 1}")
                act.wait_ge(sem("tails"), h + 1)
                sl = slice(h * TOK, (h + 1) * TOK)
                nc.scalar.activation(X[0], gT[:, sl], ACT.Exp).then_inc(sem("etail"), 1)
                nc.scalar.activation(X[1], X[1], ACT.Exp).then_inc(sem("etail"), 1)
                evacuate_spot(h, f"level{NLEV}")
                for c in range(2):
                    act.wait_ge(sem("kdn_ps"), 2 * h + c + 1)
                    nc.scalar.activation(KdN[:, c * 512:(c + 1) * 512], ps[2 + c][:, :], ACT.Copy).then_inc(sem("kdn"), 1)
                for c in range(8):
                    act.wait_ge(sem("o_ps"), 8 * h + c + 1)
                    nc.scalar.activation(hi[:, c * HW + h * P:c * HW + (h + 1) * P], ps[2 + c % 2][:, 0:P], ACT.Copy).then_inc(sem("o_ev"), 1)
                    evacuate_spot(h, f"chunk{c}")
                act.wait_ge(sem("os_ps"), h + 1)
                nc.scalar.activation(hi[0:SMP, 8 * HW + h * P:8 * HW + (h + 1) * P], ps[0][0:SMP, 0:P], ACT.Copy).then_inc(sem("o_ev"), 1)
                evacuate_spot(h, "end")
            act.wait_ge(sem("o_ev"), 9 * H)
            nc.scalar.activation(kkT[:, 0:4096], hi[:, 0:4096], ACT.Square).then_inc(sem("sq"), 1)
            nc.scalar.activation(gT[0:SMP, 1024:1536], hi[0:SMP, 4096:4608], ACT.Square).then_inc(sem("sq"), 1)
            act.wait_ge(sem("ev_G"), upto["G"][-1])
            nc.scalar.activation(gate[:, 0:4096], gate[:, 0:4096], ACT.Silu).then_inc(sem("gated"), 1)
            nc.scalar.activation(gate[0:SMP, 4096:4608], gate[0:SMP, 4096:4608], ACT.Silu).then_inc(sem("gated"), 1)
            act.wait_ge(sem("ms2"), 1)
            nc.scalar.activation(rstd2, ss2, ACT.Sqrt).then_inc(sem("rstd2"), 1)
            for i in range(TILES):
                act.wait_ge(sem("knat_ps"), i + 1)
                if i >= KBUF:
                    act.wait_ge(sem(f"knat_out{i % KBUF}"), 16 * (i // KBUF))
                nc.scalar.activation(knat[i % KBUF][0:ROWS[i], :], ps[6 + i % 2][0:ROWS[i], :], ACT.Copy).then_inc(sem("knat_ready"), 1)
            phase_end(act, 1)
            units = [(h, i) for h in range(H) for i in range(8)]

            def exps(n):
                h, i = units[n]
                for m in range(2):
                    act.wait_ge(sem("z_ready"), 2 * n + m + 1)
                    sl = slice(m * 1024, m * 1024 + (i + 1) * P)
                    a = att[:, 8 * (n % 2):8 * (n % 2) + 8]
                    nc.scalar.activation(zp[n % 2][:, sl], zp[n % 2][:, sl], ACT.Exp, bias=a[:, m:m + 1],
                                         accum_out=a[:, 2 + m:3 + m]).then_inc(sem("p_ready"), 1)

            def squares(h):
                act.wait_ge(sem("o_kept"), 8 * (h + 1))
                nc.scalar.activation(osq_p, oN[:, h * SEQ:(h + 1) * SEQ], ACT.Square).then_inc(sem("o_sq"), 1)

            def rms(h):
                act.wait_ge(sem("o_ms"), h + 1)
                nc.scalar.activation(rstd2[:, 0:8], ss2[:, 0:8], ACT.Sqrt).then_inc(sem("o_rms"), 1)

            exps(0)
            exps(1)
            for n, (h, i) in enumerate(units):
                for j in range(0, i + 1, 4):
                    act.wait_ge(sem("pT_ps"), cumT[(h, i, j)])
                    w = min(4, i + 1 - j) * P
                    nc.scalar.activation(pT[n % 2][:, j * P:j * P + w], ps[4 + (j // 4)][:, 0:w], ACT.Copy).then_inc(sem("pT"), 1)
                if n + 2 < len(units):
                    exps(n + 2)
                act.wait_ge(sem("oa_ps"), n + 1)
                nc.scalar.activation(oN[:, n * P:(n + 1) * P], ps[6][:, 0:P], ACT.Copy, scale=rs1[:, n % 4:n % 4 + 1]).then_inc(sem("o_kept"), 1)
                if h and i == 0:
                    squares(h - 1)
                if h and i == 1:
                    rms(h - 1)
            squares(H - 1)
            rms(H - 1)
            act.drain().then_inc(sem("prompt_left"), 1)

            def soft(b):
                act.wait_ge(sem("s_done"), b + 1)
                act.wait_ge(sem("z_free"), b + 1)
                nc.scalar.activation(z[:, 0:512], ps[0][:, :], ACT.Copy).then_inc(sem("z_act"), 1)
                act.wait_ge(sem("nmx"), b + 1)
                nc.scalar.activation(z, z, ACT.Exp, bias=nmx, accum_out=sumc).then_inc(sem("z_exp"), 1)

            def move_probs(b):
                for g in range(3):
                    act.wait_ge(sem("PT_ps"), b * 3 + g + 1)
                    n = 512 if g < 2 else P
                    r = P if g < 2 else SMP
                    o = PT[0:r, :].rearrange("p (i k c) -> p i k c", i=4, c=8)[:, :, g * 16:g * 16 + n // 32, :]
                    nc.scalar.activation(o, ps[3 + g % 2][0:r, 0:n].rearrange("p (k i c) -> p i k c", i=4, c=8), ACT.Copy).then_inc(sem("PT"), 1)

            act.wait_ge(sem("prompt_gone"), 1)
            soft(0)
            with act.Fori(0, NB - 1) as t:
                move_probs(t)
                soft(t + 1)
            move_probs(NB - 1)
            act.wait_ge(sem("rw"), 64)
        @block.tensor
        def _(pe):
            pe.wait_ge(sem("tab"), 16)
            pe.wait_ge(sem("ones"), 1)
            for i in range(TILES):
                r = ROWS[i]
                pe.wait_ge(sem("xn"), i + 1)
                if i >= 4:
                    pe.wait_ge(sem("hT"), i - 3)
                for k in range(KC):
                    b = ps[(2 * i + k // 4) % 8]
                    last_mm = nc.tensor.transpose(b[:, (k % 4) * P:(k % 4) * P + r], x_all[0:r, i * D + k * P:i * D + (k + 1) * P], ident[0:r, 0:r])
                last_mm.then_inc(sem("xT_ps"), 1)
            pe.wait_ge(sem("hT"), TILES)
            pe.wait_ge(sem("lam_in"), 1)
            nc.tensor.matmul(ps[3][:, 0:2], ones[0:QK, :], lamv[0:QK, 0:2], start=True, stop=True).then_inc(sem("lam_ps"), 1)
            pe.wait_ge(sem("oh_in"), 16)
            R = BUCKETS + 1
            for h in range(H):
                pe.wait_ge(sem("rbb"), h + 1)
                nc.tensor.matmul(ps[4 + h][:, 0:384], rbw[0:R, h * P:(h + 1) * P], oh[0:R, 0:384], start=True, stop=True).then_inc(sem("band_ps"), 1)
            def project(g):
                s, kind, dst, half, c, n = items[g]
                if g == 0 or items[g - 1][0] != s:
                    pe.wait_ge(sem(f"w_in{s % 2}"), 16 * (s // 2 + 1))
                first, banks = (0, 8) if g < G_MIX else (G_MIX, 2) if g < G_VAL else (G_VAL, 6)
                if g >= first + banks:
                    q = items[g - banks][1]
                    pe.wait_ge(sem(f"ev_{q}"), upto[q][g - banks + 1])
                if g == 3:
                    pe.wait_ge(sem("lam_e"), 1)
                if 4 <= g < 8:
                    pe.wait_ge(sem("rowb"), g - 3)
                w = head3(wring[s % 2], 256)
                for k in range(KC):
                    if kind == "T":
                        mm = nc.tensor.matmul(bank(g)[:, 0:N3], w[:, k, c * P:(c + 1) * P],
                                              hT[:, k * TOK + n * N3:k * TOK + (n + 1) * N3], start=(k == 0), stop=(k == KC - 1))
                    else:
                        mm = nc.tensor.matmul(bank(g)[0:ROWS[c], 0:256], tok(hT, k, c), w[:, k, :],
                                              start=(k == 0), stop=(k == KC - 1))
                mm.then_inc(sem("proj"), 1)

            def all_left(g):
                for q in ("T", "N", "G"):
                    pe.wait_ge(sem(f"ev_{q}"), upto[q][g])

            for g in range(G_MIX):
                project(g)
            all_left(G_MIX)
            def project_spot(h, spot):
                if (h, spot) in spot_item:
                    project(spot_item[(h, spot)])

            k = 0
            for h in range(H):
                if h:
                    pe.wait_ge(sem("o_ev"), 9 * h)
                for l in range(NLEV + 1):
                    if l < NLEV:
                        pe.wait_ge(sem("xl_ready"), NLEV * h + l + 1)
                    else:
                        pe.wait_ge(sem("q_ready"), H)
                    bb = 2 * (l % 2)
                    if k >= 2:
                        pe.wait_ge(sem("lev_ev"), k - 1)
                    for c in range(8):
                        if l == 0:
                            mm = nc.tensor.matmul(ps[bb + c // 4][0:64, (c % 4) * P + 64:(c % 4 + 1) * P],
                                                  X[0][:, c * P:c * P + 64], X[0][:, c * P + 64:(c + 1) * P], start=True, stop=True)
                            continue
                        if l < NLEV:
                            a = b_ = X[l % 2][:, c * P:(c + 1) * P]
                        else:
                            a = tok(kkT, h, c)
                            b_ = tok(hqT, h, c)
                        mm = nc.tensor.matmul(ps[bb + c // 4][:, (c % 4) * P:(c % 4 + 1) * P], a, b_, start=True, stop=True)
                    if l >= NLEV - 2:
                        a = X[l % 2][:, SEQ:TOK] if l < NLEV else tok(kkT, h, 8)
                        b_ = X[l % 2][:, SEQ:TOK] if l < NLEV else tok(hqT, h, 8)
                        mm = nc.tensor.matmul(ps[6 + l % 2][0:SMP, 0:SMP], a, b_, start=True, stop=True)
                    mm.then_inc(sem("lev_ps"), 1)
                    k += 1
                    project_spot(h, f"level{l}")
                pe.wait_ge(sem("kd_ready"), h + 1)
                pe.wait_ge(sem("lev_ev"), k)
                for c in range(9):
                    b = ps[2 + c // 4] if c < 8 else ps[1]
                    mm = nc.tensor.transpose(b[0:ROWS[c], (c % 4) * P:(c % 4 + 1) * P], tok(kkT, h, c), ident)
                    if c in (3, 7):
                        mm.then_inc(sem("kdn_ps"), 1)
                mm.then_inc(sem("kdns_ps"), 1)
                pe.wait_ge(sem("kdn"), 2 * h + 2)
                for c in range(8):
                    vv = hi[:, c * HW + h * P:c * HW + (h + 1) * P]
                    nc.tensor.matmul(ps[6 + c % 2][:, 0:P], KdN[:, c * P:(c + 1) * P], vv, start=True, stop=True).then_inc(sem("ds_ps"), 1)
                    if c >= 2:
                        pe.wait_ge(sem("o_ev"), 9 * h + c - 1)
                    nc.tensor.matmul(ps[2 + c % 2][:, 0:P], AT[:, c * P:(c + 1) * P], vv, start=True, stop=False)
                    pe.wait_ge(sem("state"), 9 * h + c + 1)
                    nc.tensor.matmul(ps[2 + c % 2][:, 0:P], tok(hqT, h, c), S[:, c * P:(c + 1) * P], start=False, stop=True).then_inc(sem("o_ps"), 1)
                    project_spot(h, f"chunk{c}")
                pe.wait_ge(sem("state"), 9 * h + 9)
                pe.wait_ge(sem("smp_ready"), h + 1)
                pe.wait_ge(sem("s0_in"), 16 * (h + 1))
                vs = hi[0:SMP, 8 * HW + h * P:8 * HW + (h + 1) * P]
                for b in range(NB):
                    mm = nc.tensor.matmul(ps[6 + b // 4][:, (b % 4) * P:(b % 4 + 1) * P], kkT[0:SMP, h * TOK + b * P:h * TOK + (b + 1) * P], vs, start=True, stop=True)
                mm.then_inc(sem("dss_ps"), 1)
                nc.tensor.matmul(ps[0][0:SMP, 0:P], ATs[0:SMP, :], vs, start=True, stop=False)
                for b in range(NB):
                    mm = nc.tensor.matmul(ps[0][0:SMP, 0:P], Qpad[:, b * SMP:(b + 1) * SMP], S0[:, b * P:(b + 1) * P], start=False, stop=(b == NB - 1))
                mm.then_inc(sem("os_ps"), 1)
                project_spot(h, "end")
            all_left(G_VAL)
            pe.wait_ge(sem("o_ev"), 9 * H)
            pe.wait_ge(sem("snew_ready"), H)
            def flip_new_keys(i):
                r = ROWS[i]
                if i >= 2:
                    pe.wait_ge(sem("knat_ready"), i - 1)
                for h in range(H):
                    mm = nc.tensor.transpose(ps[6 + i % 2][0:r, h * P:(h + 1) * P], tok(kT, h, i), ident)
                mm.then_inc(sem("knat_ps"), 1)

            for g in range(G_VAL, len(items)):
                project(g)
                if (g - G_VAL) % 2:
                    flip_new_keys((g - G_VAL) // 2)
            all_left(len(items))
            pe.wait_ge(sem("knat_ready"), TILES)
            pe.wait_ge(sem("og_ready"), 1)
            for i in range(TILES):
                if i >= 2:
                    pe.wait_ge(sem("og_ev"), i - 1)
                for h in range(H):
                    mm = nc.tensor.transpose(ps[i % 2][:, h * P:h * P + ROWS[i]], hi[0:ROWS[i], i * HW + h * P:i * HW + (h + 1) * P], ident[0:ROWS[i], 0:ROWS[i]])
                mm.then_inc(sem("og_ps"), 1)
            phase_end(pe, 1)
            pe.sem_inc(sem("v_used"), PAGES)
            units = [(h, i) for h in range(H) for i in range(8)]

            def scores(n):
                h, i = units[n]
                for m in range(2):
                    if n:
                        pe.wait_ge(sem("z_sum"), 2 * n + m - 1)
                    rows = slice(QK * m, QK * m + QK)
                    for j in range(0, i + 1, 4):
                        w = min(4, i + 1 - j) * P
                        mm = nc.tensor.matmul(ps[2 * m + j // 4][:, 0:w], qT[rows, h * TOK + i * P:h * TOK + (i + 1) * P],
                                              kT[rows, h * TOK + j * P:h * TOK + j * P + w], start=True, stop=True)
                    mm.then_inc(sem("s_ps"), 1)

            def flip(n):
                h, i = units[n]
                pe.wait_ge(sem("a_ready"), n + 1)
                for j in range(i + 1):
                    mm = nc.tensor.transpose(ps[4 + j // 4][:, (j % 4) * P:(j % 4 + 1) * P], zp[n % 2][:, j * P:(j + 1) * P], ident)
                    if j % 4 == 3 or j == i:
                        mm.then_inc(sem("pT_ps"), 1)

            def weigh(n):
                h, i = units[n]
                if n:
                    pe.wait_ge(sem("o_kept"), n)
                for j in range(i + 1):
                    if j % 4 == 0:
                        pe.wait_ge(sem("pT"), cumT[(h, i, j)])
                    mm = nc.tensor.matmul(ps[6][:, 0:P], pT[n % 2][:, j * P:(j + 1) * P], v_nat[:, j * HW + h * P:j * HW + (h + 1) * P],
                                          start=(j == 0), stop=(j == i))
                mm.then_inc(sem("oa_ps"), 1)

            def turn(h, half):
                pe.wait_ge(sem("o_norm"), h + 1)
                if h or half:
                    pe.wait_ge(sem("mix_ev"), 2 * h + half)
                for c in range(4):
                    n = 8 * h + 4 * half + c
                    mm = nc.tensor.transpose(ps[7][:, c * P:(c + 1) * P], oN[:, n * P:(n + 1) * P], ident)
                mm.then_inc(sem("ot_ps"), 1)

            scores(0)
            scores(1)
            for n, (h, i) in enumerate(units):
                flip(n)
                if n + 2 < len(units):
                    scores(n + 2)
                weigh(n)
                if h and i in (3, 4):
                    turn(h - 1, i - 3)
            turn(H - 1, 0)
            turn(H - 1, 1)
            pe.wait_ge(sem("prompt_gone"), 1)

            pe.sem_inc(sem("kt_used"), 4)
            pe.wait_ge(sem("kn_ready"), 1)

            def keys(b):
                pe.wait_ge(sem("qcur"), b * 8 + 8)
                pe.wait_ge(sem("s_free"), b + 1)
                q = qcur
                for g in range(4):
                    pe.wait_ge(sem("k_used"), b * PAGES + 8 * g + 8)
                    k8 = kt[g].rearrange("p (n c w) -> p n c w", n=8, w=32)
                    for h in range(H):
                        for j in range(4):
                            c = h * 4 + j
                            mm = nc.tensor.matmul(ps[g // 2][32 * h:32 * h + 32, (g % 2) * 256:(g % 2) * 256 + 256],
                                                  q[:, c * 32:(c + 1) * 32], k8[:, :, c, :], start=(j == 0), stop=(j == 3))
                    mm.then_inc(sem("kt_used"), 1)
                for h in range(H):
                    for j in range(4):
                        c = h * 4 + j
                        mm = nc.tensor.matmul(ps[2][32 * h:32 * h + 32, 0:SMP], q[0:32, c * 32:(c + 1) * 32], kn[0:32, c * 32:(c + 1) * 32],
                                              start=(j == 0), stop=(j == 3))
                mm.then_inc(sem("s_done"), 1)

            def flip(b):
                pe.wait_ge(sem("z_exp"), b + 1)
                for g in range(9):
                    if g == 8:
                        pe.wait_ge(sem("PT"), b * 3 + 1)
                    n = P if g < 8 else SMP
                    mm = nc.tensor.transpose(ps[3 + g // 4 % 2][0:n, (g % 4) * P:(g % 4 + 1) * P], z[:, g * P:g * P + n], ident)
                    if g in (3, 7, 8):
                        mm.then_inc(sem("PT_ps"), 1)

            def values(b, k0, maxima=False):
                pe.wait_ge(sem("o_free"), b + 1)
                for g in range(8):
                    pe.wait_ge(sem("PT"), b * 3 + g // 4 + 1)
                    pe.wait_ge(sem(f"pages{g}"), k0)
                    if maxima and g == 2:
                        top_rows(b + 1)
                    if maxima and g == 3:
                        top_columns(b + 1)
                    for i in range(4):
                        lhs = PT[:, (i * 9 + g) * COLS:(i * 9 + g + 1) * COLS]
                        mm = nc.tensor.matmul(ps[5][0:COLS, :], lhs, ring4[g][:, i * HW:(i + 1) * HW],
                                              start=(g == 0 and i == 0), stop=False)
                    mm.then_inc(sem("v_groups"), 1)
                    pe.wait_ge(sem("v_groups"), b * 8 + g + 1)
                    pe.sem_inc(sem("v_used"), 4)
                pe.wait_ge(sem("PT"), b * 3 + 3)
                pe.sem_inc(sem("pe_held"), 1)
                lhs = PT[0:SMP, 8 * COLS:9 * COLS]
                nc.tensor.matmul(ps[5][0:COLS, :], lhs, vnew, start=False, stop=True).then_inc(sem("pv"), 1)

            def top_rows(b):
                pe.wait_ge(sem("mxc"), b + 1)
                nc.tensor.transpose(ps[6][0:1, 0:P], mxc, ident).then_inc(sem("mx_ps"), 1)

            def top_columns(b):
                pe.wait_ge(sem("mall"), b + 1)
                nc.tensor.matmul(ps[7][:, 0:1], mall[0:1, :], ones[0:1, 0:1], start=True, stop=True).then_inc(sem("mb_ps"), 1)

            keys(0)
            top_rows(0)
            top_columns(0)
            flip(0)
            with pe.Fori(0, NB - 1) as t:
                keys(t + 1)
                values(t, t * 128 + 192, True)
                flip(t + 1)
            values(NB - 1, 64 * 2 * NB)
        @block.vector
        def _(dve):
            V = nc.vector
            ch = Chain(dve, sem("dve"))

            def step(ins):
                ch.step(ins)
                ch.wait()

            def mean_eps(a, n):
                return V.tensor_scalar(a, a, 1.0 / n, EPS, ALU.mult, ALU.add)

            def inverse(r, v, chain=None):
                c = chain or ch
                t = nwt[0:r.shape[0], 0:r.shape[1]]
                for ins in (lambda: V.reciprocal(r, r),
                            lambda: V.tensor_tensor(t, r, r, ALU.mult),
                            lambda: V.scalar_tensor_tensor(out=t, in0=t, scalar=-0.5, in1=v, op0=ALU.mult, op1=ALU.mult),
                            lambda: V.scalar_tensor_tensor(out=r, in0=t, scalar=1.5, in1=r, op0=ALU.add, op1=ALU.mult)):
                    c.step(ins())
                    c.wait()

            def inverse_of(g):
                dve.wait_ge(sem("rms"), g + 1)
                c = slice(2 * g, min(2 * g + 2, TILES))
                r = ROWS[2 * g]
                ch.step(mean_eps(ss[0:r, c], D))
                inverse(rstd[0:r, c], ss[0:r, c])
                dve.sem_inc(sem("rstd"), 1)

            inverse_of(0)
            inverse_of(1)
            dve.wait_ge(sem("small0"), 1)
            dve.wait_ge(sem("vecs"), NV_TOTAL)
            step(V.tensor_tensor(lamv[0:QK, 0:2], lamv[0:QK, 0:2], lamv[0:QK, 2:4], ALU.mult))
            dve.sem_inc(sem("lam_in"), 1)
            for h in range(H):
                V.tensor_copy(rbw[0:BUCKETS + 1, h * P:(h + 1) * P], rb[0:BUCKETS + 1, h:h + 1].broadcast_to([BUCKETS + 1, P])).then_inc(sem("rbb"), 1)
            for i in range(TILES):
                r = ROWS[i]
                if i % 2 == 0 and i // 2 + 2 < 5:
                    inverse_of(i // 2 + 2)
                dve.wait_ge(sem("xT_ps"), i + 1)
                for g in range(2):
                    o = head3(hT, TOK)[:, 4 * g:4 * g + 4, i * P:i * P + r]
                    last = V.tensor_tensor(o, head3(ps[(2 * i + g) % 8][:, :], P)[:, :, 0:r],
                                           n1w[:, 4 * g:4 * g + 4].unsqueeze(2).broadcast_to([P, 4, r]), ALU.mult)
                last.then_inc(sem("hT"), 1)
            for h in range(H):
                dve.wait_ge(sem("band_ps"), h + 1)
                V.tensor_copy(rowb[h], ps[4 + h][:, 0:384]).then_inc(sem("rowb"), 1)
            dve.wait_ge(sem("lam_e"), 1)
            step(V.tensor_tensor(nlam, lamp[:, 1:2], lamp[:, 0:1], ALU.subtract))
            step(V.tensor_scalar(nlam, nlam, -LAM_INIT, None, ALU.add))
            step(V.tensor_scalar(daw, daw, 1.0 - LAM_INIT, None, ALU.mult))
            step(V.scalar_tensor_tensor(out=comb[0:COLS, :], in0=cst("map2", COLS), scalar=nlam[0:COLS, :], in1=cst("map1", COLS), op0=ALU.mult, op1=ALU.add))
            V.tensor_tensor(lg1, lg0, lg1, ALU.subtract).then_inc(sem("lbd"), 1)
            dve.wait_ge(sem("lbe"), 1)
            step(V.tensor_scalar(omlb, lbT, -1.0, 1.0, ALU.mult, ALU.add))
            for h in range(H):
                sl = slice(h * TOK, (h + 1) * TOK)
                g, q, kk = gT[:, sl], hqT[:, sl], kkT[:, sl]
                dve.wait_ge(sem("ev_T"), 3 * (H + h + 1))
                step(V.tensor_scalar(g, g, omlb[:, h:h + 1], lbT[:, h:h + 1], ALU.mult, ALU.add))
                V.tensor_scalar(kk, g, -1.0, 1.0, ALU.mult, ALU.add).then_inc(sem("f_ready"), 1)
                V.tensor_scalar(q, q, P ** -0.5, None, ALU.mult).then_inc(sem("q_ready"), 1)
            dve.wait_ge(sem("pool"), 3)
            for h in range(H):
                g = gT[:, h * TOK:(h + 1) * TOK]
                dve.wait_ge(sem("lnf"), h + 1)
                ch.step(V.tensor_tensor_scan(g, reset, g, 0.0, ALU.mult, ALU.add))

            ch.wait()
            dve.sem_inc(sem("s0_free"), 1)

            def evacuate(g):
                s, kind, dst, half, c, n = items[g]
                dve.wait_ge(sem("proj"), g + 1)
                r = ROWS[c]
                V.tensor_copy(dst[0:r, c * HW + half * 256:c * HW + half * 256 + 256], bank(g)[0:r, 0:256]).then_inc(sem("ev_N"), 1)

            for g in range(G_MIX):
                if items[g][1] == "N":
                    evacuate(g)

            dve.wait_ge(sem("dbias"), 16 * (16 * 4 + H))
            step(V.tensor_scalar(blast, blast, farc, None, ALU.subtract))
            step(V.tensor_scalar(bias4, bias4, farc, None, ALU.subtract))
            step(V.memset(biasn, NEG))
            step(V.tensor_copy(bass.AP(tensor=biasn.tensor, offset=biasn.offset, ap=[list(biasn.ap[0]), [SMP + NT, NB], [1, NT]]),
                               bias4.unsqueeze(1).broadcast_to([P, NB, NT])))

            dve.wait_ge(sem("q_ready"), H)
            dve.wait_ge(sem("f_ready"), H)
            ch.wait()
            k = 0
            lev = cst("level").bitcast(I32)
            for h in range(H):
                sl = slice(h * TOK, (h + 1) * TOK)
                g, q, kk = gT[:, sl], hqT[:, sl], kkT[:, sl]

                def diff(l):
                    w = LEVELS[l]
                    n = TOK if w < NT else SEQ
                    gg = g[:, 0:n].rearrange("p (b w) -> p b w", w=2 * w)
                    xx = X[l % 2][:, 0:n].rearrange("p (b w) -> p b w", w=2 * w)
                    mid = gg[:, :, w - 1:w].broadcast_to([P, n // (2 * w), w])
                    if l >= 2:
                        dve.wait_ge(sem("lev_ps"), k0 + l - 1)
                    V.tensor_tensor(xx[:, :, 0:w], mid, gg[:, :, 0:w], ALU.subtract)
                    V.tensor_tensor(xx[:, :, w:2 * w], gg[:, :, w:2 * w], mid, ALU.subtract).then_inc(sem("diff"), 1)

                def scale(l):
                    w = LEVELS[l]
                    n = TOK if w < NT else SEQ
                    dve.wait_ge(sem("expd"), NLEV * h + l + 1)
                    xx = X[l % 2][:, 0:n].rearrange("p (b w) -> p b w", w=2 * w)
                    V.tensor_tensor(xx[:, :, 0:w], xx[:, :, 0:w], kk[:, 0:n].rearrange("p (b w) -> p b w", w=2 * w)[:, :, 0:w], ALU.mult)
                    V.tensor_tensor(xx[:, :, w:2 * w], xx[:, :, w:2 * w], q[:, 0:n].rearrange("p (b w) -> p b w", w=2 * w)[:, :, w:2 * w], ALU.mult).then_inc(sem("xl_ready"), 1)

                def collect(l):
                    dve.wait_ge(sem("lev_ps"), k0 + l + 1)
                    if l:
                        dve.wait_ge(sem("lev_ev"), k0 + l)
                    for c in range(2):
                        if l == 0:
                            last = V.tensor_copy(head3(AT[0:64, c * 512:(c + 1) * 512], P)[:, :, 64:P], head3(ps[c][0:64, :], P)[:, :, 64:P])
                            continue
                        last = V.copy_predicated(AT[:, c * 512:(c + 1) * 512].rearrange("p (a b) -> p a b", b=P),
                                                 lev[:, l * P:(l + 1) * P].unsqueeze(1).broadcast_to([P, 4, P]),
                                                 ps[2 * (l % 2) + c][:, :].rearrange("p (a b) -> p a b", b=P))
                    if l >= NLEV - 2:
                        last = V.copy_predicated(ATs[0:SMP, :], lev[0:SMP, l * P:l * P + SMP], ps[6 + l % 2][0:SMP, 0:SMP])
                    last.then_inc(sem("lev_ev"), 1)

                k0 = (NLEV + 1) * h
                diff(0)
                diff(1)
                if h:
                    dve.wait_ge(sem("o_ps"), 8 * h)
                    dve.wait_ge(sem("os_ps"), h)
                ch.step(V.memset(AT, 0.0))
                ch.step(V.memset(ATs, 0.0))
                ch.step(V.memset(Qpad, 0.0))
                ch.wait()
                scale(0)
                for l in range(NLEV):
                    if l + 1 < NLEV:
                        scale(l + 1)
                    collect(l)
                    if l + 2 < NLEV:
                        diff(l + 2)
                collect(NLEV)
                k += NLEV + 1
                gp, gs = head3(g[:, 0:SEQ], P), head3(g[:, SEQ:TOK], NT)
                x1p, x1s = head3(X[1][:, 0:SEQ], P), head3(X[1][:, SEQ:TOK], NT)
                V.tensor_tensor(x1p, gp[:, :, P - 1:P].broadcast_to([P, 8, P]), gp, ALU.subtract)
                V.tensor_tensor(x1s, gs[:, :, NT - 1:NT].broadcast_to([P, NB, NT]), gs, ALU.subtract).then_inc(sem("tails"), 1)
                dve.wait_ge(sem("etail"), 2 * h + 2)
                V.tensor_tensor(kk, kk, X[1], ALU.mult).then_inc(sem("kd_ready"), 1)
                step(V.tensor_tensor(q, q, X[0], ALU.mult))
                step(V.tensor_copy(bass.AP(tensor=Qpad.tensor, offset=Qpad.offset, ap=[list(Qpad.ap[0]), [SMP + NT, NB], [1, NT]]),
                                   head3(q[:, SEQ:TOK], NT)))
                if h:
                    dve.wait_ge(sem("state_out"), 16 * h)
                step(V.memset(S[:, 0:P], 0.0))
                dve.sem_inc(sem("state"), 1)
                dve.wait_ge(sem("kdns_ps"), h + 1)
                for b in range(NB):
                    ch.step(V.tensor_scalar(kkT[0:SMP, h * TOK + b * P:h * TOK + (b + 1) * P], ps[1][0:SMP, 0:P], cst("own", SMP)[:, b:b + 1], None, ALU.mult))
                ch.wait()
                dve.sem_inc(sem("smp_ready"), 1)
                for c in range(8):
                    dve.wait_ge(sem("ds_ps"), 8 * h + c + 1)
                    V.scalar_tensor_tensor(out=S[:, (c + 1) * P:(c + 2) * P], in0=S[:, c * P:(c + 1) * P],
                                           scalar=X[0][:, c * P + P - 1:c * P + P], in1=ps[6 + c % 2][:, 0:P],
                                           op0=ALU.mult, op1=ALU.add).then_inc(sem("state"), 1)
                    dve.wait_ge(sem("state"), 9 * h + c + 2)
                dve.sem_inc(sem("state_ready"), 1)
                dve.wait_ge(sem("dss_ps"), h + 1)
                dve.wait_ge(sem("os_ps"), h + 1)
                for b in range(NB):
                    c = SEQ + b * NT + NT - 1
                    ch.step(V.scalar_tensor_tensor(out=S0[:, b * P:(b + 1) * P], in0=S0[:, b * P:(b + 1) * P], scalar=X[0][:, c:c + 1],
                                                   in1=ps[6 + b // 4][:, (b % 4) * P:(b % 4 + 1) * P], op0=ALU.mult, op1=ALU.add))
                ch.wait()
                dve.sem_inc(sem("snew_ready"), 1)
            dve.wait_ge(sem("sq"), 2)
            step(V.memset(ss2, 1.0))
            step(V.tensor_reduce(ss2[:, 0:32], head3(kkT[:, 0:4096], P), AX, ALU.add))
            step(V.tensor_reduce(ss2[0:SMP, 32:36], head3(gT[0:SMP, 1024:1536], P), AX, ALU.add))
            mean_eps(ss2, P).then_inc(sem("ms2"), 1)
            dve.wait_ge(sem("rstd2"), 1)
            inverse(rstd2, ss2)
            for o, r2, e in ((hi[:, 0:4096], rstd2[:, 0:32], gate[:, 0:4096]), (hi[0:SMP, 4096:4608], rstd2[0:SMP, 32:36], gate[0:SMP, 4096:4608])):
                n = r2.shape[1]
                step(V.tensor_tensor(head3(o, P), head3(o, P), r2.unsqueeze(2).broadcast_to([o.shape[0], n, P]), ALU.mult))
                dve.wait_ge(sem("gated"), 2)
                step(V.tensor_tensor(o, o, e, ALU.mult))
            dve.sem_inc(sem("og_ready"), 1)
            dve.wait_ge(sem("hgrn_out"), 2)
            for g in range(G_VAL, len(items)):
                evacuate(g)
            dve.wait_ge(sem("band_in"), 16 * H)
            for h in range(H):
                ch.step(V.tensor_copy(band[:, h * 1152:h * 1152 + 896], band[:, h * 1152 + 896:h * 1152 + 897].broadcast_to([P, 896])))
            for i in range(TILES):
                dve.wait_ge(sem("og_ps"), i + 1)
                r = ROWS[i]
                V.tensor_scalar(head3(mixT, TOK)[:, 4:8, i * P:i * P + r], head3(ps[i % 2][:, :], P)[:, :, 0:r], hgw, None, ALU.mult).then_inc(sem("og_ev"), 1)
            phase_end(dve, 1)

            units = [(h, i) for h in range(H) for i in range(8)]

            def bias_max(n):
                h, i = units[n]
                w = (i + 1) * P
                a = att[:, 8 * (n % 2):8 * (n % 2) + 8]
                for m in range(2):
                    dve.wait_ge(sem("s_ps"), 2 * n + m + 1)
                    top = a[:, 6 + m:7 + m]
                    for j in range(0, i + 1, 4):
                        ww = min(4, i + 1 - j) * P
                        if j:
                            ch.wait()
                        last = V.tensor_tensor_reduce(out=zp[n % 2][:, m * 1024 + j * P:m * 1024 + j * P + ww], in0=ps[2 * m + j // 4][:, 0:ww],
                                                      in1=band[:, h * 1152 + 1152 - w + j * P:h * 1152 + 1152 - w + j * P + ww],
                                                      scale=1.0, scalar=top if j else -3e38, op0=ALU.add, op1=ALU.max, accum_out=top)
                        if j + 4 <= i:
                            ch.step(last)
                    last.then_inc(sem("z_sum"), 1)
                    dve.wait_ge(sem("z_sum"), 2 * n + m + 1)
                    V.tensor_scalar(a[:, m:m + 1], top, -1.0, None, ALU.mult).then_inc(sem("z_ready"), 1)

            def combine(n):
                h, i = units[n]
                w = (i + 1) * P
                a = att[:, 8 * (n % 2):8 * (n % 2) + 8]
                zb = zp[n % 2]
                dve.wait_ge(sem("p_ready"), 2 * n + 2)
                step(V.reciprocal(a[:, 4:5], a[:, 3:4]))
                ch.step(V.reciprocal(rs1[:, n % 4:n % 4 + 1], a[:, 2:3]))
                step(V.scalar_tensor_tensor(out=a[:, 5:6], in0=a[:, 4:5], scalar=nlam, in1=a[:, 2:3], op0=ALU.mult, op1=ALU.mult))
                V.scalar_tensor_tensor(out=zb[:, 0:w], in0=zb[:, 1024:1024 + w], scalar=a[:, 5:6], in1=zb[:, 0:w],
                                       op0=ALU.mult, op1=ALU.add).then_inc(sem("a_ready"), 1)

            def mean_square(h):
                dve.wait_ge(sem("o_sq"), h + 1)
                step(V.tensor_reduce(ss2[:, 0:8], head3(osq_p, P), AX, ALU.add))
                mean_eps(ss2[:, 0:8], P).then_inc(sem("o_ms"), 1)

            def normalise(h):
                dve.wait_ge(sem("o_rms"), h + 1)
                inverse(rstd2[:, 0:8], ss2[:, 0:8])
                o = head3(oN[:, h * SEQ:(h + 1) * SEQ], P)
                V.tensor_tensor(o, o, rstd2[:, 0:8].unsqueeze(2).broadcast_to([P, 8, P]), ALU.mult).then_inc(sem("o_norm"), 1)

            def place(h, half):
                dve.wait_ge(sem("ot_ps"), 2 * h + half + 1)
                V.tensor_scalar(mixT[:, h * TOK + half * 512:h * TOK + half * 512 + 512], ps[7][:, :], daw, None, ALU.mult).then_inc(sem("mix_ev"), 1)

            bias_max(0)
            combine(0)
            bias_max(1)
            for n, (h, i) in enumerate(units):
                if n + 1 < len(units):
                    combine(n + 1)
                if n + 2 < len(units):
                    bias_max(n + 2)
                if h and i == 1:
                    mean_square(h - 1)
                if h and i == 2:
                    normalise(h - 1)
                if h and i in (3, 4):
                    place(h - 1, i - 3)
            mean_square(H - 1)
            normalise(H - 1)
            place(H - 1, 0)
            place(H - 1, 1)
            dve.wait_ge(sem("prompt_left"), 1)
            dve.wait_ge(sem("mix_ev"), 2 * H)
            dve.sem_inc(sem("prompt_gone"), 2)

            dve.wait_ge(sem("qx"), 21)
            dve.sem_inc(sem("kn_ready"), 1)
            dve.sem_inc(sem("prompt_done"), 1)
            dve.sem_inc(sem("s_free"), 1)
            dve.sem_inc(sem("z_free"), 1)
            dve.sem_inc(sem("o_free"), 1)

            def set_queries(b):
                dve.wait_ge(sem("s_done0"), b + 1)
                for i in range(4):
                    for m in range(2):
                        src = (qx[32 * i:32 * i + 32, ds(b * 64, 64)] if not isinstance(b, int) else qx[32 * i:32 * i + 32, b * 64:b * 64 + 64])
                        V.tensor_scalar(qcur[32 * i:32 * i + 32, :].rearrange("p (h j i m t) -> p h j i m t", h=H, j=4, i=4, m=2)[:, :, 2 * m:2 * m + 2, i, m, :],
                                        src.rearrange("p (h j t) -> p h j t", h=H, j=4)[:, :, 2 * m:2 * m + 2, :], 1.0, None, ALU.mult).then_inc(sem("qcur"), 1)

            def flip_keys(b):
                for j in range(PAGES):
                    if j % 8 == 0:
                        dve.wait_ge(sem("kt_used"), b * 4 + j // 8 + 1)
                    if j % 4 == 0:
                        dve.wait_ge(sem(f"pages{j // 4}"), 64 if isinstance(b, int) and b == 0 else b * 128)
                    V.transpose(kt[j // 8][:, (j % 8) * HW:(j % 8 + 1) * HW], ring[j]).then_inc(sem("k_used"), 1)

            def take_scores(b):
                dve.wait_ge(sem("s_done"), b + 1)
                dve.wait_ge(sem("z_free"), b + 1)
                ch.step(V.tensor_copy(z[:, 512:992], ps[1][:, 0:480]))
                ch.step(V.tensor_tensor(z[:, 992:1024], ps[1][:, 480:512], blast, ALU.add))
                bn = biasn[:, ds(b * SMP, SMP)] if not isinstance(b, int) else biasn[:, b * SMP:(b + 1) * SMP]
                ch.step(V.tensor_tensor(z[:, 1024:1056], ps[2][:, 0:SMP], bn, ALU.add))
                ch.wait()
                dve.wait_ge(sem("z_act"), b + 1)
                dve.sem_inc(sem("s_free"), 1)
                dve.sem_inc(sem("s_done0"), 1)
                V.tensor_reduce(mxc, z, AX, ALU.max).then_inc(sem("mxc"), 1)
                dve.wait_ge(sem("mx_ps"), b + 1)
                ch.step(V.tensor_reduce(m32[0:1, :].rearrange("p (h c) -> p h c", h=H), ps[6][0:1, 0:P].rearrange("p (h i c) -> p h c i", h=H, i=4), AX, ALU.max))
                ch.wait()
                V.tensor_copy(mall[0:1, :].rearrange("p (h i c) -> p h i c", h=H, i=4),
                              m32[0:1, :].rearrange("p (h c) -> p h c", h=H).unsqueeze(2).broadcast_to([1, H, 4, 8])).then_inc(sem("mall"), 1)
                dve.wait_ge(sem("mb_ps"), b + 1)
                V.tensor_scalar(nmx, ps[7][:, 0:1], -1.0, None, ALU.mult).then_inc(sem("nmx"), 1)

            def keep_sums(b):
                dve.wait_ge(sem("z_exp"), b + 1)
                dve.wait_ge(sem("PT_ps"), b * 3 + 3)
                sa = sum_all[:, ds(b, 1)] if not isinstance(b, int) else sum_all[:, b:b + 1]
                ch.step(V.tensor_scalar(sa, sumc, 1.0, None, ALU.mult))
                ch.wait()
                dve.sem_inc(sem("z_free"), 1)

            def keep_output(b):
                dve.wait_ge(sem("pv"), b + 1)
                ch.step(V.tensor_scalar(o_sel[0:COLS, :], ps[5][0:COLS, 0:P], cst("head", COLS)[:, 0:1], None, ALU.mult))
                for h in range(1, H):
                    ch.wait()
                    last = h == H - 1
                    o = o_sel[0:COLS, :] if not last else (o_all[0:COLS, ds(b * P, P)] if not isinstance(b, int) else o_all[0:COLS, b * P:(b + 1) * P])
                    ch.step(V.scalar_tensor_tensor(out=o, in0=ps[5][0:COLS, h * P:(h + 1) * P], scalar=cst("head", COLS)[:, h:h + 1],
                                                   in1=o_sel[0:COLS, :], op0=ALU.mult, op1=ALU.add))
                ch.wait()
                dve.sem_inc(sem("o_free"), 1)

            dve.sem_inc(sem("s_done0"), 1)
            set_queries(0)
            flip_keys(0)
            take_scores(0)
            set_queries(1)
            flip_keys(1)
            keep_sums(0)
            with dve.Fori(0, NB - 2) as t:
                ch.enter(t, 9)
                take_scores(t + 1)
                set_queries(t + 2)
                flip_keys(t + 2)
                keep_output(t)
                keep_sums(t + 1)
            ch.leave(NB - 2)
            take_scores(NB - 1)
            keep_output(NB - 2)
            keep_sums(NB - 1)
            keep_output(NB - 1)
        block_a.__exit__(None, None, None)
        nc.all_engine_barrier()
        nc.clear_and_free_semaphores(list(sems.values()))
        sems.clear()
        part[0] = "_b"
        nc.all_engine_barrier()

        block = ctx.enter_context(nc.Block())

        @block.sync
        def _(sp):
            for i in range(TILES):
                sp.wait_ge(sem("xh_ready"), i + 1)
                sp.dma_start(rows_d[i * P:i * P + ROWS[i], :], xh[i % 2][0:ROWS[i], :]).then_inc(sem(f"xh_out{i % 2}"), 16)
            sp.wait_ge(sem("routed"), 1)
            sp.wait_ge(sem("zeros_out"), 16 * (CAP - SURE))
            sp.drain().then_inc(sem("phase"), 1)
            nit = sp.value_load(nit_i[0:1, 0:1], min_val=1, max_val=PAIRS)
            with sp.Fori(0, nit) as t:
                for s in range(2):
                    e = sp.value_load(eid[0:1, ds(t * 2 + s, 1)], min_val=0, max_val=NE - 1)
                    sp.wait_ge(sem("h_ps"), t * 2 + s + 1)
                    w13 = wslot[s][:, 0:4096].rearrange("p (k f) -> p k f", k=KC)
                    sp.dma_start(w13[:, :, 0:FF], w1_v[ds(e * D, D), :].rearrange("(k p) f -> p k f", p=P)).then_inc(sem(f"wexp{s}"), 16)
                    sp.dma_start(w13[:, :, FF:2 * FF], w3_v[ds(e * D, D), :].rearrange("(k p) f -> p k f", p=P)).then_inc(sem(f"wexp{s}"), 16)
                for s in range(2):
                    e = sp.value_load(eid[0:1, ds(t * 2 + s, 1)], min_val=0, max_val=NE - 1)
                    sp.wait_ge(sem("ye_ps"), t * 2 + s + 1)
                    sp.dma_start(wslot[s][:, 4096:6144].rearrange("p (k f) -> p k f", k=2),
                                 w2_v[ds(e * FF, FF), :].rearrange("(k p) f -> p k f", p=P)).then_inc(sem(f"wdown{s}"), 16)
            phase_end(sp, 2)
            for i in range(TILES):
                sp.wait_ge(sem("y_ready"), i + 1)
                dst = ys_v if i == TILES - 1 else yp_v[:, i, :]
                sp.dma_start(dst, ya[i % YBUF][0:ROWS[i], :]).then_inc(sem(f"y_out{i % YBUF}"), 16)
            for i in range(YBUF):
                sp.wait_ge(sem(f"y_out{i}"), 16 * len(range(i, TILES, YBUF)))

        @block.gpsimd
        def _(pool):
            nc.gpsimd.memset(zero_rows, 0.0).then_inc(sem("zeros"), 1)
            pool.wait_ge(sem("zeros"), 1)
            for j in range(SURE, CAP):
                pool.dma_start(ye_d[j * P:(j + 1) * P, :], zero_rows).then_inc(sem("zeros_out"), 16)
            pool.wait_ge(sem("xh_out0"), 16 * 5)
            pool.wait_ge(sem("xh_out1"), 16 * 4)
            pool.wait_ge(sem("zeros_out"), 16 * (CAP - SURE))
            phase_end(pool, 1)
            nit = pool.value_load(nit_i[0:1, 0:1], min_val=1, max_val=PAIRS)
            with pool.Fori(0, nit) as t:
                for s in range(2):
                    pool.wait_ge(sem("xgT_ps"), t * 2 + s + 1)
                    nc.gpsimd.tensor_copy(idx_cur[:, s:s + 1], ids[:, ds(t * 2 + s, 1)]).then_inc(sem("idx"), 1)
                    pool.wait_ge(sem("idx"), t * 2 + s + 1)
                    pool.sem_inc(sem("idx_seen"), 1)
                    pool.indirect_dma_start(out=xg[s], out_offset=None, in_=rows_d,
                                            in_offset=bass.IndirectOffsetOnAxis(ap=idx_cur[:, s:s + 1], axis=0)).then_inc(sem(f"xg_in{s}"), 16)
            phase_end(pool, 2)
            for i in range(TILES):
                if i >= YBUF:
                    pool.wait_ge(sem("ssf"), i - YBUF + 1)
                    pool.wait_ge(sem(f"y_out{i % YBUF}"), 16 * (i // YBUF))
                for c, buf in enumerate((ya, yb)):
                    pool.indirect_dma_start(out=buf[i % YBUF][0:ROWS[i], :], out_offset=None, in_=ye_d,
                                            in_offset=bass.IndirectOffsetOnAxis(ap=slot_i[0:ROWS[i], c * TILES + i:c * TILES + i + 1], axis=0)).then_inc(sem(f"yg{c}{i % YBUF}"), 16)

        @block.scalar
        def _(act):
            ch = Chain(act, sem("act"))
            for i in range(TILES):
                r = ROWS[i]
                if i == 1:
                    act.wait_ge(sem("dss"), 1)
                    nc.scalar.activation(osq[0:16, :], o16[0:16, :], ACT.Square).then_inc(sem("dsq"), 1)
                    act.wait_ge(sem("dms"), 1)
                    nc.scalar.activation(orms[0:16, :], oms[0:16, :], ACT.Sqrt).then_inc(sem("drms"), 1)
                act.wait_ge(sem("x1_ready"), i + 1)
                nc.scalar.activation(sqj[0:r, :], x1[0:r, i * D:(i + 1) * D], ACT.Square,
                                     accum_out=ss[0:r, i:i + 1]).then_inc(sem("ss1"), 1)
                act.wait_ge(sem("ss1"), i + 1)
                nc.scalar.activation(rstd[0:r, i:i + 1], ss[0:r, i:i + 1], ACT.Sqrt, scale=1.0 / D, bias=epsc[0:r, :]).then_inc(sem("rms1"), 1)
            act.wait_ge(sem("gshift"), 1)
            nc.scalar.activation(gexp, gexp, ACT.Exp).then_inc(sem("gexp"), 1)
            act.wait_ge(sem("eshift"), 1)
            nc.scalar.activation(gate2, gate2, ACT.Exp).then_inc(sem("eexp"), 1)
            act.wait_ge(sem("gates"), 1)
            for i in range(TILES):
                nc.scalar.activation(diag2[:, i * P:(i + 1) * P], ident, ACT.Copy, scale=gate2[:, i:i + 1]).then_inc(sem("diag2"), 1)
            phase_end(act, 1)
            turns = act.value_load(more_i[0:1, 0:1], min_val=1, max_val=PAIRS - 1)

            def silu(t, s):
                act.wait_ge(sem("h_ps"), t * 2 + s + 3)
                act.wait_ge(sem("heT_ps"), t * 2 + s + 1)
                nc.scalar.activation(he[s], ps[4 + s][:, 0:FF], ACT.Silu).then_inc(sem("h_silu"), 1)

            def keep_flipped(t, s):
                act.wait_ge(sem("heT_ps"), t * 2 + s + 3)
                nc.scalar.activation(heT[s], ps[6 + s][:, 0:FF], ACT.Copy).then_inc(sem("heT"), 1)

            def results(t, s):
                act.wait_ge(sem("ye_ps"), t * 2 + s + 3)
                act.wait_ge(sem(f"ye_out{s}"), t * 16 + 16)
                nc.scalar.activation(ysb[s][:, 0:512], ps[2][:, :], ACT.Copy).then_inc(sem("ye_a"), 1)
                act.wait_ge(sem("ye_a"), t * 2 + s + 1)
                act.wait_ge(sem("ye_v"), t * 2 + s + 1)
                rows = ye_d[ds((t * 2 + s) * P, P), :] if not isinstance(t, int) else ye_d[(t * 2 + s) * P:(t * 2 + s + 1) * P, :]
                act.dma_start(rows, ysb[s]).then_inc(sem(f"ye_out{s}"), 16)

            def pair(t, first=False):
                if not first:
                    results(t - 1, 1)
                silu(t, 0)
                keep_flipped(t, 0)
                silu(t, 1)
                results(t, 0)
                keep_flipped(t, 1)

            pair(0, True)
            with act.Fori(0, turns) as t:
                pair(t + 1)
            results(turns, 1)
            nit = turns + 1
            act.wait_ge(sem("ye_out0"), nit * 16 + 16)
            act.wait_ge(sem("ye_out1"), nit * 16 + 16)
            act.sem_inc(sem("ye_seen"), 1)
            phase_end(act, 2)
            act.dma_start(fw, final_norm_w.rearrange("(a n) -> a n", a=1).broadcast_to([P, D])).then_inc(sem("fw"), 16)
            for i in range(TILES):
                r = ROWS[i]
                act.wait_ge(sem("x2_ready"), i + 1)
                nc.scalar.activation(yb[i % YBUF][0:r, :], ya[i % YBUF][0:r, :], ACT.Square,
                                     accum_out=ss[0:r, i:i + 1]).then_inc(sem("ssf"), 1)
                act.wait_ge(sem("ssf"), i + 1)
                nc.scalar.activation(rstd[0:r, i:i + 1], ss[0:r, i:i + 1], ACT.Sqrt, scale=1.0 / D, bias=epsc[0:r, :]).then_inc(sem("rmsf"), 1)

        @block.tensor
        def _(pe):
            for name in ("ye_ps", "xgT_ps", "h_ps", "heT_ps"):
                pe.sem_inc(sem(name), 2)

            def project(i):
                r = ROWS[i]
                if i >= 2:
                    pe.wait_ge(sem("x1_ready"), i - 1)
                for n in range(2):
                    for k in range(KC):
                        mm = nc.tensor.matmul(ps[2 * (i % 2) + n][0:r, :], tok(mixT, k, i), wout[:, k * D + n * 512:k * D + (n + 1) * 512],
                                              start=(k == 0), stop=(k == KC - 1))
                    mm.then_inc(sem("x1_ps"), 1)

            def flip(i):
                r = ROWS[i]
                pe.wait_ge(sem("xh_ready"), i + 1)
                if i:
                    pe.wait_ge(sem("h2T"), 2 * i)
                for k in range(KC):
                    mm = nc.tensor.transpose(ps[4 + k // 4][:, (k % 4) * P:(k % 4) * P + r], xh[i % 2][0:r, k * P:(k + 1) * P], ident[0:r, 0:r])
                    if k % 4 == 3:
                        mm.then_inc(sem("h2T_ps"), 1)

            def router(i):
                r = ROWS[i]
                pe.wait_ge(sem("h2T"), 2 * i + 2)
                if i:
                    pe.wait_ge(sem("lg"), i)
                for k in range(KC):
                    mm = nc.tensor.matmul(ps[6][0:r, 0:20], h2T[i % 2][:, k * P:k * P + r], wr[:, k * 20:(k + 1) * 20], start=(k == 0), stop=(k == KC - 1))
                mm.then_inc(sem("lg_ps"), 1)

            nc.tensor.matmul(ps[7][0:COLS, 0:NB], cst("rowsum"), sum_all, start=True, stop=True).then_inc(sem("dsum_ps"), 1)
            project(0)
            pe.wait_ge(sem("dnorm"), 1)
            for n in range(2):
                mm = nc.tensor.matmul(ps[4 + n][0:16, :], comb[0:COLS, :], o_all[0:COLS, n * 512:(n + 1) * 512], start=True, stop=True)
            mm.then_inc(sem("dmix_ps"), 1)
            project(1)
            pe.wait_ge(sem("d_ready"), 1)
            for b in range(NB):
                mm = nc.tensor.transpose(ps[6][:, b * 16:(b + 1) * 16], o16[0:16, b * P:(b + 1) * P], ident[0:16, 0:16])
            mm.then_inc(sem("dT_ps"), 1)
            flip(0)
            for i in range(TILES):
                if i + 2 < TILES:
                    project(i + 2)
                if i == 0:
                    pe.wait_ge(sem("d_placed"), 1)
                router(i)
                if i + 1 < TILES:
                    flip(i + 1)
            pe.wait_ge(sem("counts_in"), 1)
            nc.tensor.matmul(ps[7][:, 0:TILES * 16], cst("tri"), Mx, start=True, stop=False)
            nc.tensor.matmul(ps[7][:, 0:TILES * 16], ones, cum, start=False, stop=True)
            nc.tensor.matmul(ps[6][:, 64:80], ones, rk[:, 0:16], start=True, stop=True).then_inc(sem("rank_ps"), 1)
            for k in range(2 * TILES):
                if k % TILES == 0:
                    pe.wait_ge(sem("slots_ready"), k // TILES + 1)
                r = ROWS[k % TILES]
                mm = nc.tensor.matmul(ps[5][:, 0:CAP], inrow[0:r, k * P:(k + 1) * P], intile[0:r, k * CAP:(k + 1) * CAP],
                                      start=(k == 0), stop=(k == 2 * TILES - 1))
            mm.then_inc(sem("ids_ps"), 1)
            phase_end(pe, 1)
            turns = pe.value_load(more_i[0:1, 0:1], min_val=1, max_val=PAIRS - 1)

            def flip_rows(t, s):
                pe.wait_ge(sem("xT_s"), t * 4 + 2 * s + 2)
                pe.wait_ge(sem(f"xg_in{s}"), t * 16 + 16)
                for k in range(KC):
                    mm = nc.tensor.transpose(ps[k // 4][:, (k % 4) * P:(k % 4 + 1) * P], xg[s][:, k * P:(k + 1) * P], ident)
                mm.then_inc(sem("xgT_ps"), 1)

            def hidden(t, s, k0, k1):
                if k0 == 0:
                    pe.wait_ge(sem("xT_s"), t * 4 + 2 * s + 4)
                    pe.wait_ge(sem(f"wexp{s}"), t * 32 + 32)
                    pe.wait_ge(sem("he_ready"), t * 2 + s + 1)
                w13 = wslot[s][:, 0:4096].rearrange("p (k f) -> p k f", k=KC)
                for k in range(k0, k1):
                    mm = nc.tensor.matmul(ps[4 + s][:, :], xT[s][:, k * P:(k + 1) * P], w13[:, k, :], start=(k == 0), stop=(k == KC - 1))
                if k1 == KC:
                    mm.then_inc(sem("h_ps"), 1)

            def flip_hidden(t, s):
                pe.wait_ge(sem("he_ready"), t * 2 + s + 3)
                for k in range(2):
                    mm = nc.tensor.transpose(ps[6 + s][:, k * P:(k + 1) * P], he[s][:, k * P:(k + 1) * P], ident)
                mm.then_inc(sem("heT_ps"), 1)

            def down(t, s):
                pe.wait_ge(sem("heT"), t * 2 + s + 1)
                pe.wait_ge(sem(f"wdown{s}"), t * 16 + 16)
                pe.wait_ge(sem("ybank_free"), t * 4 + 2 * s + 2)
                w2 = wslot[s][:, 4096:6144]
                for n in range(2):
                    for k in range(2):
                        mm = nc.tensor.matmul(ps[2 + n][:, :], heT[s][:, k * P:(k + 1) * P], w2[:, k * D + n * 512:k * D + (n + 1) * 512], start=(k == 0), stop=(k == 1))
                mm.then_inc(sem("ye_ps"), 1)

            def pair(t, first=False):
                flip_rows(t, 0)
                if not first:
                    down(t - 1, 1)
                hidden(t, 0, 0, 5)
                flip_rows(t, 1)
                hidden(t, 0, 5, KC)
                hidden(t, 1, 0, 6)
                flip_hidden(t, 0)
                hidden(t, 1, 6, KC)
                down(t, 0)
                flip_hidden(t, 1)

            pair(0, True)
            with pe.Fori(0, turns) as t:
                pair(t + 1)
            down(turns, 1)
            phase_end(pe, 2)
            pe.wait_ge(sem("diag2"), TILES)
            for i in range(TILES):
                r = ROWS[i]
                if i >= 4:
                    pe.wait_ge(sem("x2_ready"), i - 3)
                for n in range(2):
                    nc.tensor.matmul(ps[2 * (i % 4) + n][0:r, :], ident[0:r, 0:r], x1[0:r, i * D + n * 512:i * D + (n + 1) * 512], start=True, stop=False)
                pe.wait_ge(sem(f"yg1{i % YBUF}"), 16 * (i // YBUF + 1))
                for n in range(2):
                    mm = nc.tensor.matmul(ps[2 * (i % 4) + n][0:r, :], diag2[0:r, i * P:i * P + r], yb[i % YBUF][0:r, n * 512:(n + 1) * 512], start=False, stop=True)
                mm.then_inc(sem("mixed"), 1)

        @block.vector
        def _(dve):
            V = nc.vector
            ch = Chain(dve, sem("dve"))

            def step(ins):
                ch.step(ins)
                ch.wait()

            def mean_eps(a, n):
                return V.tensor_scalar(a, a, 1.0 / n, EPS, ALU.mult, ALU.add)

            def inverse(r, v, chain=None):
                c = chain or ch
                t = nwt[0:r.shape[0], 0:r.shape[1]]
                for ins in (lambda: V.reciprocal(r, r),
                            lambda: V.tensor_tensor(t, r, r, ALU.mult),
                            lambda: V.scalar_tensor_tensor(out=t, in0=t, scalar=-0.5, in1=v, op0=ALU.mult, op1=ALU.mult),
                            lambda: V.scalar_tensor_tensor(out=r, in0=t, scalar=1.5, in1=r, op0=ALU.add, op1=ALU.mult)):
                    c.step(ins())
                    c.wait()


            def residual(i):
                r = ROWS[i]
                dve.wait_ge(sem("x1_ps"), 2 * i + 2)
                for n in range(2):
                    xx = x1[0:r, i * D + n * 512:i * D + (n + 1) * 512]
                    last = V.tensor_tensor(xx, ps[2 * (i % 2) + n][0:r, :], xx, ALU.add)
                last.then_inc(sem("x1_ready"), 1)

            def norm2(i):
                r = ROWS[i]
                dve.wait_ge(sem("rms1"), i + 1)
                ch.step(mean_eps(ss[0:r, i:i + 1], D))
                inverse(rstd[0:r, i:i + 1], ss[0:r, i:i + 1])
                if i >= 2:
                    dve.wait_ge(sem(f"xh_out{i % 2}"), 16 * (i // 2))
                V.tensor_scalar(xh[i % 2][0:r, :], x1[0:r, i * D:(i + 1) * D], rstd[0:r, i:i + 1], None, ALU.mult).then_inc(sem("xh_ready"), 1)

            def keep_flipped(i):
                r = ROWS[i]
                for g in range(2):
                    dve.wait_ge(sem("h2T_ps"), 2 * i + g + 1)
                    V.tensor_tensor(h2T[i % 2][:, 512 * g:512 * g + 512].rearrange("p (a b) -> p a b", b=P)[:, :, 0:r],
                                    head3(ps[4 + g][:, :], P)[:, :, 0:r],
                                    n2w[:, 4 * g:4 * g + 4].unsqueeze(2).broadcast_to([P, 4, r]), ALU.mult).then_inc(sem("h2T"), 1)

            def logits(i):
                r = ROWS[i]
                dve.wait_ge(sem("lg_ps"), i + 1)
                V.tensor_tensor(lgall[0:r, i * 20:(i + 1) * 20], ps[6][0:r, 0:20], rbias[0:r, :], ALU.add).then_inc(sem("lg"), 1)

            lg3 = head3(lgall, 20)
            ohg, off = head3(rk[:, 0:36], NG), head3(cmp[:, 0:36], NG)
            v3, i3 = head3(v12, 2), head3(i12, 2)
            o1, o2, M3, c3, r3 = (head3(a, NE) for a in (oh1, oh2, Mx, cum, rk))
            step(V.memset(c3[:, 0, :], 0.0))
            step(V.memset(gpad, -3e38))

            def choose(i):
                dve.wait_ge(sem("lg"), i + 1)
                step(V.tensor_copy(head3(gpad, 8)[:, i, 0:NG], lg3[:, i, 0:NG]))
                step(V.max(g8, gpad[:, i * 8:(i + 1) * 8]))
                ch.step(V.tensor_scalar(gexp[:, i * 4:(i + 1) * 4], lgall[:, i * 20:i * 20 + 4], g8[:, 0:1], None, ALU.subtract))
                step(V.max_index(gi, g8, gpad[:, i * 8:(i + 1) * 8]))
                step(V.tensor_copy(gidx[:, i:i + 1], gi[:, 0:1]))
                step(V.tensor_tensor(ohg[:, i, :], cst("iota")[:, 0:NG], gidx[:, i:i + 1].broadcast_to([P, NG]), ALU.is_equal))
                ch.step(V.tensor_scalar(off[:, i, :], ohg[:, i, :], -NEG, NEG, ALU.mult, ALU.add))
                lmi = lm[:, i * 16:(i + 1) * 16].rearrange("p (g e) -> p g e", e=EG)
                lei = lgall[:, i * 20 + NG:(i + 1) * 20].rearrange("p (g e) -> p g e", e=EG)
                step(V.tensor_tensor(lmi, lei, ohg[:, i, :].unsqueeze(2).broadcast_to([P, NG, EG]), ALU.mult))
                step(V.tensor_tensor(lmi, lmi, off[:, i, :].unsqueeze(2).broadcast_to([P, NG, EG]), ALU.add))
                step(V.max(e8, lm[:, i * 16:(i + 1) * 16]))
                ch.step(V.tensor_copy(v12[:, 2 * i:2 * i + 2], e8[:, 0:2]))
                step(V.max_index(ei, e8, lm[:, i * 16:(i + 1) * 16]))
                step(V.tensor_copy(i12[:, 2 * i:2 * i + 2], ei[:, 0:2]))
                ch.step(V.tensor_tensor(o1[:, i, :], cst("iota")[:, 0:NE], i12[:, 2 * i:2 * i + 1].broadcast_to([P, NE]), ALU.is_equal))
                step(V.tensor_tensor(o2[:, i, :], cst("iota")[:, 0:NE], i12[:, 2 * i + 1:2 * i + 2].broadcast_to([P, NE]), ALU.is_equal))
                step(V.tensor_tensor(M3[:, i, :], o1[:, i, :], o2[:, i, :], ALU.add))
                if i == TILES - 1:
                    step(V.tensor_scalar(M3[:, i, :], M3[:, i, :], cst("valid"), None, ALU.mult))
                else:
                    step(V.tensor_tensor(c3[:, i + 1, :], c3[:, i, :], M3[:, i, :], ALU.add))

            dve.wait_ge(sem("dsum_ps"), 1)
            step(V.reciprocal(rsum[0:COLS, :], ps[7][0:COLS, 0:NB]))
            step(V.tensor_tensor(head3(o_all[0:COLS, :], P), head3(o_all[0:COLS, :], P), rsum[0:COLS, :].unsqueeze(2).broadcast_to([COLS, NB, P]), ALU.mult))
            dve.sem_inc(sem("dnorm"), 1)
            residual(0)
            dve.wait_ge(sem("dmix_ps"), 1)
            for n in range(2):
                ch.step(V.tensor_copy(o16[0:16, n * 512:(n + 1) * 512], ps[4 + n][0:16, :]))
            ch.wait()
            dve.sem_inc(sem("dss"), 1)
            norm2(0)
            dve.wait_ge(sem("dsq"), 1)
            step(V.tensor_reduce(oms[0:16, :], head3(osq[0:16, :], P), AX, ALU.add))
            step(mean_eps(oms[0:16, :], P))
            dve.sem_inc(sem("dms"), 1)
            dve.wait_ge(sem("drms"), 1)
            inverse(orms[0:16, :], oms[0:16, :])
            step(V.tensor_tensor(head3(o16[0:16, :], P), head3(o16[0:16, :], P), orms[0:16, :].unsqueeze(2).broadcast_to([16, NB, P]), ALU.mult))
            dve.sem_inc(sem("d_ready"), 1)
            residual(1)
            dve.wait_ge(sem("dT_ps"), 1)
            for h in range(H):
                ch.step(V.tensor_scalar(head3(mixT[:, h * TOK + SEQ:(h + 1) * TOK], NT),
                                        ps[6][:, 0:128].rearrange("p (b h t) -> p b h t", b=NB, h=H)[:, :, h, :], daw, None, ALU.mult))
            ch.wait()
            dve.sem_inc(sem("d_placed"), 1)
            keep_flipped(0)
            norm2(1)
            for i in range(TILES):
                if i + 2 < TILES:
                    residual(i + 2)
                logits(i)
                if i + 1 < TILES:
                    keep_flipped(i + 1)
                if i + 2 < TILES:
                    norm2(i + 2)
                choose(i)
            dve.sem_inc(sem("gshift"), 1)
            V.tensor_tensor(gate2.unsqueeze(2), v3[:, :, 1:2], v3[:, :, 0:1], ALU.subtract).then_inc(sem("eshift"), 1)
            step(V.tensor_tensor(rk[:, 0:16], c3[:, 8, :], M3[:, 8, :], ALU.add))
            dve.sem_inc(sem("counts_in"), 1)
            dve.wait_ge(sem("rank_ps"), 1)
            step(V.tensor_scalar(cnt_i, ps[6][:, 64:80], 127.0, None, ALU.add))
            step(V.tensor_scalar(cnt_i, cnt_i, 7, None, ALU.logical_shift_right))
            step(V.tensor_copy(ntl, cnt_i))
            step(V.tensor_tensor_scan(endt, ones[:, 0:NE], ntl, 0.0, ALU.mult, ALU.add))
            step(V.tensor_tensor(base, endt, ntl, ALU.subtract))
            step(V.tensor_scalar(base, base, float(P), None, ALU.mult))
            step(V.tensor_tensor(r3, head3(ps[7][:, 0:TILES * 16], NE), base.unsqueeze(1).broadcast_to([P, TILES, NE]), ALU.add))
            for c, o in ((0, oh1), (1, oh2)):
                step(V.tensor_tensor(o, o, rk, ALU.mult))
                step(V.tensor_reduce(slotf[:, c * TILES:(c + 1) * TILES], head3(o, NE), AX, ALU.add))
            step(V.tensor_copy(slot_i, slotf))
            ch.step(V.tensor_scalar(row_i, slot_i, P - 1, None, ALU.bitwise_and))
            step(V.tensor_scalar(row_j, slot_i, 7, None, ALU.logical_shift_right))
            ch.step(V.tensor_copy(rowf, row_i))
            step(V.tensor_copy(tilef, row_j))
            it3 = head3(intile, CAP)
            step(V.tensor_tensor(it3, cst("iota").unsqueeze(1).broadcast_to([P, 2 * TILES, CAP]), tilef.unsqueeze(2).broadcast_to([P, 2 * TILES, CAP]), ALU.is_equal))
            for c in range(2):
                half = slice(c * TILES, (c + 1) * TILES)
                ch.step(V.tensor_tensor(it3[:, half, :], it3[:, half, :], cst("token").unsqueeze(2).broadcast_to([P, TILES, CAP]), ALU.mult))
                ch.step(V.tensor_tensor(head3(inrow, P)[:, half, :], cst("iota128").unsqueeze(1).broadcast_to([P, TILES, P]),
                                        rowf[:, half].unsqueeze(2).broadcast_to([P, TILES, P]), ALU.is_equal))
                ch.wait()
                dve.sem_inc(sem("slots_ready"), 1)
            dve.wait_ge(sem("gexp"), 1)
            step(V.tensor_reduce(ptop, head3(gexp, 4), AX, ALU.add))
            step(V.reciprocal(ptop, ptop))
            dve.wait_ge(sem("eexp"), 1)
            step(V.tensor_scalar(gate1, gate2, 1.0, None, ALU.add))
            step(V.reciprocal(gate1, gate1))
            step(V.tensor_tensor(gate1, gate1, ptop, ALU.mult))
            step(V.tensor_tensor(gate2, gate2, gate1, ALU.mult))
            dve.sem_inc(sem("gates"), 1)
            c3_ = cmp.rearrange("p (j e) -> p j e", e=NE)
            step(V.tensor_tensor(c3_, endt.unsqueeze(1).broadcast_to([P, CAP, NE]), cst("iota").unsqueeze(2).broadcast_to([P, CAP, NE]), ALU.is_le))
            step(V.tensor_reduce(eid_f, c3_, AX, ALU.add))
            step(V.tensor_scalar(eid, eid_f, float(NE - 1), None, ALU.min))
            step(V.tensor_scalar(base[:, 0:1].bitcast(I32), endt[:, NE - 1:NE], 1.0, None, ALU.add))
            step(V.tensor_scalar(nit_i, base[:, 0:1].bitcast(I32), 1, None, ALU.logical_shift_right))
            step(V.tensor_scalar(more_i, nit_i, -1, None, ALU.add))
            dve.sem_inc(sem("routed"), 1)
            dve.wait_ge(sem("ids_ps"), 1)
            step(V.tensor_copy(ids, ps[5][:, 0:CAP]))
            phase_end(dve, 1)

            dve.sem_inc(sem("xT_s"), 2)
            dve.sem_inc(sem("he_ready"), 2)
            dve.sem_inc(sem("ybank_free"), 2)
            dve.sem_inc(sem("ye_out0"), 16)
            dve.sem_inc(sem("ye_out1"), 16)
            turns = dve.value_load(more_i[0:1, 0:1], min_val=1, max_val=PAIRS - 1)

            def rows(t, s):
                dve.wait_ge(sem("xgT_ps"), t * 2 + s + 3)
                dve.wait_ge(sem("h_ps"), t * 2 + s + 1)
                for g in range(2):
                    V.tensor_tensor(head3(xT[s][:, g * 512:(g + 1) * 512], P), head3(ps[g][:, :], P),
                                    n2w[:, 4 * g:4 * g + 4].unsqueeze(2).broadcast_to([P, 4, P]), ALU.mult).then_inc(sem("xT_s"), 1)

            def gated(t, s):
                dve.wait_ge(sem("h_silu"), t * 2 + s + 1)
                V.tensor_tensor(he[s], he[s], ps[4 + s][:, FF:2 * FF], ALU.mult).then_inc(sem("he_ready"), 1)

            def results(t, s):
                dve.wait_ge(sem("ye_ps"), t * 2 + s + 3)
                dve.wait_ge(sem(f"ye_out{s}"), t * 16 + 16)
                V.tensor_copy(ysb[s][:, 512:1024], ps[3][:, :]).then_inc(sem("ye_v"), 1)
                dve.wait_ge(sem("ye_a"), t * 2 + s + 1)
                dve.wait_ge(sem("ye_v"), t * 2 + s + 1)
                dve.sem_inc(sem("ybank_free"), 2)

            def pair(t, first=False):
                rows(t, 0)
                if not first:
                    results(t - 1, 1)
                rows(t, 1)
                gated(t, 0)
                gated(t, 1)
                results(t, 0)

            pair(0, True)
            with dve.Fori(0, turns) as t:
                pair(t + 1)
            results(turns, 1)
            phase_end(dve, 2)

            dve.wait_ge(sem("fw"), 16)
            ch2 = Chain(dve, sem("dve_last"))

            def combine(i):
                r = ROWS[i]
                dve.wait_ge(sem(f"yg0{i % YBUF}"), 16 * (i // YBUF + 1))
                dve.wait_ge(sem("mixed"), i + 1)
                a_ = ya[i % YBUF][0:r, :]
                for n in range(2):
                    last = V.scalar_tensor_tensor(out=a_[:, n * 512:(n + 1) * 512], in0=a_[:, n * 512:(n + 1) * 512], scalar=gate1[0:r, i:i + 1],
                                                  in1=ps[2 * (i % 4) + n][0:r, :], op0=ALU.mult, op1=ALU.add)
                last.then_inc(sem("x2_ready"), 1)

            combine(0)
            for i in range(TILES):
                if i + 1 < TILES:
                    combine(i + 1)
                r = ROWS[i]
                dve.wait_ge(sem("rmsf"), i + 1)
                ch2.step(mean_eps(ss[0:r, i:i + 1], D))
                inverse(rstd[0:r, i:i + 1], ss[0:r, i:i + 1], ch2)
                V.scalar_tensor_tensor(out=ya[i % YBUF][0:r, :], in0=ya[i % YBUF][0:r, :], scalar=rstd[0:r, i:i + 1], in1=fw[0:r, :],
                                       op0=ALU.mult, op1=ALU.mult).then_inc(sem("y_ready"), 1)


_INS = ['x_prompt', 'x_sample', 'cache_k', 'cache_v', 'state_hgrn', 'page_table', 'norm1_w', 'w_in', 'rel_bias',
        'lambda_q1', 'lambda_k1', 'lambda_q2', 'lambda_k2', 'da_subln_w', 'hg_lb_logits', 'hg_norm_w', 'w_out',
        'norm2_w', 'router_g_w', 'router_g_b', 'router_e_w', 'router_e_b', 'expert_w1', 'expert_w3', 'expert_w2',
        'final_norm_w']
_OUTS = [((1, SEQ, D), 'float32'), ((NB, NT, D), 'float32'), ((1, 1, SEQ, H, P), 'float32'), ((1, 1, SEQ, H, P), 'float32'),
         ((1, 1, H, P, P), 'float32'), ((1, NB, NT, H, P), 'float32'), ((1, NB, NT, H, P), 'float32'), ((1, NB, H, P, P), 'float32')]


def kernel(**inputs):
    import numpy as _np
    import concourse.bacc as _bacc
    from concourse import mybir as _mybir
    from concourse.bass_utils import run_bass_kernel_spmd as _run

    nc = _bacc.Bacc("TRN2", target_bir_lowering=False, num_devices=1)
    arrays, args = {}, []
    for name in _INS:
        a = _np.ascontiguousarray(inputs[name])
        arrays[f"in_{name}_dram"] = a
        args.append(nc.dram_tensor(f"in_{name}_dram", a.shape, _mybir.dt.from_np(a.dtype), kind="ExternalInput").ap())
    arrays["in_table_dram"] = TABLE
    args.append(nc.dram_tensor("in_table_dram", TABLE.shape, F32, kind="ExternalInput").ap())
    for i, (shape, dtype) in enumerate(_OUTS):
        dt = _mybir.dt.from_np(_np.dtype(dtype))
        args.append(nc.dram_tensor(f"out_{i}_dram", shape, dt, kind="ExternalOutput").ap())
    build(nc, *args)
    r = _run(nc, [arrays], core_ids=[0])
    return tuple(r.results[0][f"out_{i}_dram"] for i in range(len(_OUTS)))
```
